# Optimizing a Trainium2 kernel written in Bass

```python
import math
import jax, jax.numpy as jnp
from jax import lax
import numpy as np

D_MODEL = 2048
BATCH = 1
SEQ = 256
DEPTH = 2

HEAD_DIM = 128
ROPE_THETA = 10000.0
NORM_EPS = 1e-6
A_HEADS = 8
A_WIDTH = A_HEADS * HEAD_DIM
DIL_CONFIGS = ((128, 1), (512, 4), (2048, 16))
B_HEADS = 4
B_VDIM = 2 * HEAD_DIM
B_WIDTH = B_HEADS * B_VDIM
Q_BLOCK = 128
C_HEADS = D_MODEL // HEAD_DIM
C_WIDTH = C_HEADS * HEAD_DIM
MOBA_BLOCK = 256
MOBA_TOPK = 3
MOBA_Q_CHUNK = 16
AB_IN = 3 * A_WIDTH + 3 * B_WIDTH + (A_WIDTH + B_WIDTH)
C_IN = 4 * C_WIDTH
N_AB = (DEPTH + 1) // 2
N_C = DEPTH // 2


def _rmsnorm(x, g):
    x32 = x.astype(jnp.float32)
    y = x32 * lax.rsqrt(jnp.mean(x32 * x32, axis=-1, keepdims=True) + NORM_EPS)
    return y * g.astype(jnp.float32)

def _rope(t, pos):
    dh = t.shape[-1]
    inv = 1.0 / (ROPE_THETA ** (jnp.arange(0, dh, 2, dtype=jnp.float32) / dh))
    ang = pos.astype(jnp.float32)[:, None] * inv[None, :]
    cos = jnp.concatenate([jnp.cos(ang), jnp.cos(ang)], axis=-1)
    sin = jnp.concatenate([jnp.sin(ang), jnp.sin(ang)], axis=-1)
    x1, x2 = jnp.split(t, 2, axis=-1)
    rot = jnp.concatenate([-x2, x1], axis=-1)
    return t * cos + rot * sin

def _heads(t, n_heads):
    b, s, w = t.shape
    return t.reshape(b, s, n_heads, w // n_heads).transpose(0, 2, 1, 3)

def _merge(t):
    b, h, s, d = t.shape
    return t.transpose(0, 2, 1, 3).reshape(b, s, h * d)

def _dilated_group(q, k, v, dil, nback):
    B, H, S, Dh = q.shape
    blk = nback
    L = -(-S // dil)
    L = -(-L // blk) * blk
    Sp = L * dil
    nb = L // blk
    pad = ((0, 0), (0, 0), (0, Sp - S), (0, 0))

    def split(t):
        t = jnp.pad(t, pad).reshape(B, H, L, dil, Dh).transpose(0, 1, 3, 2, 4)
        return t.reshape(B, H, dil, nb, blk, Dh)

    def with_prev(t):
        prev = jnp.pad(t[:, :, :, :-1], ((0, 0), (0, 0), (0, 0), (1, 0), (0, 0), (0, 0)))
        return jnp.concatenate([prev, t], axis=4)

    qs = split(q)
    kk = with_prev(split(k))
    vv = with_prev(split(v))
    s = jnp.einsum('bhrnid,bhrnjd->bhrnij', qs, kk) * (Dh ** -0.5)
    nbi = jnp.arange(nb)[:, None, None]
    i = jnp.arange(blk)[None, :, None]
    j = jnp.arange(2 * blk)[None, None, :]
    rel = blk + i - j
    kidx = (nbi - 1) * blk + j
    mask = (rel >= 0) & (rel <= nback) & (kidx >= 0)
    s = jnp.where(mask, s, -jnp.inf)
    m = jnp.max(s, axis=-1, keepdims=True)
    p = jnp.exp(s - m)
    den = jnp.sum(p, axis=-1, keepdims=True)
    o = jnp.einsum('bhrnij,bhrnjd->bhrnid', p, vv) / den
    lse = m + jnp.log(den)

    def unsplit(t):
        c = t.shape[-1]
        t = t.reshape(B, H, dil, L, c).transpose(0, 1, 3, 2, 4).reshape(B, H, Sp, c)
        return t[:, :, :S]

    return unsplit(o), unsplit(lse)

def _dilated_mixture(q, k, v):
    outs, lses = [], []
    for window, dil in DIL_CONFIGS:
        o, lse = _dilated_group(q, k, v, dil, window // dil)
        outs.append(o)
        lses.append(lse)
    w = jax.nn.softmax(jnp.stack(lses, axis=0), axis=0)
    return jnp.sum(w * jnp.stack(outs, axis=0), axis=0)

def _diff_attention(q1, q2, k1, k2, v, lam):
    B, H, S, Dh = q1.shape
    scale = Dh ** -0.5
    kpos = jnp.arange(S)

    def blk(c):
        start = c * Q_BLOCK
        qa = lax.dynamic_slice_in_dim(q1, start, Q_BLOCK, axis=2)
        qb = lax.dynamic_slice_in_dim(q2, start, Q_BLOCK, axis=2)
        qpos = start + jnp.arange(Q_BLOCK)
        mask = kpos[None, :] <= qpos[:, None]
        p1 = jax.nn.softmax(jnp.where(mask, jnp.einsum('bhid,bhjd->bhij', qa, k1) * scale, -jnp.inf), axis=-1)
        p2 = jax.nn.softmax(jnp.where(mask, jnp.einsum('bhid,bhjd->bhij', qb, k2) * scale, -jnp.inf), axis=-1)
        return jnp.einsum('bhij,bhjd->bhid', p1 - lam * p2, v)

    o = lax.map(blk, jnp.arange(S // Q_BLOCK))
    return o.transpose(1, 2, 0, 3, 4).reshape(B, H, S, v.shape[-1])

def _moba_attention(q, k, v):
    B, H, S, Dh = q.shape
    scale = Dh ** -0.5
    nb = -(-S // MOBA_BLOCK)
    Sp = nb * MOBA_BLOCK
    pad = ((0, 0), (0, 0), (0, Sp - S), (0, 0))
    q, k, v = jnp.pad(q, pad), jnp.pad(k, pad), jnp.pad(v, pad)
    kb = k.reshape(B, H, nb, MOBA_BLOCK, Dh)
    vb = v.reshape(B, H, nb, MOBA_BLOCK, Dh)
    n_sel = min(MOBA_TOPK, nb - 1)
    if n_sel > 0:
        kmean = jnp.mean(kb, axis=3)
        gate = jnp.einsum('bhsd,bhnd->bhsn', q, kmean)
        qblk = jnp.arange(Sp) // MOBA_BLOCK
        past = jnp.arange(nb)[None, :] < qblk[:, None]
        gate = jnp.where(past, gate, -jnp.inf)
        top_vals, top_idx = lax.top_k(gate, n_sel)
        top_valid = jnp.isfinite(top_vals)
    bi = jnp.arange(B)[:, None, None, None]
    hi = jnp.arange(H)[None, :, None, None]

    def step(c):
        start = c * MOBA_Q_CHUNK
        qc = lax.dynamic_slice_in_dim(q, start, MOBA_Q_CHUNK, axis=2)
        b_own = start // MOBA_BLOCK
        ko = lax.dynamic_index_in_dim(kb, b_own, axis=2, keepdims=False)
        vo = lax.dynamic_index_in_dim(vb, b_own, axis=2, keepdims=False)
        qpos = start + jnp.arange(MOBA_Q_CHUNK)
        kpos = b_own * MOBA_BLOCK + jnp.arange(MOBA_BLOCK)
        s_own = jnp.einsum('bhid,bhjd->bhij', qc, ko) * scale
        s_own = jnp.where(kpos[None, :] <= qpos[:, None], s_own, -jnp.inf)
        if n_sel == 0:
            p = jax.nn.softmax(s_own, axis=-1)
            return jnp.einsum('bhij,bhjd->bhid', p, vo)
        ic = lax.dynamic_slice_in_dim(top_idx, start, MOBA_Q_CHUNK, axis=2)
        vc = lax.dynamic_slice_in_dim(top_valid, start, MOBA_Q_CHUNK, axis=2)
        kg = kb[bi, hi, ic]
        vg = vb[bi, hi, ic]
        s_sel = jnp.einsum('bhid,bhikjd->bhikj', qc, kg) * scale
        s_sel = jnp.where(vc[..., None], s_sel, -jnp.inf)
        s_all = jnp.concatenate([s_own, s_sel.reshape(B, H, MOBA_Q_CHUNK, n_sel * MOBA_BLOCK)], axis=-1)
        p = jax.nn.softmax(s_all, axis=-1)
        p_own = p[..., :MOBA_BLOCK]
        p_sel = p[..., MOBA_BLOCK:].reshape(B, H, MOBA_Q_CHUNK, n_sel, MOBA_BLOCK)
        return jnp.einsum('bhij,bhjd->bhid', p_own, vo) + jnp.einsum('bhikj,bhikjd->bhid', p_sel, vg)

    o = lax.map(step, jnp.arange(Sp // MOBA_Q_CHUNK))
    o = o.transpose(1, 2, 0, 3, 4).reshape(B, H, Sp, Dh)
    return o[:, :, :S]

def _layer_ab(x, norm_g, w_in, w_out, lam_vec, subln_g, layer_idx, pos):
    h = jnp.matmul(_rmsnorm(x, norm_g).astype(x.dtype), w_in).astype(jnp.float32)
    cuts = np.cumsum([A_WIDTH, A_WIDTH, A_WIDTH, B_WIDTH, B_WIDTH, B_WIDTH]).tolist()
    aq, ak, av, bq, bk, bv, z = jnp.split(h, cuts, axis=-1)
    ya = _dilated_mixture(_rope(_heads(aq, A_HEADS), pos), _rope(_heads(ak, A_HEADS), pos), _heads(av, A_HEADS))
    ya = _merge(ya)
    Bn, S = x.shape[0], x.shape[1]
    bq = _rope(bq.reshape(Bn, S, B_HEADS, 2, HEAD_DIM).transpose(0, 2, 3, 1, 4), pos)
    bk = _rope(bk.reshape(Bn, S, B_HEADS, 2, HEAD_DIM).transpose(0, 2, 3, 1, 4), pos)
    bv = _heads(bv, B_HEADS)
    lam_vec = lam_vec.astype(jnp.float32)
    lam_init = 0.8 - 0.6 * math.exp(-0.3 * layer_idx)
    lam = jnp.exp(jnp.sum(lam_vec[0] * lam_vec[1])) - jnp.exp(jnp.sum(lam_vec[2] * lam_vec[3])) + lam_init
    yb = _diff_attention(bq[:, :, 0], bq[:, :, 1], bk[:, :, 0], bk[:, :, 1], bv, lam)
    yb = _rmsnorm(yb, subln_g) * (1.0 - lam_init)
    yb = _merge(yb)
    y = jnp.concatenate([ya, yb], axis=-1) * jax.nn.silu(z)
    return x + jnp.matmul(y.astype(x.dtype), w_out)

def _layer_c(x, norm_g, w_in, w_out, pos):
    h = jnp.matmul(_rmsnorm(x, norm_g).astype(x.dtype), w_in).astype(jnp.float32)
    cq, ck, cv, z = jnp.split(h, [C_WIDTH, 2 * C_WIDTH, 3 * C_WIDTH], axis=-1)
    yc = _moba_attention(_rope(_heads(cq, C_HEADS), pos), _rope(_heads(ck, C_HEADS), pos), _heads(cv, C_HEADS))
    y = _merge(yc) * jax.nn.silu(z)
    return x + jnp.matmul(y.astype(x.dtype), w_out)

def first_inputs(seed: int = 0) -> dict:
    key = jax.random.key(seed)
    ks = jax.random.split(key, 10)
    f32 = jnp.float32
    x = jax.random.normal(ks[0], (BATCH, SEQ, D_MODEL), f32)
    norm_ab = 1.0 + 0.02 * jax.random.normal(ks[1], (N_AB, D_MODEL), f32)
    w_in_ab = jax.random.normal(ks[2], (N_AB, D_MODEL, AB_IN), f32) * D_MODEL ** -0.5
    w_out_ab = jax.random.normal(ks[3], (N_AB, A_WIDTH + B_WIDTH, D_MODEL), f32) * (A_WIDTH + B_WIDTH) ** -0.5
    lam_ab = 0.1 * jax.random.normal(ks[4], (N_AB, 4, HEAD_DIM), f32)
    subln_ab = 1.0 + 0.02 * jax.random.normal(ks[5], (N_AB, B_VDIM), f32)
    norm_c = 1.0 + 0.02 * jax.random.normal(ks[6], (N_C, D_MODEL), f32)
    w_in_c = jax.random.normal(ks[7], (N_C, D_MODEL, C_IN), f32) * D_MODEL ** -0.5
    w_out_c = jax.random.normal(ks[8], (N_C, C_WIDTH, D_MODEL), f32) * C_WIDTH ** -0.5
    final_norm = 1.0 + 0.02 * jax.random.normal(ks[9], (D_MODEL,), f32)
    return {"x": x, "norm_ab": norm_ab, "w_in_ab": w_in_ab, "w_out_ab": w_out_ab,
            "lam_ab": lam_ab, "subln_ab": subln_ab, "norm_c": norm_c, "w_in_c": w_in_c,
            "w_out_c": w_out_c, "final_norm": final_norm}

def first_block(x, norm_ab, w_in_ab, w_out_ab, lam_ab, subln_ab, norm_c, w_in_c, w_out_c, final_norm):
    pos = jnp.arange(x.shape[1], dtype=jnp.int32)
    h = x
    for i in range(DEPTH):
        j = i // 2
        if i % 2 == 0:
            h = _layer_ab(h, norm_ab[j], w_in_ab[j], w_out_ab[j], lam_ab[j], subln_ab[j], i, pos)
        else:
            h = _layer_c(h, norm_c[j], w_in_c[j], w_out_c[j], pos)
    return _rmsnorm(h, final_norm).astype(x.dtype)


DEPTH_2 = 1

GRID_W = 64
CTX_LEN = 256
EPS = 1e-6

D_SGU = D_MODEL // 4
SGU_HEADS = 4
SGU_HD = D_SGU // SGU_HEADS
SGU_CHUNK = 128
D_MLSTM = D_MODEL // 2
MLSTM_HEADS = 4
MLSTM_HD = D_MLSTM // MLSTM_HEADS
MLSTM_CHUNK = 128
QK_CONV = 3
D_POOL = D_MODEL // 4
POOL_WINDOWS = (2, 4, 8, 16)
POOL_GC = D_POOL // len(POOL_WINDOWS)
N_GATES = 2 * 2 * MLSTM_HEADS

OFF_U = 0
OFF_V = OFF_U + D_SGU
OFF_P = OFF_V + D_SGU
OFF_Q = OFF_P + D_POOL
OFF_O = OFF_Q + D_MLSTM
OFF_K = OFF_O + D_MLSTM
OFF_VM = OFF_K + D_MLSTM
OFF_G = OFF_VM + D_MLSTM
D_IN = OFF_G + N_GATES

N_KEYS = 128
N_EXPERTS = N_KEYS * N_KEYS
PEER_HEADS = 8
PEER_TOPK = 16
PEER_DK = 256
PEER_BLOCK = 128


def rmsnorm(x, g):
    xf = x.astype(jnp.float32)
    y = xf * lax.rsqrt(jnp.mean(xf * xf, axis=-1, keepdims=True) + EPS)
    return (y * g.astype(jnp.float32)).astype(x.dtype)

def ada_modulation(cond, w, b):
    m = jax.nn.silu(cond) @ w + b
    return jnp.split(m[:, None, :], 6, axis=-1)

def modulate(h, shift, scale):
    return h * (1 + scale) + shift

def chunk_sgu(u, v, g, w_s, b_s):
    B, T, _ = u.shape
    v = rmsnorm(v, g).reshape(B, T // SGU_CHUNK, SGU_CHUNK, SGU_HEADS, SGU_HD)
    mixed = jnp.einsum('hts,bcshd->bcthd', w_s, v) + b_s.T[None, None, :, :, None]
    return u * mixed.reshape(B, T, D_SGU)

def centred_dwconv(x, w):
    K, ch = w.shape
    pad = K // 2
    return lax.conv_general_dilated(x, w.astype(x.dtype)[:, None, :], window_strides=(1,),
                                    padding=[(pad, K - 1 - pad)],
                                    dimension_numbers=('NWC', 'WIO', 'NWC'), feature_group_count=ch)

def to_heads(a):
    B, T, _ = a.shape
    return a.reshape(B, T, MLSTM_HEADS, MLSTM_HD).transpose(0, 2, 1, 3)

def mlstm_inputs(q_raw, k_raw, v_raw, g_raw, conv_w, b_gate):
    k = to_heads(jax.nn.silu(centred_dwconv(k_raw, conv_w[:, D_MLSTM:])))
    v = to_heads(v_raw)
    B, T, _ = g_raw.shape
    g = (g_raw + b_gate).astype(jnp.float32).reshape(B, T, 2, 2, MLSTM_HEADS)
    g = g.transpose(2, 3, 0, 4, 1)
    q = None if q_raw is None else to_heads(jax.nn.silu(centred_dwconv(q_raw, conv_w[:, :D_MLSTM])))
    return q, k, v, g

def to_chunks(a):
    B, H, T = a.shape[:3]
    a = a.reshape((B, H, T // MLSTM_CHUNK, MLSTM_CHUNK) + a.shape[3:])
    return jnp.moveaxis(a, 2, 0)

def zero_state(batch):
    return (jnp.zeros((batch, MLSTM_HEADS, MLSTM_HD, MLSTM_HD), jnp.float32),
            jnp.zeros((batch, MLSTM_HEADS, MLSTM_HD), jnp.float32),
            jnp.zeros((batch, MLSTM_HEADS), jnp.float32))

def mlstm_scan(q, k, v, ig, fg, state, with_outputs):
    L = MLSTM_CHUNK
    causal = jnp.tril(jnp.ones((L, L), bool))
    kf = k.astype(jnp.float32) * (MLSTM_HD ** -0.5)
    xs = [to_chunks(a) for a in (kf, v.astype(jnp.float32), ig, fg)]
    if with_outputs:
        xs.append(to_chunks(q.astype(jnp.float32)))

    def step(carry, inp):
        C, n, m = carry
        kc, vc, ic, fc = inp[:4]
        b = jnp.cumsum(jax.nn.log_sigmoid(fc), axis=-1)
        b_last = b[..., -1]
        g = b_last[..., None] - b + ic
        m_new = jnp.maximum(b_last + m, g.max(-1))
        wk = jnp.exp(g - m_new[..., None])
        decay = jnp.exp(b_last + m - m_new)
        C_new = decay[..., None, None] * C + jnp.einsum('bhsv,bhsk->bhvk', vc * wk[..., None], kc)
        n_new = decay[..., None] * n + jnp.einsum('bhs,bhsk->bhk', wk, kc)
        if not with_outputs:
            return (C_new, n_new, m_new), None
        qc = inp[4]
        log_w = jnp.where(causal, b[..., :, None] - b[..., None, :] + ic[..., None, :], -jnp.inf)
        inter = b + m[..., None]
        m_t = jnp.maximum(inter, log_w.max(-1))
        w_prev = jnp.exp(inter - m_t)
        s = jnp.einsum('bhtd,bhsd->bhts', qc, kc) * jnp.exp(log_w - m_t[..., None])
        num = jnp.einsum('bhts,bhsv->bhtv', s, vc) + w_prev[..., None] * jnp.einsum('bhvk,bhtk->bhtv', C, qc)
        den = s.sum(-1) + w_prev * jnp.einsum('bhk,bhtk->bht', n, qc)
        h = num / jnp.maximum(jnp.abs(den), jnp.exp(-m_t))[..., None]
        return (C_new, n_new, m_new), h

    state, hs = lax.scan(step, state, tuple(xs))
    if not with_outputs:
        return None, state
    B, H, T, Dh = v.shape
    return jnp.moveaxis(hs, 0, 2).reshape(B, H, T, Dh), state

def mlstm_bidir(q, k, v, g, states, with_outputs):
    flip = lambda a: None if a is None else jnp.flip(a, axis=2)
    h_f, st_f = mlstm_scan(q, k, v, g[0, 0], g[0, 1], states[0], with_outputs)
    h_b, st_b = mlstm_scan(flip(q), flip(k), flip(v), flip(g[1, 0]), flip(g[1, 1]), states[1], with_outputs)
    h = h_f + jnp.flip(h_b, axis=2) if with_outputs else None
    return h, (st_f, st_b)

def mlstm_out(h, o_raw, g_norm, dtype):
    B, H, T, Dh = h.shape
    hn = h * lax.rsqrt(jnp.mean(h * h, axis=-1, keepdims=True) + EPS)
    hn = hn.transpose(0, 2, 1, 3).reshape(B, T, D_MLSTM) * g_norm.astype(jnp.float32)
    return (jax.nn.sigmoid(o_raw.astype(jnp.float32)) * hn).astype(dtype)

def window_bounds(n, w):
    idx = jnp.arange(n)
    return jnp.clip(idx - w // 2, 0, n), jnp.clip(idx - w // 2 + w, 0, n)

def grid_window_mean(x, rows, cols, w):
    B, T, ch = x.shape
    s = jnp.cumsum(jnp.cumsum(x.astype(jnp.float32).reshape(B, rows, cols, ch), axis=1), axis=2)
    s = jnp.pad(s, ((0, 0), (1, 0), (1, 0), (0, 0)))
    rlo, rhi = window_bounds(rows, w)
    clo, chi = window_bounds(cols, w)
    box = lambda r, c: jnp.take(jnp.take(s, r, axis=1), c, axis=2)
    tot = box(rhi, chi) - box(rlo, chi) - box(rhi, clo) + box(rlo, clo)
    cnt = ((rhi - rlo)[:, None] * (chi - clo)[None, :]).astype(jnp.float32)
    return (tot / cnt[None, :, :, None]).reshape(B, T, ch)

def pool_mixer(x, rows, cols, w_g, scale):
    B, T, _ = x.shape
    xg = x.reshape(B, T, len(POOL_WINDOWS), POOL_GC)
    means = jnp.stack([grid_window_mean(xg[:, :, i], rows, cols, w) for i, w in enumerate(POOL_WINDOWS)], axis=2)
    d = (means - xg.astype(jnp.float32)).astype(x.dtype)
    y = jnp.einsum('btgc,gcd->btgd', d, w_g)
    return y.reshape(B, T, D_POOL) * scale

def stream_mixers(p, h_mlstm, rows, cols, sgu_norm, sgu_w, sgu_b, mlstm_norm, pool_w, pool_scale):
    u = jax.nn.gelu(p[..., OFF_U:OFF_V])
    v = jax.nn.gelu(p[..., OFF_V:OFF_P])
    y_a = chunk_sgu(u, v, sgu_norm, sgu_w, sgu_b)
    y_b = mlstm_out(h_mlstm, p[..., OFF_O:OFF_K], mlstm_norm, p.dtype)
    y_c = pool_mixer(p[..., OFF_P:OFF_Q], rows, cols, pool_w, pool_scale)
    return jnp.concatenate([y_a, y_b, y_c], axis=-1)

def peer_ffn(h, wq, keys, u_tab, v_tab):
    B, T, D = h.shape
    ht = h.reshape(B * T, D)
    n = B * T
    q = (ht @ wq).astype(jnp.float32).reshape(n, PEER_HEADS, 2, PEER_DK // 2)
    s = jnp.einsum('nhpc,pkc->nhpk', q, keys.astype(jnp.float32))
    s1, i1 = lax.top_k(s[:, :, 0], PEER_TOPK)
    s2, i2 = lax.top_k(s[:, :, 1], PEER_TOPK)
    cand = (s1[..., :, None] + s2[..., None, :]).reshape(n, PEER_HEADS, PEER_TOPK * PEER_TOPK)
    sc, ci = lax.top_k(cand, PEER_TOPK)
    e = (jnp.take_along_axis(i1, ci // PEER_TOPK, axis=-1) * N_KEYS
         + jnp.take_along_axis(i2, ci % PEER_TOPK, axis=-1))
    gate = jax.nn.softmax(sc, axis=-1)
    nb = n // PEER_BLOCK

    def block(args):
        xb, eb, gb = args
        a = jnp.einsum('nd,nhkd->nhk', xb, jnp.take(u_tab, eb, axis=0))
        w = (gb * jax.nn.gelu(a.astype(jnp.float32))).astype(xb.dtype)
        return jnp.einsum('nhk,nhkd->nd', w, jnp.take(v_tab, eb, axis=0))

    out = lax.map(block, (ht.reshape(nb, PEER_BLOCK, D),
                          e.reshape(nb, PEER_BLOCK, PEER_HEADS, PEER_TOPK),
                          gate.reshape(nb, PEER_BLOCK, PEER_HEADS, PEER_TOPK)))
    return out.reshape(B, T, D)

def second_inputs(seed: int = 0) -> dict:
    key = jax.random.key(seed)
    ks = jax.random.split(key, 24)
    L, D = DEPTH_2, D_MODEL
    nrm = lambda k, shape, s: jax.random.normal(k, shape, jnp.float32) * s
    gate_base = jnp.array([0.0, 3.0], jnp.float32)[None, None, :, None]
    return {
        'x': nrm(ks[0], (BATCH, SEQ, D), 1.0),
        'c': nrm(ks[1], (BATCH, D), 1.0),
        'ctx': nrm(ks[2], (BATCH, CTX_LEN, D), 1.0),
        'c_ctx': nrm(ks[3], (D,), 1.0),
        'ada_w': nrm(ks[4], (L, D, 6 * D), 0.5 * D ** -0.5),
        'ada_b': nrm(ks[5], (L, 6 * D), 0.02),
        'norm_mix': 1.0 + nrm(ks[6], (L, D), 0.05),
        'norm_ffn': 1.0 + nrm(ks[7], (L, D), 0.05),
        'w_in': nrm(ks[8], (L, D, D_IN), D ** -0.5),
        'b_gate': (gate_base + nrm(ks[9], (L, 2, 2, MLSTM_HEADS), 0.1)).reshape(L, N_GATES),
        'sgu_norm': 1.0 + nrm(ks[10], (L, D_SGU), 0.05),
        'sgu_w': nrm(ks[11], (L, SGU_HEADS, SGU_CHUNK, SGU_CHUNK), SGU_CHUNK ** -0.5),
        'sgu_b': 1.0 + nrm(ks[12], (L, SGU_HEADS, SGU_CHUNK), 0.1),
        'qk_conv': nrm(ks[13], (L, QK_CONV, 2 * D_MLSTM), QK_CONV ** -0.5),
        'mlstm_norm': 1.0 + nrm(ks[14], (L, D_MLSTM), 0.05),
        'pool_w': nrm(ks[15], (L, len(POOL_WINDOWS), POOL_GC, POOL_GC), POOL_GC ** -0.5),
        'pool_scale': 1.0 + nrm(ks[16], (L, D_POOL), 0.1),
        'w_out': nrm(ks[17], (L, D, D), D ** -0.5),
        'peer_wq': nrm(ks[18], (L, D, PEER_HEADS * PEER_DK), D ** -0.5),
        'peer_keys': nrm(ks[19], (L, 2, N_KEYS, PEER_DK // 2), (PEER_DK // 2) ** -0.5),
        'peer_u': nrm(ks[20], (L, N_EXPERTS, D), D ** -0.5),
        'peer_v': nrm(ks[21], (L, N_EXPERTS, D), 0.25),
        'norm_final': 1.0 + nrm(ks[22], (D,), 0.05),
    }

def second_block(x, c, ctx, c_ctx, ada_w, ada_b, norm_mix, norm_ffn, w_in, b_gate, sgu_norm, sgu_w, sgu_b,
              qk_conv, mlstm_norm, pool_w, pool_scale, w_out, peer_wq, peer_keys, peer_u, peer_v, norm_final):
    rows = x.shape[1] // GRID_W
    ctx_len = ctx.shape[1]
    x_lat, x_ctx = x, ctx
    for l in range(DEPTH_2):
        last = l == DEPTH_2 - 1
        m_lat = ada_modulation(c, ada_w[l], ada_b[l])
        m_ctx = ada_modulation(c_ctx[None, :], ada_w[l], ada_b[l])
        mix_args = (sgu_norm[l], sgu_w[l], sgu_b[l], mlstm_norm[l], pool_w[l], pool_scale[l])

        hc = modulate(rmsnorm(x_ctx, norm_mix[l]), m_ctx[0], m_ctx[1])
        if last:
            pk = hc @ w_in[l][:, OFF_K:]
            _, kc, vc, gc = mlstm_inputs(None, pk[..., :D_MLSTM], pk[..., D_MLSTM:2 * D_MLSTM],
                                          pk[..., 2 * D_MLSTM:], qk_conv[l], b_gate[l])
            _, ctx_states = mlstm_bidir(None, kc, vc, gc, (zero_state(x.shape[0]), zero_state(x.shape[0])), False)
        else:
            pc = hc @ w_in[l]
            qc, kc, vc, gc = mlstm_inputs(pc[..., OFF_Q:OFF_O], pc[..., OFF_K:OFF_VM], pc[..., OFF_VM:OFF_G],
                                          pc[..., OFF_G:], qk_conv[l], b_gate[l])
            h_c, ctx_states = mlstm_bidir(qc, kc, vc, gc, (zero_state(x.shape[0]), zero_state(x.shape[0])), True)
            y_c = stream_mixers(pc, h_c, 1, ctx_len, *mix_args)
            x_ctx_new = x_ctx + m_ctx[2] * (y_c @ w_out[l])
            hf = modulate(rmsnorm(x_ctx_new, norm_ffn[l]), m_ctx[3], m_ctx[4])
            x_ctx_new = x_ctx_new + m_ctx[5] * peer_ffn(hf, peer_wq[l], peer_keys[l], peer_u[l], peer_v[l])

        hl = modulate(rmsnorm(x_lat, norm_mix[l]), m_lat[0], m_lat[1])
        pl = hl @ w_in[l]
        ql, kl, vl, gl = mlstm_inputs(pl[..., OFF_Q:OFF_O], pl[..., OFF_K:OFF_VM], pl[..., OFF_VM:OFF_G],
                                      pl[..., OFF_G:], qk_conv[l], b_gate[l])
        h_l, _ = mlstm_bidir(ql, kl, vl, gl, ctx_states, True)
        y_l = stream_mixers(pl, h_l, rows, GRID_W, *mix_args)
        x_lat = x_lat + m_lat[2] * (y_l @ w_out[l])
        hf = modulate(rmsnorm(x_lat, norm_ffn[l]), m_lat[3], m_lat[4])
        x_lat = x_lat + m_lat[5] * peer_ffn(hf, peer_wq[l], peer_keys[l], peer_u[l], peer_v[l])

        if not last:
            x_ctx = x_ctx_new
    return rmsnorm(x_lat, norm_final)


def setup_inputs(seed=0):
    out = dict(first_inputs(seed))
    for name, value in second_inputs(seed + 1).items():
        if name != "x":
            out[name + "_2"] = value
    return out


def reference(
    x, norm_ab, w_in_ab, w_out_ab, lam_ab, subln_ab, norm_c, w_in_c, w_out_c, final_norm, c_2,
    ctx_2, c_ctx_2, ada_w_2, ada_b_2, norm_mix_2, norm_ffn_2, w_in_2, b_gate_2, sgu_norm_2,
    sgu_w_2, sgu_b_2, qk_conv_2, mlstm_norm_2, pool_w_2, pool_scale_2, w_out_2, peer_wq_2,
    peer_keys_2, peer_u_2, peer_v_2, norm_final_2,
):
    x = first_block(
        x, norm_ab, w_in_ab, w_out_ab, lam_ab, subln_ab, norm_c, w_in_c, w_out_c, final_norm,
    )
    return second_block(
        x, c_2, ctx_2, c_ctx_2, ada_w_2, ada_b_2, norm_mix_2, norm_ffn_2, w_in_2, b_gate_2,
        sgu_norm_2, sgu_w_2, sgu_b_2, qk_conv_2, mlstm_norm_2, pool_w_2, pool_scale_2, w_out_2,
        peer_wq_2, peer_keys_2, peer_u_2, peer_v_2, norm_final_2,
    )


_drawn_inputs = setup_inputs


def setup_inputs(seed=0):
    import zlib

    import numpy as np

    out = dict(_drawn_inputs(seed))
    spreads = {}
    factors = {'norm_ab': 3.896,
     'subln_ab': 7.206,
     'norm_c': 8.0,
     'final_norm': 2.671,
     'ctx_2': 4.337,
     'c_ctx_2': 4.682,
     'ada_b_2': 2.958,
     'norm_mix_2': 4.111,
     'norm_ffn_2': 19.4,
     'sgu_norm_2': 8.0,
     'sgu_b_2': 4.645,
     'mlstm_norm_2': 41.325,
     'pool_scale_2': 3.379,
     'qk_conv_2': 3.021}
    for name, (base, spread) in spreads.items():
        noise = np.random.default_rng([zlib.crc32(name.encode()), seed]).standard_normal(out[name].shape)
        drawn = base * np.exp(spread * noise) if base else spread * noise
        out[name] = __import__('jax').numpy.asarray(drawn.astype(out[name].dtype))
    for name, factor in factors.items():
        out[name] = (out[name] * factor).astype(out[name].dtype)
    return out
```

```python
import math
from contextlib import ExitStack

import numpy as np
import concourse.bass as bass
from concourse import mybir

F32, F32R, BF16 = mybir.dt.float32, mybir.dt.float32r, mybir.dt.bfloat16
I32, U32 = mybir.dt.int32, mybir.dt.uint32
ALU, ACT, AX = mybir.AluOpType, mybir.ActivationFunctionType, mybir.AxisListType

P = 128
S = 256
T = S // P
D = 2048
K = D // P
HD = 128
EPS = 1e-6
NEG = -1e30
N = 512
KC = 4
Q = K // KC
RAW = 4
PRE = 4
GRID_W, WINDOWS = 64, (2, 4, 8, 16)
MH, MD = 4, 256
U_AT, V_AT, PL_AT, Q_AT, O_AT, K_AT, VM_AT, G_AT = 0, 512, 1024, 1536, 2560, 3584, 4608, 5632
PH, PK, NK = 8, 16, 128
DIL = ((128, 1), (512, 4), (2048, 16))


def shape_constants():
    pos = np.arange(S, dtype=np.float32)
    inv = (1.0 / (np.float32(10000.0) ** (np.arange(0, HD, 2, dtype=np.float32) / HD))).astype(np.float32)
    ang = pos[:, None] * inv[None, :]
    cos, sin = np.cos(ang), np.sin(ang)
    tiled = lambda a: np.ascontiguousarray(a.reshape(T, P, -1).transpose(1, 0, 2), dtype=np.float32)
    i, j = np.arange(S)[:, None], np.arange(S)[None, :]
    count = sum(((i - j >= 0) & ((i - j) % d == 0) & (i - j <= (w // d) * d)).astype(np.float32) for w, d in DIL)
    eye = np.eye(P, dtype=np.float32)
    return {
        "rope_cos": tiled(np.concatenate([cos, cos], 1)),
        "rope_sin": tiled(np.concatenate([-sin, sin], 1)),
        "dilated_neg": tiled(np.where(count > 0, 0, NEG)),
        "dilated_count": tiled(count),
        "causal_neg": tiled(np.where(i >= j, 0, NEG)),
        "eye": eye,
        "flip": np.ascontiguousarray(eye[::-1]),
        "order_neg": np.ascontiguousarray(np.stack([np.where(eye.cumsum(1) > 0, 0, NEG), np.where(eye.cumsum(1).T > 0, 0, NEG)], 1), dtype=np.float32),
        "windows": window_tables(),
        "band": np.ascontiguousarray(np.broadcast_to((np.arange(2 * P) == P - 1).astype(np.float32), (P, 2 * P))),
        "count16": np.ascontiguousarray(np.broadcast_to(np.arange(16, dtype=np.float32), (P, 16))),
    }


def window_tables():
    rows, cols = S // GRID_W, GRID_W
    both = []
    for w in WINDOWS:
        bound = lambda n: (np.clip(np.arange(n) - w // 2, 0, n), np.clip(np.arange(n) - w // 2 + w, 0, n))
        (rlo, rhi), (clo, chi) = bound(rows), bound(cols)
        r, c = np.arange(S) // cols, np.arange(S) % cols
        inside = ((r[:, None] >= rlo[r]) & (r[:, None] < rhi[r]) & (c[:, None] >= clo[c]) & (c[:, None] < chi[c]))
        count = (rhi - rlo)[r] * (chi - clo)[c]
        both.append(inside / count[None, :] - np.eye(S))
    table = np.stack(both, 1).reshape(T, P, len(WINDOWS), S).transpose(1, 0, 2, 3)
    return np.ascontiguousarray(table, dtype=np.float32)


def bass_hybrid_stack_kernel(nc, A, out):
    ctx = ExitStack()
    with ctx:
        BASE = 16512
        H_AT = BASE
        X_AT = H_AT + 65536
        XT_AT = X_AT + 16384
        RAW_AT = XT_AT + 32768
        WS_AT = RAW_AT + 32768
        C_AT = WS_AT + 32768
        cursor = [C_AT]

        def at(name, shape, offset, dt=F32):
            return nc.alloc_sbuf_tensor_at(name, shape, dt, offset=offset)

        def const(name, shape, dt=F32):
            t = at(name, shape, cursor[0], dt)
            size = int(np.prod(shape[1:])) * (2 if dt == BF16 else 4)
            cursor[0] += -(-size // 32) * 32
            assert cursor[0] <= 229368, (name, cursor[0])
            return t

        def sem(name):
            return ctx.enter_context(nc.semaphore(name))

        h = at("h", [P, T, 4 * D], H_AT)
        x = at("x", [P, T, D], X_AT)
        xt_hi = at("xt_hi", [P, K, S], XT_AT, F32R)
        xt_lo = at("xt_lo", [P, K, S], XT_AT + 16384, F32R)
        raw = at("raw", [P, RAW, KC, N], RAW_AT)
        w_hi = at("w_hi", [P, 2, KC * N], WS_AT, F32R)
        w_lo = at("w_lo", [P, 2, KC * N], WS_AT + 16384, F32R)
        xn = at("xn", [P, T, D], WS_AT)
        xf = at("xf", [P, 2, 4 * P], WS_AT + 16384)

        eye = const("eye_sb", [P, P])
        ones = const("ones", [P, P])
        small = const("small", [P, 64])
        g_ab = const("g_ab", [P, K])
        g_c = const("g_c", [P, K])
        first_const = cursor[0]
        rope_cos = const("rope_cos_sb", [P, T, HD])
        rope_sin = const("rope_sin_sb", [P, T, HD])
        dil_neg = const("dil_neg", [P, T, S])
        dil_count = const("dil_count", [P, T, S])
        cau_neg = const("cau_neg", [P, T, S])
        subln = const("subln", [P, 256])
        lam_in = const("lam_in", [P, 4])
        lam = const("lam", [P, 4])

        rot1 = at("rot1", [P, T, 2 * HD], XT_AT)
        rot2 = at("rot2", [P, T, 2 * HD], XT_AT + 2048)
        qk_rot = [[at(f"qk_rot{i}{s}", [P, T, 2 * HD], XT_AT + 4096 + (2 * s + i) * 2048) for i in range(2)] for s in range(2)]
        qk_t = [[at(f"qk_t{i}{s}", [P, 2, S], XT_AT + 12288 + (2 * s + i) * 2048) for i in range(2)] for s in range(2)]
        prob = [at(f"prob{s}", [P, 2, P + S], XT_AT + 20480 + s * 3072) for s in range(2)]
        prob_t = [at(f"prob_t{s}", [P, 2, 3 * P], XT_AT + 26624 + s * 3072) for s in range(2)]
        stat = [at(f"stat{s}", [P, 20], WS_AT + s * 128) for s in range(2)]
        sub_sq = at("sub_sq", [P, 1024], WS_AT + 1024)
        row_w = at("row_w", [P, D], XT_AT)

        cursor[0] = max(cursor[0], first_const)
        m_row = [const(f"m_row{i}", [P, D]) for i in range(2)]
        m_col = const("m_col", [P, 12, K])
        ada_bias = const("ada_bias", [P, 6, K])
        ada_bias_row = at("ada_bias_row", [1, 2, D], X_AT - 16384)
        c_col = const("c_col", [P, 2, K])
        g_mix = const("g_mix", [P, K])
        g_ffn = const("g_ffn", [P, K])
        mod = const("mod", [P, 3, K])
        gate_b = const("gate_b", [P, 16])
        gates = const("gates", [P, T, 16])
        wg = const("wg", [P, K, 16])
        after_ada = cursor[0]
        cursor[0] = first_const
        wg_hi = const("wg_hi", [P, K, 16], F32R)
        wg_lo = const("wg_lo", [P, K, 16], F32R)
        flip = const("flip_sb", [P, P])
        order_neg = const("order_neg_sb", [P, 2, P])
        conv_w = const("conv_w", [P, 16, 3])
        pick = const("pick", [MH, MH, P])
        m_now = const("m_now", [MH, 2])
        m_from = const("m_from", [MH, 2, 2])
        m_to = const("m_to", [MH, 2, 2])
        decay_x = const("decay_x", [MH, 4, MH])
        col = const("col", [P, 64])
        sgu_b = const("sgu_b_sb", [P, 4])
        acc = [[at(f"acc{i}{v}", [P, D], WS_AT + (2 * i + v) * 8192) for v in range(2)] for i in range(2)]
        q_t = at("q_t", [P, 8, S], XT_AT)
        k_t = at("k_t", [P, 8, S], XT_AT + 8192)
        rows = {n: at(f"row_{n}", [MH, 2, S], XT_AT + 16384 + i * 2048) for i, n in enumerate(("i", "f", "b", "m", "a_true", "nm_true", "wk", "wp"))}
        rows["th"] = at("row_th", [MH, 2, S], WS_AT + 30720)
        v_one = at("v_one", [P, T, MH, MD + 1], WS_AT)
        v_weighed = [at(f"v_weighed{i}", [P, MD + 1], WS_AT + 8256 + i * 1056) for i in range(2)]
        from_state = [at(f"from_state{i}", [P, MD + 1], WS_AT + 10368 + i * 1056) for i in range(2)]
        num = [at(f"num{i}", [P, MD + 1], WS_AT + 12480 + i * 1056) for i in range(2)]
        e_arg = [at(f"e_arg{i}", [P, P], WS_AT + 14592 + i * 512) for i in range(2)]
        p_t = [at(f"p_t{i}", [P, P], WS_AT + 15616 + i * 512) for i in range(2)]
        conv = [at(f"conv{i}", [P, S], WS_AT + 16640 + i * 1024) for i in range(2)]
        mlstm_g = at("mlstm_g", [P, 1024], WS_AT + 18688)
        square = at("square", [P, 1024], WS_AT + 22784)

        def state(d, hh, b):
            o = 5632 + (hh * 2 + b) * (MD + 1)
            return h[:, d, o:o + MD + 1]

        sgu_w = at("sgu_w_sb", [P, 4, P], WS_AT)
        sgu_g = at("sgu_g", [P, 512], WS_AT + 2048)
        pool_w = at("pool_w_sb", [P, 4, P], WS_AT + 4096)
        pool_g = at("pool_g", [P, 512], WS_AT + 6144)
        windows = at("windows_sb", [P, T, 4, S], WS_AT + 8192)
        pooled = [at(f"pooled{i}", [P, S], WS_AT + 16384 + i * 1024) for i in range(4)]
        full = at("full", [P, K, S], H_AT + 8192)
        parts = at("parts", [P, T, 3, D], H_AT + 40960, BF16)
        rest = at("rest", [P, 2, 512], WS_AT)
        hf_rows = nc.dram_tensor("hf_rows", (3, S, D), BF16, kind="Internal").ap()
        keys = at("keys", [P, 2, NK], RAW_AT)
        pq_t = at("pq_t", [P, K, S], XT_AT)
        key_s = at("key_s", [P, T, 16, NK], XT_AT + 16384)
        less = at("less", [P, 2, S], RAW_AT + 1024)
        top_v = at("top_v", [P, T, 16, 16], RAW_AT + 4096)
        top_i = at("top_i", [P, T, 16, 16], RAW_AT + 6144, U32)
        top_f = at("top_f", [P, T, 16, 16], RAW_AT + 8192)
        cand = at("cand", [P, 2, 256], RAW_AT + 10240)
        best_v = at("best_v", [P, T, PH, PK], RAW_AT + 12288)
        best_i = at("best_i", [P, T, PH, PK], RAW_AT + 13312, U32)
        best_s = at("best_s", [P, 2, PH * PK], RAW_AT + 14336, U32)
        best_f = at("best_f", [P, 2, PH * PK], RAW_AT + 15360)
        side = at("side", [P, 2, PH * PK], RAW_AT + 16384)
        expert_f = at("expert_f", [P, T, PH * PK], RAW_AT + 17408)
        gate_f = at("gate_f", [P, T, PH * PK], RAW_AT + 18432)
        gate_s = at("gate_s", [P, 32], RAW_AT + 19456)
        count16 = at("count16_sb", [P, 16], RAW_AT + 19584)
        match = at("match", [P, PH * PK, 16], WS_AT)
        cursor[0] = first_const
        idx = const("idx", [P, S], U32)
        gate_t = const("gate_t", [P, S])
        band = const("band_sb", [P, 2 * P])
        three = const("three", [3, P], BF16)
        idx4 = [const(f"idx4{i}", [P, 4], U32) for i in range(2)]
        act_in = const("act_in", [P, 8])
        act_half = const("act_half", [P, 8])
        act_out = const("act_out", [P, 8])
        u_ring = at("u_ring", [P, 4, D], RAW_AT)
        v_ring = at("v_ring", [P, 4, D], WS_AT)
        row_ring = [at(f"row_ring{i}", [3, 8, D], H_AT + i * 32768, BF16) for i in range(2)]
        z_ring = [at(f"z_ring{i}", [P, P], XT_AT + i * 512) for i in range(4)]
        zero_w = at("zero_w", [P, 512], XT_AT + 2048)
        xe = at("xe", [P, D], XT_AT + 4096)
        last_w = at("last_w", [P, D], XT_AT + 12288)
        gated = at("gated", [P, T, N], H_AT)

        bank = ctx.enter_context(nc.psum_tensor("bank", [P, 8, 512], F32))

        x_landed, const_landed, aux_landed = sem("x_landed"), sem("const_landed"), sem("aux_landed")
        w_landed = [sem(f"w_landed{i}") for i in range(RAW)]
        out_stored = sem("out_stored")
        stage_done = sem("stage_done")
        passed, passed_pool = sem("passed"), sem("passed_pool")
        raw_used = sem("raw_used")
        hi_ready = sem("hi_ready")
        chunk_multiplied = sem("chunk_multiplied")
        evacuated = sem("evacuated")
        norm_step, act_step = sem("norm_step"), sem("act_step")
        blocks_turned, block_scaled, hi_written, lo_written = sem("blocks_turned"), sem("block_scaled"), sem("hi_written"), sem("lo_written")
        roped, qk_turned, qk_copied, scored, shifted = sem("roped"), sem("qk_turned"), sem("qk_copied"), sem("scored"), sem("shifted")
        exped, weighed, p_turned, p_copied, mixed, mix_taken = (sem(n) for n in ("exped", "weighed", "p_turned", "p_copied", "mixed", "mix_taken"))

        names = """silu_done acc_ready acc_summed row_taken gates_multiplied ml_a ml_row ml_exp conv_turned convolved conv_silu
            upd_weighed upd_multiplied upd_taken ml_weighted ml_scored ml_taken ml_mixed ml_exponent ml_exped ml_scaled
            mix_ready mix_multiplied mix_scaled mix_gelu mix_square out_root out_square full_ready part_copied part_rest part_low
            back_turned hf_stored pq_copied pq_turned keys_copied keys_scored gate_shifted gate_exped chosen chosen_turned
            rings_free half_spread halves_read summed spread_weight tile_taken tile_summed gelued wg_ready"""
        (silu_done, acc_ready, acc_summed, row_taken, gates_multiplied, ml_a, ml_row, ml_exp, conv_turned, convolved, conv_silu,
         upd_weighed, upd_multiplied, upd_taken, ml_weighted, ml_scored, ml_taken, ml_mixed, ml_exponent, ml_exped, ml_scaled,
         mix_ready, mix_multiplied, mix_scaled, mix_gelu, mix_square, out_root, out_square, full_ready, part_copied, part_rest, part_low,
         back_turned, hf_stored, pq_copied, pq_turned, keys_copied, keys_scored, gate_shifted, gate_exped, chosen, chosen_turned,
         rings_free, half_spread, halves_read, summed, spread_weight, tile_taken, tile_summed, gelued, wg_ready) = (sem(n) for n in names.split())
        rows_landed = [sem(f"rows_landed{i}") for i in range(2)]
        u_landed = [sem(f"u_landed{i}") for i in range(4)]
        v_landed = [sem(f"v_landed{i}") for i in range(4)]

        block = ctx.enter_context(nc.Block())

        plan = {}
        chunks = tiles = 0
        for name, n in (("ab_in", 16), ("ab_out", 4), ("c_in", 16), ("c_out", 4)):
            plan[name] = dict(n=n, c0=chunks, g0=chunks, t0=tiles)
            chunks += n * Q
            tiles += n
        weights = {"ab_in": A["w_in_ab"][0], "ab_out": A["w_out_ab"][0], "c_in": A["w_in_c"][0], "c_out": A["w_out_c"][0]}
        ADA_C0 = chunks
        chunks += 6 * K
        groups = ADA_C0
        for name, n, first in (("ctx", 4, K_AT), ("lat", 11, 0), ("mix_out", 4, 0), ("wq", 4, 0)):
            plan[name] = dict(n=n, c0=chunks, g0=groups, t0=tiles, **{"from": first})
            chunks += n * Q
            groups += n * Q
            tiles += n + n % 2
        weights.update(ctx=A["w_in_2"][0], lat=A["w_in_2"][0], mix_out=A["w_out_2"][0], wq=A["peer_wq_2"][0])

        stages = {"pe": 0, "act": 0, "dve": 0, "pool": 0}

        def end_of_stage(eng, who):
            stages[who] += 1
            eng.drain().then_inc(stage_done, 1)
            eng.wait_ge(stage_done, 4 * stages[who])

        def wide(ap, shape):
            return ap.broadcast_to(shape)

        def stream_sp(sp, g):
            w = weights[g["name"]].rearrange("(q k p) n -> q p k n", k=KC, p=P)

            def tile(n, dt):
                for q in range(Q):
                    c = g["c0"] + Q * n + q
                    sp.wait_ge(raw_used, c + 1)
                    sp.dma_start(raw[:, q, :, :], w[q][:, :, dt(n)]).then_inc(w_landed[q], 16)

            with sp.Fori(0, g["n"]) as n:
                tile(n, lambda n: bass.ds(n * N + g.get("from", 0), N))

        def pairs_then_rest(eng, n, body, start=0):
            m = (n - start) // 2
            if m:
                with eng.Fori(0, m) as i:
                    for s in range(2):
                        body(2 * i + start + s, (start + s) % 2)
            if (n - start) % 2:
                body(n - 1, (n - 1) % 2)

        def gemm_act(act, g):
            def tile(n, s):
                for q in range(Q):
                    c, r = g["c0"] + Q * n + q, g["g0"] + Q * n + q
                    act.wait_ge(w_landed[q], 16 * (g["c0"] // Q + n + 1))
                    act.wait_ge(chunk_multiplied, PRE + r - 1)
                    act.activation(w_hi[:, q % 2, :], raw[:, q, :, :].rearrange("p k n -> p (k n)"), ACT.Copy).then_inc(hi_ready, 1)
            pairs_then_rest(act, g["n"], tile)

        def gemm_pe(pe, g):
            def tile(n, s):
                pe.wait_ge(evacuated, PRE + g["t0"] + n - 1)
                for q in range(Q):
                    pe.wait_ge(raw_used, PRE + g["c0"] + Q * n + q + 1)
                    for k in range(KC):
                        kk = q * KC + k
                        for t in range(T):
                            o = bank[:, 2 * s + t, :]
                            a_hi, a_lo = xt_hi[:, kk, t * P:(t + 1) * P], xt_lo[:, kk, t * P:(t + 1) * P]
                            b_hi, b_lo = w_hi[:, q % 2, k * N:(k + 1) * N], w_lo[:, q % 2, k * N:(k + 1) * N]
                            pe.matmul(o, a_hi, b_hi, start=kk == 0, stop=False)
                            pe.matmul(o, a_hi, b_lo, start=False, stop=False)
                            last = pe.matmul(o, a_lo, b_hi, start=False, stop=kk == K - 1)
                    last.then_inc(chunk_multiplied, 1)
            pairs_then_rest(pe, g["n"], tile)

        def gemm_dve(dve, g, take):
            def low(n, q):
                r = g["g0"] + Q * n + q
                dve.wait_ge(hi_ready, PRE + r + 1)
                dve.tensor_tensor(w_lo[:, q % 2, :], raw[:, q, :, :].rearrange("p k n -> p (k n)"),
                                  w_hi[:, q % 2, :].bitcast(F32), ALU.subtract).then_inc(raw_used, 1)

            def evacuate(n, s):
                dve.wait_ge(chunk_multiplied, PRE + g["g0"] + Q * (n + 1))
                take(dve, n, s)

            def step(n, s):
                low(n, 0)
                low(n, 1)
                evacuate(n - 1, 1 - s)
                low(n, 2)
                low(n, 3)

            for q in range(Q):
                low(0, q)
            pairs_then_rest(dve, g["n"], step, 1)
            evacuate(g["n"] - 1, (g["n"] - 1) % 2)
            if g["n"] % 2:
                dve.sem_inc(evacuated, 1)

        def take_h(dve, n, s, to=0):
            for t in range(T):
                last = dve.tensor_scalar(h[:, t, bass.ds(n * N + to, N)], bank[:, 2 * s + t, :], 1.0, None, ALU.mult)
            last.then_inc(evacuated, 1)

        def take_residual(dve, n, s):
            for t in range(T):
                o = x[:, t, bass.ds(n * N, N)]
                last = dve.tensor_tensor(o, bank[:, 2 * s + t, :], o, ALU.add)
            last.then_inc(evacuated, 1)

        NG = T * Q

        def newton(dve, r, root, v, tmp):
            dve.reciprocal(r, root)
            dve.drain()
            dve.tensor_tensor(tmp, r, r, ALU.mult)
            dve.drain()
            dve.tensor_tensor(tmp, tmp, v, ALU.mult)
            dve.drain()
            dve.tensor_scalar(tmp, tmp, -0.5, 1.5, ALU.mult, ALU.add)
            dve.drain()
            dve.tensor_tensor(r, r, tmp, ALU.mult)

        def rstd_act(act, src, u, width=D):
            for t in range(T):
                last = act.activation(xn[:, t, :], src[:, t, :], ACT.Square, accum_out=small[:, t:t + 1])
            last.then_inc(act_step, 1)
            act.wait_ge(norm_step, PRE + 3 * u + 1)
            act.activation(small[:, 4:4 + T], small[:, 2:2 + T], ACT.Sqrt).then_inc(act_step, 1)

        def rstd_dve(dve, u):
            dve.wait_ge(act_step, PRE + 2 * u + 1)
            dve.tensor_scalar(small[:, 2:2 + T], small[:, 0:T], 1.0 / D, EPS, ALU.mult, ALU.add).then_inc(norm_step, 1)
            dve.wait_ge(act_step, PRE + 2 * u + 2)
            newton(dve, small[:, 6:6 + T], small[:, 4:4 + T], small[:, 2:2 + T], small[:, 62:62 + T])
            dve.drain().then_inc(norm_step, 1)

        def turn_pe(pe, v, src, rows, column=lambda kk: kk * P):
            if rows:
                pe.wait_ge(norm_step, rows)
            for g in range(NG):
                t, b = g // Q, g % 4
                if g >= 4:
                    pe.wait_ge(lo_written, PRE + NG * v + g - 3)
                for j in range(4):
                    kk = (g % Q) * 4 + j
                    last = pe.transpose(bank[:, b, j * P:(j + 1) * P], src[:, t, column(kk):column(kk) + P], eye[:, :])
                last.then_inc(blocks_turned, 1)

        def group(xt, g):
            return xt[:, (g % Q) * 4:(g % Q) * 4 + 4, (g // Q) * P:(g // Q + 1) * P]

        def turned(g):
            return bank[:, g % 4, :].rearrange("p (k n) -> p k n", k=4)

        def turn_act(act, v, scaled):
            for g in range(NG):
                if scaled:
                    act.wait_ge(block_scaled, PRE + scaled[1] + g + 1)
                    src = xf[:, g % 2, :].rearrange("p (k n) -> p k n", k=4)
                else:
                    act.wait_ge(blocks_turned, PRE + NG * v + g + 1)
                    src = turned(g)
                act.activation(group(xt_hi, g), src, ACT.Copy).then_inc(hi_written, 1)

        def turn_dve(dve, v, scaled):
            for g in range(NG):
                src = turned(g)
                if scaled:
                    (scale, shift), s0 = scaled
                    f = xf[:, g % 2, :].rearrange("p (k n) -> p k n", k=4)
                    c = slice((g % Q) * 4, (g % Q) * 4 + 4)
                    dve.wait_ge(blocks_turned, PRE + NG * v + g + 1)
                    last = dve.tensor_tensor(f, src, wide(scale[:, c].unsqueeze(2), [P, 4, P]), ALU.mult)
                    if shift is not None:
                        dve.drain()
                        last = dve.tensor_tensor(f, f, wide(shift[:, c].unsqueeze(2), [P, 4, P]), ALU.add)
                    last.then_inc(block_scaled, 1)
                    src = f
                dve.wait_ge(hi_written, PRE + NG * v + g + 1)
                dve.tensor_tensor(group(xt_lo, g), src, group(xt_hi, g).bitcast(F32), ALU.subtract).then_inc(lo_written, 1)
                if scaled:
                    dve.drain()

        SCALE = HD ** -0.5
        W = (P, S)
        OFF = (0, P)

        def rope_dve(dve, a, p, s):
            g = a["p0"] + p
            for i, off in ((0, a["q"]), (1, a["k"])):
                src = h[:, :, bass.ds(p * 256 + off, 256)].rearrange("p t (h d) -> p t h d", h=2)
                tw = lambda b: b.rearrange("p t (h d) -> p t h d", h=2)
                r1, r2, dst = tw(rot1[:, :, :]), tw(rot2[:, :, :]), tw(qk_rot[s][i][:, :, :])
                cos = wide(rope_cos[:, :, :].unsqueeze(2), [P, T, 2, HD])
                sin = wide(rope_sin[:, :, :].unsqueeze(2), [P, T, 2, HD])
                dve.drain()
                dve.tensor_tensor(r1, src, cos, ALU.mult)
                dve.tensor_tensor(r2[:, :, :, 0:64], src[:, :, :, 64:128], sin[:, :, :, 0:64], ALU.mult)
                dve.tensor_tensor(r2[:, :, :, 64:128], src[:, :, :, 0:64], sin[:, :, :, 64:128], ALU.mult)
                dve.drain()
                dve.wait_ge(qk_turned, PRE + g - 1)
                dve.tensor_tensor(dst, r1, r2, ALU.add).then_inc(roped, 1)

        def turn_qk_pe(pe, a, p, s):
            g = a["p0"] + p
            pe.wait_ge(roped, PRE + 2 * (g + 1))
            pe.wait_ge(qk_copied, PRE + g)
            for i in range(2):
                for hh in range(2):
                    for t in range(T):
                        last = pe.transpose(bank[:, i, (hh * T + t) * P:(hh * T + t + 1) * P],
                                            qk_rot[s][i][:, t, hh * HD:(hh + 1) * HD], eye[:, :])
            last.then_inc(qk_turned, 1)

        def copy_qk_act(act, a, p, s):
            g = a["p0"] + p
            act.wait_ge(qk_turned, PRE + g + 1)
            act.wait_ge(scored, PRE + g - 1)
            for i in range(2):
                last = act.activation(qk_t[s][i][:, :, :].rearrange("p h n -> p (h n)"), bank[:, i, :], ACT.Copy)
            last.then_inc(qk_copied, 1)

        def score_pe(pe, a, p, s):
            g = a["p0"] + p
            pe.wait_ge(qk_copied, PRE + g + 1)
            pe.wait_ge(shifted, PRE + g)
            for t in range(T):
                for hh in range(2):
                    last = pe.matmul(bank[:, 2 + t, hh * S:hh * S + W[t]], qk_t[s][0][:, hh, t * P:(t + 1) * P],
                                     qk_t[s][1][:, hh, 0:W[t]], start=True, stop=True)
            last.then_inc(scored, 1)

        def shift_dve(dve, a, p, s):
            g = a["p0"] + p
            dve.wait_ge(scored, PRE + g + 1)
            dve.wait_ge(p_turned, PRE + g - 1)
            dve.sem_inc(passed, 1)
            for t in range(T):
                for hh in range(2):
                    last = dve.tensor_tensor_reduce(prob[s][:, hh, OFF[t]:OFF[t] + W[t]], bank[:, 2 + t, hh * S:hh * S + W[t]],
                                                    a["neg"][:, t, 0:W[t]], SCALE, NEG, ALU.add, ALU.max,
                                                    stat[s][:, 2 * t + hh:2 * t + hh + 1])
            dve.drain()
            dve.tensor_scalar(stat[s][:, 4:8], stat[s][:, 0:4], -1.0, None, ALU.mult).then_inc(shifted, 1)

        def exp_act(act, a, p, s):
            g = a["p0"] + p
            act.wait_ge(shifted, PRE + g + 1)
            for t in range(T):
                for hh in range(2):
                    c = 2 * t + hh
                    e = prob[s][:, hh, OFF[t]:OFF[t] + W[t]]
                    last = act.activation(e, e, ACT.Exp, bias=stat[s][:, 4 + c:5 + c], accum_out=stat[s][:, 8 + c:9 + c])
            last.then_inc(exped, 1)

        def weigh_dve(dve, a, p, s):
            g = a["p0"] + p
            dve.wait_ge(exped, PRE + g + 1)
            if a["kind"] == "dilated":
                dve.sem_inc(passed, 1)
                for t in range(T):
                    for hh in range(2):
                        c = 2 * t + hh
                        e = prob[s][:, hh, OFF[t]:OFF[t] + W[t]]
                        dve.tensor_tensor_reduce(e, e, dil_count[:, t, 0:W[t]], 1.0, 0.0, ALU.mult, ALU.add,
                                                 stat[s][:, 8 + c:9 + c])
                dve.drain()
            last = dve.reciprocal(stat[s][:, 12:16], stat[s][:, 8:12])
            if a["kind"] == "difference":
                dve.drain()
                for t in range(T):
                    dve.tensor_scalar(stat[s][:, 16 + t:17 + t], stat[s][:, 13 + 2 * t:14 + 2 * t], lam[:, 2:3], None, ALU.mult)
                dve.drain()
                for t in range(T):
                    e = prob[s][:, 1, OFF[t]:OFF[t] + W[t]]
                    dve.tensor_scalar(e, e, stat[s][:, 16 + t:17 + t], None, ALU.mult)
                dve.drain()
                for t in range(T):
                    e = prob[s][:, 0, OFF[t]:OFF[t] + W[t]]
                    last = dve.scalar_tensor_tensor(e, e, stat[s][:, 12 + 2 * t:13 + 2 * t], prob[s][:, 1, OFF[t]:OFF[t] + W[t]],
                                                    ALU.mult, ALU.add)
            last.then_inc(weighed, 1)

        def heads_of(a):
            return 1 if a["kind"] == "difference" else 2

        def turn_p_pe(pe, a, p, s):
            g = a["p0"] + p
            pe.wait_ge(weighed, PRE + g + 1)
            pe.wait_ge(p_copied, PRE + g)
            for hh in range(heads_of(a)):
                for b in range(3):
                    last = pe.transpose(bank[:, 4 + hh, b * P:(b + 1) * P], prob[s][:, hh, b * P:(b + 1) * P], eye[:, :])
            last.then_inc(p_turned, 1)

        def copy_p_act(act, a, p, s):
            g = a["p0"] + p
            act.wait_ge(p_turned, PRE + g + 1)
            act.wait_ge(mixed, PRE + g - 1)
            for hh in range(heads_of(a)):
                last = act.activation(prob_t[s][:, hh, :], bank[:, 4 + hh, 0:3 * P], ACT.Copy)
            last.then_inc(p_copied, 1)

        def mix_pe(pe, a, p, s):
            g = a["p0"] + p
            w = 256 // heads_of(a)
            pe.wait_ge(p_copied, PRE + g + 1)
            pe.wait_ge(mix_taken, PRE + g)
            for hh in range(heads_of(a)):
                v = [h[:, t, bass.ds(p * 256 + (a["v"] + hh * w), w)] for t in range(T)]
                o = [bank[:, 6, t * 256 + hh * w:t * 256 + hh * w + w] for t in range(T)]
                pe.matmul(o[0], prob_t[s][:, hh, 0:P], v[0], start=True, stop=True)
                pe.matmul(o[1], prob_t[s][:, hh, P:2 * P], v[0], start=True, stop=False)
                last = pe.matmul(o[1], prob_t[s][:, hh, 2 * P:3 * P], v[1], start=False, stop=True)
            last.then_inc(mixed, 1)

        def out_dve(dve, a, p, s):
            g = a["p0"] + p
            dve.wait_ge(mixed, PRE + g + 1)
            for t in range(T):
                if a["kind"] == "difference":
                    last = dve.tensor_scalar(h[:, t, bass.ds(p * 256 + a["q"], 256)], bank[:, 6, t * 256:(t + 1) * 256], 1.0, None, ALU.mult)
                else:
                    for hh in range(2):
                        z = h[:, t, bass.ds(p * 256 + (a["z"] + hh * HD), HD)]
                        last = dve.scalar_tensor_tensor(z, bank[:, 6, t * 256 + hh * HD:t * 256 + (hh + 1) * HD],
                                                        stat[s][:, 12 + 2 * t + hh:13 + 2 * t + hh], z, ALU.mult, ALU.mult)
            last.then_inc(mix_taken, 1)

        def steps(eng, n, step):
            if n > 2:
                with eng.Fori(0, (n - 2) // 2) as i:
                    step(2 * i, 0, 2)
                    step(2 * i + 1, 1, 2)
            step(n - 2, 0, 1)
            step(n - 1, 1, 0)

        def attention_pe(pe, a):
            def step(p, s, ahead):
                if ahead:
                    turn_qk_pe(pe, a, p + 1, 1 - s)
                turn_p_pe(pe, a, p, s)
                if ahead:
                    score_pe(pe, a, p + 1, 1 - s)
                mix_pe(pe, a, p, s)
            turn_qk_pe(pe, a, 0, 0)
            score_pe(pe, a, 0, 0)
            steps(pe, a["n"], step)

        def attention_act(act, a):
            def step(p, s, ahead):
                if ahead:
                    copy_qk_act(act, a, p + 1, 1 - s)
                copy_p_act(act, a, p, s)
                if ahead:
                    exp_act(act, a, p + 1, 1 - s)
            copy_qk_act(act, a, 0, 0)
            exp_act(act, a, 0, 0)
            steps(act, a["n"], step)

        def attention_dve(dve, a):
            def step(p, s, ahead):
                if ahead > 1:
                    rope_dve(dve, a, p + 2, s)
                if ahead:
                    shift_dve(dve, a, p + 1, 1 - s)
                out_dve(dve, a, p, s)
                if ahead:
                    weigh_dve(dve, a, p + 1, 1 - s)
            rope_dve(dve, a, 0, 0)
            rope_dve(dve, a, 1, 1)
            shift_dve(dve, a, 0, 0)
            weigh_dve(dve, a, 0, 0)
            steps(dve, a["n"], step)

        ATT = {
            "a": dict(kind="dilated", n=4, p0=0, q=0, k=1024, v=2048, z=6144, neg=dil_neg),
            "b": dict(kind="difference", n=4, p0=4, q=3072, k=4096, v=5120, z=7168, neg=cau_neg),
            "c": dict(kind="causal", n=8, p0=8, q=0, k=2048, v=4096, z=6144, neg=cau_neg),
        }
        LAM_INIT = 0.8 - 0.6 * math.exp(-0.3 * 0)
        for name in plan:
            plan[name]["name"] = name
        gate = lambda b: b[:, :, 6144:8192]

        ADA = dict(c0=ADA_C0)
        NV = lambda g: 2 if g < 2 else 1

        def ada_sp(sp):
            w = A["ada_w_2"][0].rearrange("(k p) n -> k p n", p=P)
            for g in range(6):
                with sp.Fori(0, K // RAW) as i:
                    for j in range(RAW):
                        sp.wait_ge(raw_used, ADA["c0"] + g * K + RAW * i + j + 1)
                        sp.dma_start(raw[:, j, :, :].rearrange("p k n -> p (k n)"),
                                     w[bass.ds(RAW * i + j, 1), :, g * D:(g + 1) * D].rearrange("o p n -> p (o n)")).then_inc(w_landed[j], 16)

        def ada_act(act):
            act.activation(c_col[:, :, :], c_col[:, :, :], ACT.Silu).then_inc(silu_done, 1)
            for i, g in enumerate((2, 5)):
                act.wait_ge(acc_summed, g + 1)
                act.activation(m_row[i][:, :].rearrange("p (c n) -> p c n", c=4), bank[:, 4:8, :], ACT.Copy).then_inc(row_taken, 1)

        def ada_dve(dve):
            dve.wait_ge(silu_done, 1)
            for g in range(6):
                if g >= 2:
                    dve.wait_ge(acc_summed, g - 1)
                for v in range(NV(g)):
                    dve.memset(acc[g % 2][v][:, :], 0.0)
                with dve.Fori(0, K // RAW) as i:
                    for j in range(RAW):
                        dve.drain()
                        dve.wait_ge(w_landed[j], 16 * ((ADA["c0"] + g * K) // RAW + 1 + i))
                        for v in range(NV(g)):
                            o = acc[g % 2][v][:, :]
                            last = dve.scalar_tensor_tensor(o, raw[:, j, :, :].rearrange("p k n -> p (k n)"),
                                                            c_col[:, v, bass.ds(RAW * i + j, 1)], o, ALU.mult, ALU.add)
                        last.then_inc(raw_used, 1)
                dve.drain().then_inc(acc_ready, 1)
            dve.wait_ge(acc_summed, 6)
            for v in range(2):
                for g in (0, 1) if v else (0, 1, 3, 4):
                    o = (v * 6 + g) * K
                    dve.tensor_tensor(m_col[:, v * 6 + g, :], bank[:, 0, o:o + K], ada_bias[:, g, :], ALU.add)
            dve.drain()
            for i, (v, g, norm) in enumerate(((1, 1, g_mix), (0, 1, g_mix), (0, 4, g_ffn))):
                dve.scalar_tensor_tensor(mod[:, i, :], m_col[:, v * 6 + g, :], 1.0, norm[:, :], ALU.add, ALU.mult)

        def ada_pe(pe):
            for g in range(6):
                pe.wait_ge(acc_ready, g + 1)
                if g in (2, 5):
                    if g == 5:
                        pe.wait_ge(row_taken, 1)
                    for c in range(4):
                        pe.matmul(bank[:, 4 + c, :], ones[:, :], acc[g % 2][0][:, c * 512:(c + 1) * 512], start=True, stop=False)
                        last = pe.matmul(bank[:, 4 + c, :], ones[0:1, :], ada_bias_row[0:1, g // 3, c * 512:(c + 1) * 512], start=False, stop=True)
                else:
                    for v in range(NV(g)):
                        for kk in range(K):
                            o = (v * 6 + g) * K + kk
                            last = pe.matmul(bank[:, 0, o:o + 1], acc[g % 2][v][:, kk * P:(kk + 1) * P], ones[:, 0:1], start=True, stop=True)
                last.then_inc(acc_summed, 1)

        def gates_pe(pe, u):
            for t in range(T):
                for kk in range(K):
                    a_hi, a_lo = xt_hi[:, kk, t * P:(t + 1) * P], xt_lo[:, kk, t * P:(t + 1) * P]
                    o = bank[:, 4 + t, 0:16]
                    pe.matmul(o, a_hi, wg_hi[:, kk, :], start=kk == 0, stop=False)
                    pe.matmul(o, a_hi, wg_lo[:, kk, :], start=False, stop=False)
                    last = pe.matmul(o, a_lo, wg_hi[:, kk, :], start=False, stop=kk == K - 1)
            last.then_inc(gates_multiplied, 1)

        def gates_dve(dve, u):
            dve.wait_ge(gates_multiplied, u + 1)
            for t in range(T):
                dve.tensor_tensor(gates[:, t, :], bank[:, 4 + t, 0:16], gate_b[:, :], ALU.add)

        r_ = lambda n: rows[n][:, :, :]
        chunk = lambda n: rows[n][:, :, :].rearrange("h d (c n) -> h d c n", c=2)

        def ml_rows_pe(pe):
            for kind in range(2):
                for d in range(2):
                    for ci in range(2):
                        t = 1 - ci if d else ci
                        o = (d * 2 + ci) * P
                        last = pe.matmul(bank[0:MH, 4 + kind, o:o + P], gates[:, t, d * 8 + kind * 4:d * 8 + kind * 4 + 4],
                                         (flip if d else eye)[:, :], start=True, stop=True)
            last.then_inc(ml_a, 1)

        def ml_rows_dve(dve, u):
            dve.wait_ge(ml_a, 2 * u + 1)
            for kind, n in ((0, "i"), (1, "f")):
                dve.tensor_copy(r_(n), bank[0:MH, 4 + kind, :].rearrange("h (d n) -> h d n", d=2))
            dve.drain()
            dve.scalar_tensor_tensor(r_("b"), r_("f"), -1.0, r_("f"), ALU.mult, ALU.max)
            dve.drain().then_inc(ml_row, 1)
            dve.wait_ge(ml_exp, 3 * u + 1)
            dve.tensor_scalar(r_("b"), r_("b"), 1.0, None, ALU.add)
            dve.drain().then_inc(ml_row, 1)
            dve.wait_ge(ml_exp, 3 * u + 2)
            dve.scalar_tensor_tensor(r_("f"), r_("f"), 0.0, r_("b"), ALU.min, ALU.subtract)
            dve.drain()
            for d in range(2):
                for ci in range(2):
                    o = slice(ci * P, (ci + 1) * P)
                    dve.tensor_tensor_scan(rows["b"][:, d, o], ones[0:MH, :], rows["f"][:, d, o], 0.0, ALU.mult, ALU.add)
            dve.drain()
            dve.tensor_tensor(r_("i"), r_("i"), r_("b"), ALU.subtract)
            for ci in range(2):
                o = slice(ci * P, (ci + 1) * P)
                dve.drain()
                dve.tensor_copy(m_from[:, :, ci], m_now[:, :])
                dve.drain()
                for d in range(2):
                    dve.tensor_tensor_scan(rows["m"][:, d, o], ones[0:MH, :], rows["i"][:, d, o], m_now[:, d:d + 1], ALU.mult, ALU.max)
                dve.drain()
                dve.tensor_copy(m_to[:, :, ci], rows["m"][:, :, ci * P + P - 1])
                dve.drain()
                dve.tensor_tensor(m_now[:, :], rows["b"][:, :, ci * P + P - 1], m_to[:, :, ci], ALU.add)
            dve.drain()
            dve.tensor_tensor(r_("th"), r_("b"), r_("m"), ALU.add)
            dve.drain()
            dve.tensor_tensor(chunk("f"), chunk("i"), wide(m_to[:, :, :].unsqueeze(3), [MH, 2, 2, P]), ALU.subtract)
            dve.tensor_tensor(chunk("b"), wide(m_from[:, :, :].unsqueeze(3), [MH, 2, 2, P]), chunk("m"), ALU.subtract)
            dve.drain()
            dve.tensor_tensor(m_from[:, :, :], m_from[:, :, :], m_to[:, :, :], ALU.subtract)
            for d in range(2):
                step = -1 if d else 1
                dve.tensor_copy(rows["a_true"][:, d, :], rows["i"][:, d, ::step])
                dve.tensor_scalar(rows["nm_true"][:, d, :], rows["m"][:, d, ::step], -1.0, None, ALU.mult)
            dve.drain().then_inc(ml_row, 1)
            dve.wait_ge(ml_exp, 3 * u + 3)
            dve.tensor_tensor(decay_x[:, :, :], wide(m_from[:, :, :].rearrange("h d c -> h (d c)").unsqueeze(2), [MH, 4, MH]),
                              wide(eye[0:MH, 0:MH].unsqueeze(1), [MH, 4, MH]), ALU.mult)

        def ml_rows_act(act, u):
            act.wait_ge(ml_row, 3 * u + 1)
            act.activation(r_("b"), r_("b"), ACT.Exp, scale=-1.0).then_inc(ml_exp, 1)
            act.wait_ge(ml_row, 3 * u + 2)
            act.activation(r_("b"), r_("b"), ACT.Ln).then_inc(ml_exp, 1)
            act.wait_ge(ml_row, 3 * u + 3)
            for d in range(2):
                step = -1 if d else 1
                act.activation(rows["wk"][:, d, :], rows["f"][:, d, ::step], ACT.Exp)
                act.activation(rows["wp"][:, d, :], rows["b"][:, d, ::step], ACT.Exp)
            act.activation(m_from[:, :, :], m_from[:, :, :], ACT.Exp)
            for d in range(2):
                step = -1 if d else 1
                last = act.activation(rows["i"][:, d, :], rows["th"][:, d, ::step], ACT.Exp, scale=-1.0)
            act.drain().then_inc(ml_exp, 1)

        def conv_blocks(out):
            return [(K_AT + j * P, k_t, j, 8 + j) for j in range(8)] + ([(Q_AT + j * P, q_t, j, j) for j in range(8)] if out else [])

        def conv_pe(pe, c0, out):
            for i, (at_, _, _, _) in enumerate(conv_blocks(out)):
                if i >= 4:
                    pe.wait_ge(convolved, c0 + i - 3)
                for t in range(T):
                    last = pe.transpose(bank[:, i % 4, t * P:(t + 1) * P], h[:, t, at_:at_ + P], eye[:, :])
                last.then_inc(conv_turned, 1)

        def conv_dve(dve, c0, out):
            for i, (_, _, _, b) in enumerate(conv_blocks(out)):
                src, dst = bank[:, i % 4, 0:S], conv[i % 2]
                dve.wait_ge(conv_turned, c0 + i + 1)
                if i >= 2:
                    dve.wait_ge(conv_silu, c0 + i - 1)
                dve.tensor_scalar(dst[:, :], src, conv_w[:, b, 1:2], None, ALU.mult)
                dve.drain()
                dve.scalar_tensor_tensor(dst[:, 1:S], src[:, 0:S - 1], conv_w[:, b, 0:1], dst[:, 1:S], ALU.mult, ALU.add)
                dve.drain()
                dve.scalar_tensor_tensor(dst[:, 0:S - 1], src[:, 1:S], conv_w[:, b, 2:3], dst[:, 0:S - 1], ALU.mult, ALU.add).then_inc(convolved, 1)

        def conv_act(act, c0, out):
            for i, (_, target, j, _) in enumerate(conv_blocks(out)):
                act.wait_ge(convolved, c0 + i + 1)
                act.activation(target[:, j, :], conv[i % 2][:, :], ACT.Silu).then_inc(conv_silu, 1)

        def ml_cols_pe(pe, u):
            for g in range(4):
                t, half = g // 2, g % 2
                for j in range(4):
                    last = pe.transpose(bank[:, g, j * P:(j + 1) * P], k_t[:, half * 4 + j, t * P:(t + 1) * P], eye[:, :])
            for q, n in enumerate(("wk", "wp", "i")):
                for d in range(2):
                    for t in range(T):
                        o = q * 16 + d * 8 + t * 4
                        pe.matmul(bank[:, 6, o:o + 4], rows[n][:, d, t * P:(t + 1) * P], eye[0:MH, 0:MH], start=True, stop=True)
            pe.matmul(bank[:, 6, 48:64], ones[0:MH, :], decay_x[:, :, :].rearrange("h c n -> h (c n)"), start=True, stop=True).then_inc(ml_a, 1)

        def ml_cols_act(act, u):
            act.wait_ge(ml_a, 2 * u + 2)
            for g in range(4):
                t, half = g // 2, g % 2
                act.activation(h[:, t, K_AT + half * 512:K_AT + half * 512 + 512], bank[:, g, :], ACT.Copy, scale=MD ** -0.5)

        def ml_cols_dve(dve, u):
            for t in range(T):
                dve.tensor_copy(v_one[:, t, :, 0:MD], h[:, t, VM_AT:VM_AT + 1024].rearrange("p (h d) -> p h d", h=MH))
                dve.memset(v_one[:, t, :, MD:MD + 1], 1.0)
            dve.wait_ge(ml_a, 2 * u + 2)
            dve.tensor_copy(col[:, :], bank[:, 6, 0:64])

        def units(ci):
            return [(d, 1 - ci if d else ci, hh) for d in range(2) for hh in range(MH)]

        def coef(q, d, t, hh):
            return col[:, q * 16 + d * 8 + t * 4 + hh:q * 16 + d * 8 + t * 4 + hh + 1]

        def update_act(act, w0, ci):
            for j, (d, t, hh) in enumerate(units(ci)):
                if j >= 2:
                    act.wait_ge(upd_multiplied, w0 + j - 1)
                act.activation(v_weighed[j % 2][:, :], v_one[:, t, hh, :], ACT.Copy, scale=coef(0, d, t, hh)).then_inc(upd_weighed, 1)

        def update_pe(pe, w0, ci):
            for j, (d, t, hh) in enumerate(units(ci)):
                pe.wait_ge(upd_weighed, w0 + j + 1)
                if j >= 4:
                    pe.wait_ge(upd_taken, w0 + j - 3)
                for b in range(2):
                    o = K_AT + hh * MD + b * P
                    last = pe.matmul(bank[:, 2 * (j % 4) + b, 0:MD + 1], h[:, t, o:o + P], v_weighed[j % 2][:, :], start=True, stop=True)
                last.then_inc(upd_multiplied, 1)

        def update_dve(dve, w0, ci):
            for j, (d, t, hh) in enumerate(units(ci)):
                dve.wait_ge(upd_multiplied, w0 + j + 1)
                decay = col[:, 48 + (d * 2 + ci) * 4 + hh:49 + (d * 2 + ci) * 4 + hh]
                for b in range(2):
                    st = state(d, hh, b)
                    last = dve.scalar_tensor_tensor(st, st, decay, bank[:, 2 * (j % 4) + b, 0:MD + 1], ALU.mult, ALU.add)
                last.then_inc(upd_taken, 1)

        def unit_pe(pe, ci):
            us = units(ci)
            u0 = 8 * ci

            def first(j):
                d, t, hh = us[j]
                tok = slice(t * P, (t + 1) * P)
                if j >= 2:
                    pe.wait_ge(ml_weighted, u0 + j - 1)
                o = bank[:, j % 2, 0:P]
                pe.matmul(o, rows["a_true"][:, d, tok], pick[:, hh, :], start=True, stop=False)
                pe.matmul(o, pick[:, hh, :], rows["nm_true"][:, d, tok], start=False, stop=True)
                o = bank[:, 2 + j % 2, 0:P]
                for b in range(2):
                    last = pe.matmul(o, k_t[:, hh * 2 + b, tok], q_t[:, hh * 2 + b, tok], start=b == 0, stop=b == 1)
                last.then_inc(ml_scored, 1)

            def second(j):
                d, t, hh = us[j]
                tok = slice(t * P, (t + 1) * P)
                if j >= 2:
                    pe.wait_ge(ml_taken, u0 + j - 1)
                o = bank[:, 6 + j % 2, 0:MD + 1]
                for b in range(2):
                    pe.matmul(o, q_t[:, hh * 2 + b, tok], state(d, hh, b), start=b == 0, stop=b == 1)
                pe.wait_ge(ml_weighted, u0 + j + 1)
                pe.matmul(bank[:, 4 + j % 2, 0:MD + 1], p_t[j % 2][:, :], v_one[:, t, hh, :], start=True, stop=True).then_inc(ml_mixed, 1)

            first(0)
            for j in range(8):
                if j < 7:
                    first(j + 1)
                second(j)

        def unit_act(act, ci):
            us = units(ci)
            u0 = 8 * ci
            for j in range(9):
                if j < 8:
                    act.wait_ge(ml_exponent, u0 + j + 1)
                    act.activation(e_arg[j % 2][:, :], e_arg[j % 2][:, :], ACT.Exp).then_inc(ml_exped, 1)
                if j:
                    d, t, hh = us[j - 1]
                    act.wait_ge(ml_mixed, u0 + j)
                    act.activation(from_state[(j - 1) % 2][:, :], bank[:, 6 + (j - 1) % 2, 0:MD + 1], ACT.Copy, scale=coef(1, d, t, hh)).then_inc(ml_scaled, 1)

        def unit_dve(dve, ci):
            us = units(ci)
            u0 = 8 * ci

            def finish(j):
                d, t, hh = us[j]
                dve.wait_ge(ml_scaled, u0 + j + 1)
                n_ = num[j % 2]
                dve.tensor_tensor(n_[:, :], bank[:, 4 + j % 2, 0:MD + 1], from_state[j % 2][:, :], ALU.add)
                dve.drain()
                den = n_[:, MD:MD + 1]
                floor = small[:, 10 + j % 2:11 + j % 2]
                dve.tensor_scalar(floor, den, coef(2, d, t, hh), None, ALU.max)
                dve.drain()
                dve.scalar_tensor_tensor(den, den, -1.0, floor, ALU.mult, ALU.max)
                dve.drain()
                dve.reciprocal(small[:, 8 + j % 2:9 + j % 2], den)
                dve.drain()
                o = h[:, t, Q_AT + hh * MD:Q_AT + (hh + 1) * MD]
                r = small[:, 8 + j % 2:9 + j % 2]
                if ci == 0:
                    last = dve.tensor_scalar(o, n_[:, 0:MD], r, None, ALU.mult)
                else:
                    last = dve.scalar_tensor_tensor(o, n_[:, 0:MD], r, o, ALU.mult, ALU.add)
                last.then_inc(ml_taken, 1)

            for j in range(9):
                if j < 8:
                    d, t, hh = us[j]
                    dve.wait_ge(ml_scored, u0 + j + 1)
                    dve.tensor_tensor(e_arg[j % 2][:, :], bank[:, j % 2, 0:P], order_neg[:, d, :], ALU.add).then_inc(ml_exponent, 1)
                if j:
                    finish(j - 1)
                if j < 8:
                    dve.wait_ge(ml_exped, u0 + j + 1)
                    dve.scalar_tensor_tensor(p_t[j % 2][:, :], bank[:, 2 + j % 2, 0:P], MD ** -0.5, e_arg[j % 2][:, :], ALU.mult, ALU.mult).then_inc(ml_weighted, 1)

        def mixers_pe(pe):
            pe.wait_ge(aux_landed, 16 * 7)
            pe.wait_ge(mix_ready, 1)
            for t in range(T):
                for g in range(4):
                    last = pe.matmul(bank[:, t, g * P:(g + 1) * P], sgu_w[:, g, :], h[:, t, V_AT + g * P:V_AT + (g + 1) * P], start=True, stop=True)
            last.then_inc(mix_multiplied, 1)
            for g in range(4):
                for t in range(T):
                    last = pe.matmul(bank[:, 2 + g, 0:S], h[:, t, PL_AT + g * P:PL_AT + (g + 1) * P], windows[:, t, g, :], start=t == 0, stop=t == 1)
            last.then_inc(mix_multiplied, 1)
            pe.wait_ge(mix_scaled, 1)
            for t in range(T):
                for g in range(4):
                    last = pe.matmul(bank[:, 6 + t, g * P:(g + 1) * P], pooled[g][:, t * P:(t + 1) * P], pool_w[:, g, :], start=True, stop=True)
            last.then_inc(mix_multiplied, 1)

        def mixers_act(act):
            for dst, src in ((sgu_w, "sgu_w_2"), (pool_w, "pool_w_2")):
                act.dma_start(dst[:, :, :], A[src]).then_inc(aux_landed, 16)
            act.dma_start(windows[:, :, :, :], A["windows"]).then_inc(aux_landed, 16)
            act.dma_start(sgu_g[:, :], A["sgu_norm_2"].partition_broadcast(P)).then_inc(aux_landed, 16)
            act.dma_start(pool_g[:, :], A["pool_scale_2"].partition_broadcast(P)).then_inc(aux_landed, 16)
            for t in range(T):
                act.activation(h[:, t, U_AT:U_AT + 1024], h[:, t, U_AT:U_AT + 1024], ACT.Gelu_apprx_tanh)
            act.drain()
            for t in range(T):
                act.activation(square[:, t * 512:(t + 1) * 512], h[:, t, V_AT:V_AT + 512], ACT.Square, accum_out=small[:, t:t + 1])
            act.drain().then_inc(mix_gelu, 1)
            act.wait_ge(mix_square, 1)
            act.activation(small[:, 4:6], small[:, 2:4], ACT.Sqrt).then_inc(mix_gelu, 1)
            act.wait_ge(mix_multiplied, 2)
            for g in range(4):
                last = act.activation(pooled[g][:, :], bank[:, 2 + g, 0:S], ACT.Copy)
            last.then_inc(mix_scaled, 1)

        def mixers_dve(dve):
            dve.wait_ge(mix_gelu, 1)
            dve.tensor_scalar(small[:, 2:4], small[:, 0:2], 1.0 / 512, EPS, ALU.mult, ALU.add)
            dve.drain().then_inc(mix_square, 1)
            dve.wait_ge(mix_gelu, 2)
            newton(dve, small[:, 6:8], small[:, 4:6], small[:, 2:4], small[:, 62:64])
            dve.drain()
            dve.wait_ge(aux_landed, 16 * 7)
            for t in range(T):
                v = h[:, t, V_AT:V_AT + 512]
                last = dve.scalar_tensor_tensor(v, v, small[:, 6 + t:7 + t], sgu_g[:, :], ALU.mult, ALU.mult)
            dve.drain().then_inc(mix_ready, 1)
            dve.wait_ge(mix_multiplied, 1)
            for t in range(T):
                for g in range(4):
                    u = h[:, t, U_AT + g * P:U_AT + (g + 1) * P]
                    dve.scalar_tensor_tensor(u, bank[:, t, g * P:(g + 1) * P], sgu_b[:, g:g + 1], u, ALU.add, ALU.mult)
            dve.wait_ge(mix_multiplied, 3)
            for t in range(T):
                dve.tensor_tensor(h[:, t, PL_AT:PL_AT + 512], bank[:, 6 + t, :], pool_g[:, :], ALU.mult)

        def ml_out_act(act):
            act.dma_start(mlstm_g[:, :], A["mlstm_norm_2"].partition_broadcast(P)).then_inc(aux_landed, 16)
            for t in range(T):
                act.activation(h[:, t, O_AT:O_AT + 1024], h[:, t, O_AT:O_AT + 1024], ACT.Sigmoid)
            act.drain().then_inc(out_root, 1)
            act.wait_ge(out_square, 1)
            act.activation(small[:, 24:32], small[:, 16:24], ACT.Sqrt).then_inc(out_root, 1)

        def ml_out_dve(dve):
            heads = lambda ap: ap.rearrange("p (h d) -> p h d", h=MH)
            for t in range(T):
                y = h[:, t, Q_AT:Q_AT + 1024]
                dve.tensor_tensor(square[:, :], y, y, ALU.mult)
                dve.drain()
                dve.tensor_reduce(small[:, 8 + 4 * t:12 + 4 * t], heads(square[:, :]), AX.X, ALU.add)
                dve.drain()
            dve.tensor_scalar(small[:, 16:24], small[:, 8:16], 1.0 / MD, EPS, ALU.mult, ALU.add)
            dve.drain().then_inc(out_square, 1)
            dve.wait_ge(out_root, 2)
            newton(dve, small[:, 32:40], small[:, 24:32], small[:, 16:24], small[:, 48:56])
            dve.drain()
            dve.wait_ge(aux_landed, 16 * 8)
            for t in range(T):
                y = h[:, t, Q_AT:Q_AT + 1024]
                dve.tensor_tensor(heads(y), heads(y), wide(small[:, 32 + 4 * t:36 + 4 * t].unsqueeze(2), [P, MH, MD]), ALU.mult)
                dve.drain()
                dve.tensor_tensor(y, y, mlstm_g[:, :], ALU.mult)
                dve.drain()
                dve.tensor_tensor(y, y, h[:, t, O_AT:O_AT + 1024], ALU.mult)

        def mixed_column(kk):
            return U_AT + kk * P if kk < 4 else Q_AT + (kk - 4) * P if kk < 12 else PL_AT + (kk - 12) * P

        def take_gated(dve, n, s):
            for t in range(T):
                o = x[:, t, bass.ds(n * N, N)]
                b = bank[:, 2 * s + t, :]
                dve.drain()
                dve.tensor_tensor(gated[:, t, :], b, m_row[0][:, bass.ds(n * N, N)], ALU.mult)
                dve.drain()
                last = dve.tensor_tensor(o, gated[:, t, :], o, ALU.add)
            last.then_inc(evacuated, 1)

        def hf_dve(dve):
            dve.tensor_tensor(full[:, :, :], xt_hi[:, :, :].bitcast(F32), xt_lo[:, :, :].bitcast(F32), ALU.add)
            dve.drain().then_inc(full_ready, 1)
            for g in range(NG):
                t, c = g // Q, slice((g % Q) * 512, (g % Q) * 512 + 512)
                dve.wait_ge(part_copied, 2 * g + 1)
                dve.tensor_tensor(rest[:, g % 2, :], bank[:, g % 4, :], parts[:, t, 0, c], ALU.subtract).then_inc(part_rest, 1)
                dve.wait_ge(part_copied, 2 * g + 2)
                dve.tensor_tensor(parts[:, t, 2, c], rest[:, g % 2, :], parts[:, t, 1, c], ALU.subtract).then_inc(part_low, 1)

        def hf_act(act):
            for g in range(NG):
                t, c = g // Q, slice((g % Q) * 512, (g % Q) * 512 + 512)
                act.wait_ge(back_turned, g + 1)
                act.activation(parts[:, t, 0, c], bank[:, g % 4, :], ACT.Copy).then_inc(part_copied, 1)
                act.wait_ge(part_rest, g + 1)
                act.activation(parts[:, t, 1, c], rest[:, g % 2, :], ACT.Copy).then_inc(part_copied, 1)
            act.wait_ge(part_low, NG)
            for i in range(3):
                act.dma_start(hf_rows[i].rearrange("(t p) d -> p t d", p=P), parts[:, :, i, :]).then_inc(hf_stored, 16)

        def hf_pe(pe):
            pe.wait_ge(full_ready, 1)
            for g in range(NG):
                t = g // Q
                if g >= 4:
                    pe.wait_ge(part_low, g - 3)
                for j in range(4):
                    last = pe.transpose(bank[:, g % 4, j * P:(j + 1) * P], full[:, (g % Q) * 4 + j, t * P:(t + 1) * P], eye[:, :])
                last.then_inc(back_turned, 1)

        def keys_pe(pe):
            for g in range(NG):
                t = g // Q
                if g >= 4:
                    pe.wait_ge(pq_copied, g - 3)
                for j in range(4):
                    kk = (g % Q) * 4 + j
                    last = pe.transpose(bank[:, g % 4, j * P:(j + 1) * P], h[:, t, kk * P:(kk + 1) * P], eye[:, :])
                last.then_inc(pq_turned, 1)
            pe.wait_ge(pq_copied, NG)
            for g in range(NG):
                t = g // Q
                if g >= 4:
                    pe.wait_ge(keys_copied, g - 3)
                for j in range(4):
                    kk = (g % Q) * 4 + j
                    last = pe.matmul(bank[:, 4 + g % 4, j * P:(j + 1) * P], pq_t[:, kk, t * P:(t + 1) * P], keys[:, kk % 2, :], start=True, stop=True)
                last.then_inc(keys_scored, 1)

        def keys_act(act):
            for g in range(NG):
                act.wait_ge(pq_turned, g + 1)
                act.activation(group(pq_t, g), turned(g), ACT.Copy).then_inc(pq_copied, 1)
            for g in range(NG):
                t = g // Q
                act.wait_ge(keys_scored, g + 1)
                act.activation(key_s[:, t, (g % Q) * 4:(g % Q) * 4 + 4, :], bank[:, 4 + g % 4, :].rearrange("p (k n) -> p k n", k=4), ACT.Copy).then_inc(keys_copied, 1)

        def top16(dve, values, scratch, best, where):
            dve.drain()
            dve.max(best[:, 0:8], values)
            dve.drain()
            dve.max_index(where[:, 0:8], best[:, 0:8], values)
            dve.match_replace(scratch, best[:, 0:8], values, -3e38)
            dve.drain()
            dve.max(best[:, 8:16], scratch)
            dve.drain()
            dve.max_index(where[:, 8:16], best[:, 8:16], scratch)

        def choose_dve(dve):
            dve.wait_ge(keys_copied, NG)
            for t in range(T):
                for j in range(16):
                    top16(dve, key_s[:, t, j, :], less[:, j % 2, 0:NK], top_v[:, t, j, :], top_i[:, t, j, :])
            dve.drain()
            dve.tensor_copy(top_f[:, :, :, :].rearrange("p t j k -> p (t j k)"), top_i[:, :, :, :].rearrange("p t j k -> p (t j k)"))
            for t in range(T):
                for j in range(PH):
                    c = cand[:, j % 2, :]
                    dve.drain()
                    dve.tensor_tensor(c.rearrange("p (a b) -> p a b", a=16), wide(top_v[:, t, 2 * j, :].unsqueeze(2), [P, 16, 16]),
                                      wide(top_v[:, t, 2 * j + 1, :].unsqueeze(1), [P, 16, 16]), ALU.add)
                    top16(dve, c, less[:, j % 2, :], best_v[:, t, j, :], best_i[:, t, j, :])
                dve.drain()
                pairs = best_i[:, t, :, :].rearrange("p h k -> p (h k)")
                dve.tensor_scalar(best_s[:, 0, :], pairs, 4, None, ALU.logical_shift_right)
                dve.tensor_scalar(best_s[:, 1, :], pairs, 15, None, ALU.bitwise_and)
                dve.drain()
                dve.tensor_copy(best_f[:, :, :].rearrange("p a n -> p (a n)"), best_s[:, :, :].rearrange("p a n -> p (a n)"))
                dve.drain()
                for i in range(2):
                    dve.drain()
                    dve.tensor_tensor(match[:, :, :], wide(best_f[:, i, :].unsqueeze(2), [P, PH * PK, 16]),
                                      wide(count16[:, :].unsqueeze(1), [P, PH * PK, 16]), ALU.is_equal)
                    dve.drain()
                    for j in range(PH):
                        m = match[:, j * PK:(j + 1) * PK, :]
                        dve.tensor_tensor(m, m, wide(top_f[:, t, 2 * j + i, :].unsqueeze(1), [P, PK, 16]), ALU.mult)
                    dve.drain()
                    dve.tensor_reduce(side[:, i, :], match[:, :, :], AX.X, ALU.add)
                dve.drain()
                dve.scalar_tensor_tensor(expert_f[:, t, :], side[:, 0, :], float(NK), side[:, 1, :], ALU.mult, ALU.add)
                g3 = gate_f[:, t, :].rearrange("p (h k) -> p h k", h=PH)
                dve.tensor_tensor(g3, best_v[:, t, :, :], wide(best_v[:, t, :, 0:1], [P, PH, PK]), ALU.subtract)
                dve.drain().then_inc(gate_shifted, 1)
                dve.wait_ge(gate_exped, t + 1)
                dve.tensor_reduce(gate_s[:, 8 * t:8 * t + 8], g3, AX.X, ALU.add)
                dve.drain()
                dve.reciprocal(gate_s[:, 16 + 8 * t:24 + 8 * t], gate_s[:, 8 * t:8 * t + 8])
                dve.drain()
                dve.tensor_tensor(g3, g3, wide(gate_s[:, 16 + 8 * t:24 + 8 * t].unsqueeze(2), [P, PH, PK]), ALU.mult)
                dve.drain().then_inc(chosen, 1)
            dve.wait_ge(chosen_turned, 1)
            dve.tensor_copy(idx[:, :], bank[:, 0, 0:S])
            dve.tensor_copy(gate_t[:, :], bank[:, 1, 0:S])
            dve.memset(three[:, :], 1.0)
            dve.memset(zero_w[:, :], 0.0)

        def choose_act(act):
            for t in range(T):
                act.wait_ge(gate_shifted, t + 1)
                act.activation(gate_f[:, t, :], gate_f[:, t, :], ACT.Exp).then_inc(gate_exped, 1)

        def choose_pe(pe):
            pe.wait_ge(chosen, T)
            for t in range(T):
                pe.transpose(bank[:, 0, t * P:(t + 1) * P], expert_f[:, t, :], eye[:, :])
                last = pe.transpose(bank[:, 1, t * P:(t + 1) * P], gate_f[:, t, :], eye[:, :])
            last.then_inc(chosen_turned, 1)

        TOK = 16
        PASSES = P // TOK

        def experts_pool(pool):
            def four(n0, b):
                pool.tensor_copy(idx4[b][:, :], idx[:, bass.ds(n0, 4)])
                pool.drain()
                for j in range(4):
                    n = n0 + j
                    at_ = lambda: bass.IndirectOffsetOnAxis(ap=idx4[b][:, j:j + 1], axis=0)
                    pool.wait_ge(halves_read, 2 * PRE + 2 * n - 6)
                    pool.sem_inc(passed_pool, 1)
                    pool.indirect_dma_start(u_ring[:, j, :], None, A["peer_u_2"][0], at_()).then_inc(u_landed[j], 16)
                    pool.wait_ge(summed, PRE + n - 3)
                    pool.sem_inc(passed_pool, 1)
                    pool.indirect_dma_start(v_ring[:, j, :], None, A["peer_v_2"][0], at_()).then_inc(v_landed[j], 16)

            with pool.Fori(0, S // 8) as i:
                four(8 * i, 0)
                four(8 * i + 4, 1)

        def experts_sp(sp):
            sp.wait_ge(hf_stored, 48)
            sp.wait_ge(rings_free, 1)
            for r in range(2):
                sp.dma_start(row_ring[r][:, :, :], hf_rows[:, r * 8:(r + 1) * 8, :]).then_inc(rows_landed[r], 16)
            with sp.Fori(0, S // TOK - 1) as i:
                for r in range(2):
                    sp.wait_ge(half_spread, PRE + 2 * (TOK * i + 8 * (r + 1)))
                    sp.dma_start(row_ring[r][:, :, :], hf_rows[:, bass.ds(TOK * i + TOK + 8 * r, 8), :]).then_inc(rows_landed[r], 16)

        def experts_pe(pe):
            def row(n, j, m):
                r = j // 8
                if j % 8 == 0:
                    pe.wait_ge(rows_landed[r], 16 * (m + 1))
                for hf in range(2):
                    pe.wait_ge(halves_read, 2 * PRE + 2 * n + hf - 1)
                    for b in range(2):
                        c = (2 * hf + b) * 512
                        last = pe.matmul(bank[:, 2 * hf + b, :], three[0:3, :], row_ring[r][0:3, j % 8, c:c + 512], start=True, stop=True)
                    last.then_inc(half_spread, 1)

            def add(n, j, m):
                pe.wait_ge(v_landed[j % 4], 16 * (4 * m + j // 4 + 1))
                pe.wait_ge(spread_weight, PRE + n + 1)
                for b in range(4):
                    last = pe.matmul(bank[:, 4 + b, :], z_ring[j % 4][:, :], v_ring[:, j % 4, b * 512:(b + 1) * 512],
                                     start=False, stop=False, skip_group_check=True)
                last.then_inc(summed, 1)

            def tokens(m, end=TOK):
                for j in range(TOK):
                    if j + 2 < end:
                        row(m * TOK + j + 2, (j + 2) % TOK, m + (j + 2) // TOK)
                    add(m * TOK + j, j, m)

            for t in range(T):
                row(t * P, 0, t * PASSES)
                row(t * P + 1, 1, t * PASSES)
                if t:
                    pe.wait_ge(tile_taken, t)
                for b in range(4):
                    pe.matmul(bank[:, 4 + b, :], zero_w[:, 0:P], zero_w[:, :], start=True, stop=False, skip_group_check=True)
                with pe.Fori(0, PASSES - 1) as i:
                    tokens(i + t * PASSES, TOK + 2)
                tokens((t + 1) * PASSES - 1)
                for b in range(4):
                    last = pe.matmul(bank[:, 4 + b, :], zero_w[:, 0:P], zero_w[:, :], start=False, stop=True, skip_group_check=True)
                last.then_inc(tile_summed, 1)

        def experts_act(act):
            with act.Fori(0, S // 8) as i:
                for j in range(8):
                    act.wait_ge(halves_read, 2 * PRE + 2 * (8 * i + j) + 2)
                    act.activation(act_out[:, j:j + 1], act_in[:, j:j + 1], ACT.Gelu_apprx_tanh).then_inc(gelued, 1)

        def experts_dve(dve):
            def dot(n, j, m):
                dve.wait_ge(u_landed[j % 4], 16 * (4 * m + j // 4 + 1))
                dve.sem_inc(passed, 1)
                for hf in range(2):
                    u = u_ring[:, j % 4, hf * 1024:(hf + 1) * 1024]
                    dve.wait_ge(half_spread, PRE + 2 * n + hf + 1)
                    dve.sem_inc(passed, 1)
                    a = act_half[:, j % 8:j % 8 + 1]
                    dve.tensor_tensor_reduce(u, u, bank[:, 2 * hf:2 * hf + 2, :].rearrange("p b n -> p (b n)"), 1.0, a if hf else 0.0,
                                             ALU.mult, ALU.add, act_in[:, j % 8:j % 8 + 1] if hf else a).then_inc(halves_read, 1)
                    if not hf:
                        dve.drain()

            def weight(n, j, i):
                dve.wait_ge(gelued, PRE + n + 1)
                dve.sem_inc(passed, 1)
                dve.wait_ge(summed, PRE + n - 3)
                dve.sem_inc(passed, 1)
                dve.tensor_scalar(z_ring[j % 4][:, :], band[:, bass.ds(P - 1 - (TOK * i + j), P)], act_out[:, j % 8:j % 8 + 1],
                                  gate_t[:, bass.ds(n, 1)], ALU.mult, ALU.mult).then_inc(spread_weight, 1)

            for t in range(T):
                with dve.Fori(0, PASSES) as i:
                    m = i + t * PASSES
                    for j in range(TOK):
                        dot(m * TOK + j, j, m)
                        weight(m * TOK + j, j, i)
                dve.wait_ge(tile_summed, t + 1)
                sums = bank[:, 4:8, :].rearrange("p b n -> p (b n)")
                dve.tensor_tensor(xe[:, :], sums, m_row[1][:, :], ALU.mult)
                dve.drain().then_inc(tile_taken, 1)
                dve.tensor_tensor(x[:, t, :], x[:, t, :], xe[:, :], ALU.add)
                dve.drain()

        def pe_program(pe):
            pe.sem_inc(chunk_multiplied, PRE)
            for s_ in (blocks_turned, qk_turned, scored, p_turned, mixed, half_spread, summed):
                pe.sem_inc(s_, PRE)
            pe.wait_ge(const_landed, 16 * 16)
            turn_pe(pe, 0, xn, PRE + 3)
            end_of_stage(pe, "pe")
            gemm_pe(pe, plan["ab_in"])
            end_of_stage(pe, "pe")
            pe.wait_ge(aux_ready, 1)
            pe.matmul(bank[:, 7, 0:2], ones[:, :], lam[:, 0:2], start=True, stop=True).then_inc(aux_summed, 1)
            end_of_stage(pe, "pe")
            attention_pe(pe, ATT["a"])
            end_of_stage(pe, "pe")
            attention_pe(pe, ATT["b"])
            end_of_stage(pe, "pe")
            end_of_stage(pe, "pe")
            turn_pe(pe, 1, gate(h), 0)
            end_of_stage(pe, "pe")
            gemm_pe(pe, plan["ab_out"])
            end_of_stage(pe, "pe")
            turn_pe(pe, 2, xn, PRE + 6)
            end_of_stage(pe, "pe")
            gemm_pe(pe, plan["c_in"])
            end_of_stage(pe, "pe")
            end_of_stage(pe, "pe")
            attention_pe(pe, ATT["c"])
            end_of_stage(pe, "pe")
            turn_pe(pe, 3, gate(h), 0)
            end_of_stage(pe, "pe")
            gemm_pe(pe, plan["c_out"])
            end_of_stage(pe, "pe")
            end_of_stage(pe, "pe")
            ada_pe(pe)
            end_of_stage(pe, "pe")
            end_of_stage(pe, "pe")
            turn_pe(pe, 4, xn, PRE + 12)
            end_of_stage(pe, "pe")
            gemm_pe(pe, plan["ctx"])
            gates_pe(pe, 0)
            end_of_stage(pe, "pe")
            ml_rows_pe(pe)
            conv_pe(pe, 0, False)
            end_of_stage(pe, "pe")
            ml_cols_pe(pe, 0)
            end_of_stage(pe, "pe")
            for ci in range(2):
                update_pe(pe, 8 * ci, ci)
                end_of_stage(pe, "pe")
            turn_pe(pe, 5, xn, PRE + 15)
            end_of_stage(pe, "pe")
            gemm_pe(pe, plan["lat"])
            gates_pe(pe, 1)
            end_of_stage(pe, "pe")
            ml_rows_pe(pe)
            conv_pe(pe, 8, True)
            end_of_stage(pe, "pe")
            mixers_pe(pe)
            end_of_stage(pe, "pe")
            ml_cols_pe(pe, 1)
            end_of_stage(pe, "pe")
            unit_pe(pe, 0)
            end_of_stage(pe, "pe")
            update_pe(pe, 16, 0)
            end_of_stage(pe, "pe")
            unit_pe(pe, 1)
            end_of_stage(pe, "pe")
            end_of_stage(pe, "pe")
            turn_pe(pe, 6, h, 0, mixed_column)
            end_of_stage(pe, "pe")
            gemm_pe(pe, plan["mix_out"])
            end_of_stage(pe, "pe")
            turn_pe(pe, 7, xn, PRE + 18)
            end_of_stage(pe, "pe")
            hf_pe(pe)
            end_of_stage(pe, "pe")
            gemm_pe(pe, plan["wq"])
            end_of_stage(pe, "pe")
            end_of_stage(pe, "pe")
            keys_pe(pe)
            end_of_stage(pe, "pe")
            choose_pe(pe)
            end_of_stage(pe, "pe")
            experts_pe(pe)
            end_of_stage(pe, "pe")
            end_of_stage(pe, "pe")

        def act_program(act):
            for s_ in (hi_ready, act_step, hi_written, qk_copied, exped, p_copied, gelued):
                act.sem_inc(s_, PRE)
            act.wait_ge(x_landed, 16)
            rstd_act(act, x, 0)
            turn_act(act, 0, ((g_ab, None), 0))
            end_of_stage(act, "act")
            gemm_act(act, plan["ab_in"])
            end_of_stage(act, "act")
            act.activation(gate(h), gate(h), ACT.Silu)
            act.wait_ge(aux_summed, 1)
            act.activation(lam[:, 0:2], bank[:, 7, 0:2], ACT.Exp).then_inc(aux_summed, 1)
            end_of_stage(act, "act")
            attention_act(act, ATT["a"])
            end_of_stage(act, "act")
            attention_act(act, ATT["b"])
            end_of_stage(act, "act")
            act.wait_ge(aux_ready, 3)
            act.activation(small[:, 24:32], small[:, 16:24], ACT.Sqrt).then_inc(aux_summed, 1)
            end_of_stage(act, "act")
            turn_act(act, 1, None)
            end_of_stage(act, "act")
            gemm_act(act, plan["ab_out"])
            end_of_stage(act, "act")
            rstd_act(act, x, 1)
            turn_act(act, 2, ((g_c, None), NG))
            end_of_stage(act, "act")
            gemm_act(act, plan["c_in"])
            end_of_stage(act, "act")
            act.activation(gate(h), gate(h), ACT.Silu)
            end_of_stage(act, "act")
            attention_act(act, ATT["c"])
            end_of_stage(act, "act")
            turn_act(act, 3, None)
            end_of_stage(act, "act")
            gemm_act(act, plan["c_out"])
            end_of_stage(act, "act")
            act.dma_start(row_w[:, :], A["final_norm"].partition_broadcast(P)).then_inc(aux_landed, 16)
            rstd_act(act, x, 2)
            end_of_stage(act, "act")
            act.dma_start(ada_bias_row[:, :, :], A["ada_b_rows"]).then_inc(aux_landed, 16)
            act.wait_ge(aux_landed, 32)
            ada_act(act)
            end_of_stage(act, "act")
            for dst, src in ((flip, "flip"), (order_neg, "order_neg"), (conv_w, "qk_conv_2"), (sgu_b, "sgu_b_2")):
                act.dma_start(dst[:, :] if len(dst.shape) == 2 else dst[:, :, :], A[src]).then_inc(ctx_landed, 16)
            act.dma_start(h[:, :, 0:D], A["ctx_2"][0].rearrange("(t p) d -> p t d", p=P)).then_inc(ctx_landed, 16)
            act.activation(wg_hi[:, :, :], wg[:, :, :], ACT.Copy).then_inc(wg_ready, 1)
            act.wait_ge(ctx_landed, 80)
            end_of_stage(act, "act")
            rstd_act(act, h[:, :, 0:D], 3)
            turn_act(act, 4, (True, 2 * NG))
            end_of_stage(act, "act")
            gemm_act(act, plan["ctx"])
            end_of_stage(act, "act")
            ml_rows_act(act, 0)
            conv_act(act, 0, False)
            end_of_stage(act, "act")
            ml_cols_act(act, 0)
            end_of_stage(act, "act")
            for ci in range(2):
                update_act(act, 8 * ci, ci)
                end_of_stage(act, "act")
            rstd_act(act, x, 4)
            turn_act(act, 5, (True, 3 * NG))
            end_of_stage(act, "act")
            gemm_act(act, plan["lat"])
            end_of_stage(act, "act")
            ml_rows_act(act, 1)
            conv_act(act, 8, True)
            end_of_stage(act, "act")
            mixers_act(act)
            end_of_stage(act, "act")
            ml_cols_act(act, 1)
            end_of_stage(act, "act")
            unit_act(act, 0)
            end_of_stage(act, "act")
            update_act(act, 16, 0)
            end_of_stage(act, "act")
            unit_act(act, 1)
            end_of_stage(act, "act")
            ml_out_act(act)
            end_of_stage(act, "act")
            turn_act(act, 6, None)
            end_of_stage(act, "act")
            gemm_act(act, plan["mix_out"])
            end_of_stage(act, "act")
            rstd_act(act, x, 5)
            turn_act(act, 7, (True, 4 * NG))
            end_of_stage(act, "act")
            hf_act(act)
            end_of_stage(act, "act")
            gemm_act(act, plan["wq"])
            end_of_stage(act, "act")
            for dst, src in ((keys, "peer_keys_2"), (count16, "count16"), (band, "band")):
                act.dma_start(dst[:, :] if len(dst.shape) == 2 else dst[:, :, :], A[src]).then_inc(keys_landed, 16)
            act.wait_ge(keys_landed, 48)
            end_of_stage(act, "act")
            keys_act(act)
            end_of_stage(act, "act")
            choose_act(act)
            end_of_stage(act, "act")
            act.dma_start(last_w[:, :], A["norm_final_2"].partition_broadcast(P)).then_inc(aux_landed, 16)
            experts_act(act)
            end_of_stage(act, "act")
            rstd_act(act, x, 6)
            end_of_stage(act, "act")

        def normalise_dve(dve, u, src):
            rstd_dve(dve, u)
            for t in range(T):
                last = dve.tensor_scalar(xn[:, t, :], src[:, t, :], small[:, 6 + t:7 + t], None, ALU.mult)
            last.then_inc(norm_step, 1)
            dve.drain()

        def dve_program(dve):
            dve.sem_inc(raw_used, PRE)
            dve.sem_inc(halves_read, 2 * PRE)
            for s_ in (evacuated, norm_step, block_scaled, lo_written, roped, shifted, weighed, mix_taken, spread_weight):
                dve.sem_inc(s_, PRE)
            dve.memset(ones[:, :], 1.0)
            dve.wait_ge(const_landed, 16 * 16)
            dve.tensor_tensor(lam[:, 0:1], lam_in[:, 0:1], lam_in[:, 1:2], ALU.mult)
            dve.tensor_tensor(lam[:, 1:2], lam_in[:, 2:3], lam_in[:, 3:4], ALU.mult)
            dve.drain().then_inc(aux_ready, 1)
            normalise_dve(dve, 0, x)
            turn_dve(dve, 0, ((g_ab, None), 0))
            end_of_stage(dve, "dve")
            gemm_dve(dve, plan["ab_in"], take_h)
            end_of_stage(dve, "dve")
            dve.wait_ge(aux_summed, 2)
            dve.tensor_tensor(lam[:, 3:4], lam[:, 1:2], lam[:, 0:1], ALU.subtract)
            dve.drain()
            dve.tensor_scalar(lam[:, 2:3], lam[:, 3:4], -LAM_INIT, None, ALU.add).then_inc(aux_ready, 1)
            end_of_stage(dve, "dve")
            attention_dve(dve, ATT["a"])
            end_of_stage(dve, "dve")
            attention_dve(dve, ATT["b"])
            end_of_stage(dve, "dve")
            hb = ATT["b"]
            heads = lambda ap: ap.rearrange("p (h d) -> p h d", h=4)
            for t in range(T):
                y = h[:, t, hb["q"]:hb["q"] + 1024]
                dve.tensor_tensor(sub_sq[:, :], y, y, ALU.mult)
                dve.drain()
                dve.tensor_reduce(small[:, 8 + 4 * t:12 + 4 * t], heads(sub_sq[:, :]), AX.X, ALU.add)
                dve.drain()
            dve.tensor_scalar(small[:, 16:24], small[:, 8:16], 1.0 / 256, EPS, ALU.mult, ALU.add).then_inc(aux_ready, 1)
            dve.wait_ge(aux_summed, 3)
            newton(dve, small[:, 32:40], small[:, 24:32], small[:, 16:24], small[:, 48:56])
            dve.drain()
            dve.tensor_scalar(small[:, 40:48], small[:, 32:40], 1.0 - LAM_INIT, None, ALU.mult)
            dve.drain()
            for t in range(T):
                y = h[:, t, hb["q"]:hb["q"] + 1024]
                z = h[:, t, hb["z"]:hb["z"] + 1024]
                dve.tensor_tensor(heads(y), heads(y), wide(small[:, 40 + 4 * t:44 + 4 * t].unsqueeze(2), [P, 4, 256]), ALU.mult)
                dve.drain()
                dve.tensor_tensor(heads(y), heads(y), wide(subln[:, :].unsqueeze(1), [P, 4, 256]), ALU.mult)
                dve.drain()
                dve.tensor_tensor(z, z, y, ALU.mult)
            end_of_stage(dve, "dve")
            turn_dve(dve, 1, None)
            end_of_stage(dve, "dve")
            gemm_dve(dve, plan["ab_out"], take_residual)
            end_of_stage(dve, "dve")
            normalise_dve(dve, 1, x)
            turn_dve(dve, 2, ((g_c, None), NG))
            end_of_stage(dve, "dve")
            gemm_dve(dve, plan["c_in"], take_h)
            end_of_stage(dve, "dve")
            end_of_stage(dve, "dve")
            attention_dve(dve, ATT["c"])
            end_of_stage(dve, "dve")
            turn_dve(dve, 3, None)
            end_of_stage(dve, "dve")
            gemm_dve(dve, plan["c_out"], take_residual)
            end_of_stage(dve, "dve")
            rstd_dve(dve, 2)
            dve.wait_ge(aux_landed, 16)
            for t in range(T):
                dve.scalar_tensor_tensor(x[:, t, :], x[:, t, :], small[:, 6 + t:7 + t], row_w[:, :], ALU.mult, ALU.mult)
            dve.drain().then_inc(norm_step, 1)
            end_of_stage(dve, "dve")
            ada_dve(dve)
            end_of_stage(dve, "dve")
            dve.memset(h[:, :, 5632:5632 + 8 * (MD + 1)], 0.0)
            dve.memset(m_now[:, :], 0.0)
            dve.tensor_copy(pick[:, :, :], wide(eye[0:MH, 0:MH].unsqueeze(2), [MH, MH, P]))
            dve.wait_ge(wg_ready, 1)
            dve.tensor_tensor(wg_lo[:, :, :], wg[:, :, :], wg_hi[:, :, :].bitcast(F32), ALU.subtract)
            end_of_stage(dve, "dve")
            normalise_dve(dve, 3, h[:, :, 0:D])
            turn_dve(dve, 4, ((mod[:, 0, :], m_col[:, 6, :]), 2 * NG))
            end_of_stage(dve, "dve")
            gemm_dve(dve, plan["ctx"], lambda e, n, s: take_h(e, n, s, K_AT))
            gates_dve(dve, 0)
            end_of_stage(dve, "dve")
            ml_rows_dve(dve, 0)
            conv_dve(dve, 0, False)
            end_of_stage(dve, "dve")
            ml_cols_dve(dve, 0)
            end_of_stage(dve, "dve")
            for ci in range(2):
                update_dve(dve, 8 * ci, ci)
                end_of_stage(dve, "dve")
            normalise_dve(dve, 4, x)
            turn_dve(dve, 5, ((mod[:, 1, :], m_col[:, 0, :]), 3 * NG))
            end_of_stage(dve, "dve")
            gemm_dve(dve, plan["lat"], take_h)
            gates_dve(dve, 1)
            end_of_stage(dve, "dve")
            ml_rows_dve(dve, 1)
            conv_dve(dve, 8, True)
            end_of_stage(dve, "dve")
            mixers_dve(dve)
            end_of_stage(dve, "dve")
            ml_cols_dve(dve, 1)
            end_of_stage(dve, "dve")
            unit_dve(dve, 0)
            end_of_stage(dve, "dve")
            update_dve(dve, 16, 0)
            end_of_stage(dve, "dve")
            unit_dve(dve, 1)
            end_of_stage(dve, "dve")
            ml_out_dve(dve)
            end_of_stage(dve, "dve")
            turn_dve(dve, 6, None)
            end_of_stage(dve, "dve")
            gemm_dve(dve, plan["mix_out"], take_gated)
            end_of_stage(dve, "dve")
            normalise_dve(dve, 5, x)
            turn_dve(dve, 7, ((mod[:, 2, :], m_col[:, 3, :]), 4 * NG))
            end_of_stage(dve, "dve")
            hf_dve(dve)
            end_of_stage(dve, "dve")
            gemm_dve(dve, plan["wq"], take_h)
            end_of_stage(dve, "dve")
            end_of_stage(dve, "dve")
            end_of_stage(dve, "dve")
            choose_dve(dve)
            end_of_stage(dve, "dve")
            dve.sem_inc(rings_free, 1)
            experts_dve(dve)
            end_of_stage(dve, "dve")
            rstd_dve(dve, 6)
            dve.wait_ge(aux_landed, 16 * 8 + 16)
            for t in range(T):
                dve.scalar_tensor_tensor(x[:, t, :], x[:, t, :], small[:, 6 + t:7 + t], last_w[:, :], ALU.mult, ALU.mult)
            end_of_stage(dve, "dve")

        aux_ready, aux_summed, ctx_landed, keys_landed = (sem(n) for n in ("aux_ready", "aux_summed", "ctx_landed", "keys_landed"))
        TOTAL = [0]

        @block.vector
        def _(dve):
            dve_program(dve)
            TOTAL[0] = stages["dve"]

        @block.tensor
        def _(pe):
            pe_program(pe)

        @block.scalar
        def _(act):
            act_program(act)

        @block.gpsimd
        def _(pool):
            for n in range(TOTAL[0]):
                if n == TOTAL[0] - 2:
                    experts_pool(pool)
                end_of_stage(pool, "pool")

        @block.sync
        def _(sp):
            sp.dma_start(x[:, :, :], A["x"][0].rearrange("(t p) d -> p t d", p=P)).then_inc(x_landed, 16)
            for dst, src in ((eye, "eye"), (rope_cos, "rope_cos"), (rope_sin, "rope_sin"), (dil_neg, "dilated_neg"),
                             (dil_count, "dilated_count"), (cau_neg, "causal_neg"), (g_ab, "norm_ab"), (g_c, "norm_c"),
                             (lam_in, "lam_ab"), (c_col, "c_cols"), (ada_bias, "ada_b_cols"), (g_mix, "norm_mix_2"),
                             (g_ffn, "norm_ffn_2"), (wg, "w_gates")):
                ap = dst[:, :, :] if len(dst.shape) == 3 else dst[:, :]
                sp.dma_start(ap, A[src]).then_inc(const_landed, 16)
            sp.dma_start(gate_b[:, :], A["b_gate_2"].partition_broadcast(P)).then_inc(const_landed, 16)
            sp.dma_start(subln[:, :], A["subln_ab"].rearrange("a n -> (a n)").partition_broadcast(P)).then_inc(const_landed, 16)
            for name in ("ab_in", "ab_out", "c_in", "c_out", None, "ctx", "lat", "mix_out", "wq"):
                stream_sp(sp, plan[name]) if name else ada_sp(sp)
            experts_sp(sp)
            sp.wait_ge(stage_done, 4 * TOTAL[0])
            sp.dma_start(out[0].rearrange("(t p) d -> p t d", p=P), x[:, :, :]).then_inc(out_stored, 16)
            sp.wait_ge(out_stored, 16)


def _columns(a):
    return np.ascontiguousarray(np.reshape(a, (-1, P)).T)


def host_layout(i):
    keep = ("x", "w_in_ab", "w_out_ab", "w_in_c", "w_out_c", "subln_ab", "final_norm", "ctx_2", "ada_w_2", "w_in_2", "w_out_2",
            "peer_wq_2", "peer_u_2", "peer_v_2", "norm_final_2")
    a = {k: i[k] for k in keep}
    a.update({k: _columns(i[k]) for k in ("norm_ab", "norm_c", "norm_mix_2", "norm_ffn_2")})
    a["lam_ab"] = i["lam_ab"][0].T
    a["c_cols"] = np.stack([_columns(i["c_2"]), _columns(i["c_ctx_2"])], 1)
    a["ada_b_cols"] = _columns(i["ada_b_2"]).reshape(P, 6, K)
    a["ada_b_rows"] = i["ada_b_2"].reshape(1, 6, D)[:, 2::3, :]
    a["w_gates"] = i["w_in_2"][0, :, G_AT:].reshape(K, P, 16).transpose(1, 0, 2)
    a["b_gate_2"] = i["b_gate_2"][0]
    a["sgu_norm_2"], a["pool_scale_2"], a["mlstm_norm_2"] = (i[k][0] for k in ("sgu_norm_2", "pool_scale_2", "mlstm_norm_2"))
    a["sgu_w_2"] = i["sgu_w_2"][0].transpose(2, 0, 1)
    a["sgu_b_2"] = i["sgu_b_2"][0].T
    a["pool_w_2"] = i["pool_w_2"][0].transpose(1, 0, 2)
    a["qk_conv_2"] = i["qk_conv_2"][0].reshape(3, 16, P).transpose(2, 1, 0)
    a["peer_keys_2"] = i["peer_keys_2"][0].transpose(2, 0, 1)
    a.update(shape_constants())
    return {k: np.ascontiguousarray(v) for k, v in a.items()}


def kernel(**inputs):
    import concourse.bacc as bacc
    from concourse.bass_utils import run_bass_kernel_spmd

    nc = bacc.Bacc("TRN2", target_bir_lowering=False, num_devices=1)
    arrays = host_layout({k: np.asarray(v) for k, v in inputs.items()})
    A = {k: nc.dram_tensor(f"in_{k}", v.shape, mybir.dt.from_np(v.dtype), kind="ExternalInput").ap() for k, v in arrays.items()}
    out = nc.dram_tensor("out", (1, S, D), F32, kind="ExternalOutput").ap()
    bass_hybrid_stack_kernel(nc, A, out)
    result = run_bass_kernel_spmd(nc, [{f"in_{k}": v for k, v in arrays.items()}], core_ids=[0])
    return result.results[0]["out"]
```

```python
import math
from contextlib import ExitStack

import numpy as np
import concourse.bass as bass
from concourse import mybir

F32, F32R, BF16 = mybir.dt.float32, mybir.dt.float32r, mybir.dt.bfloat16
I32, U32 = mybir.dt.int32, mybir.dt.uint32
ALU, ACT, AX = mybir.AluOpType, mybir.ActivationFunctionType, mybir.AxisListType

P = 128
S = 256
T = S // P
D = 2048
K = D // P
HD = 128
EPS = 1e-6
NEG = -1e30
N = 512
KC = 2
Q = K // KC
RAW = 4
WS = 4
PRE = 4
GRID_W, WINDOWS = 64, (2, 4, 8, 16)
MH, MD = 4, 256
U_AT, V_AT, PL_AT, Q_AT, O_AT, K_AT, VM_AT, G_AT = 0, 512, 1024, 1536, 2560, 3584, 4608, 5632
PH, PK, NK = 8, 16, 128
DIL = ((128, 1), (512, 4), (2048, 16))


def shape_constants():
    pos = np.arange(S, dtype=np.float32)
    inv = (1.0 / (np.float32(10000.0) ** (np.arange(0, HD, 2, dtype=np.float32) / HD))).astype(np.float32)
    ang = pos[:, None] * inv[None, :]
    cos, sin = np.cos(ang), np.sin(ang)
    tiled = lambda a: np.ascontiguousarray(a.reshape(T, P, -1).transpose(1, 0, 2), dtype=np.float32)
    i, j = np.arange(S)[:, None], np.arange(S)[None, :]
    count = sum(((i - j >= 0) & ((i - j) % d == 0) & (i - j <= (w // d) * d)).astype(np.float32) for w, d in DIL)
    eye = np.eye(P, dtype=np.float32)
    return {
        "rope_cos": tiled(np.concatenate([cos, cos], 1)),
        "rope_sin": tiled(np.concatenate([-sin, sin], 1)),
        "dilated_neg": tiled(np.where(count > 0, 0, NEG)),
        "dilated_count": tiled(count),
        "causal_neg": tiled(np.where(i >= j, 0, NEG)),
        "eye": eye,
        "flip": np.ascontiguousarray(eye[::-1]),
        "order_neg": np.ascontiguousarray(np.stack([np.where(eye.cumsum(1) > 0, 0, NEG), np.where(eye.cumsum(1).T > 0, 0, NEG)], 1), dtype=np.float32),
        "windows": window_tables(),
        "count128": np.ascontiguousarray(np.broadcast_to(np.arange(P, dtype=np.float32), (P, P))),
        "count16": np.ascontiguousarray(np.broadcast_to(np.arange(16, dtype=np.float32), (P, 16))),
    }


def window_tables():
    rows, cols = S // GRID_W, GRID_W
    both = []
    for w in WINDOWS:
        bound = lambda n: (np.clip(np.arange(n) - w // 2, 0, n), np.clip(np.arange(n) - w // 2 + w, 0, n))
        (rlo, rhi), (clo, chi) = bound(rows), bound(cols)
        r, c = np.arange(S) // cols, np.arange(S) % cols
        inside = ((r[:, None] >= rlo[r]) & (r[:, None] < rhi[r]) & (c[:, None] >= clo[c]) & (c[:, None] < chi[c]))
        count = (rhi - rlo)[r] * (chi - clo)[c]
        both.append(inside / count[None, :] - np.eye(S))
    table = np.stack(both, 1).reshape(T, P, len(WINDOWS), S).transpose(1, 0, 2, 3)
    return np.ascontiguousarray(table, dtype=np.float32)


def bass_hybrid_stack_kernel(nc, A, out):
    ctx = ExitStack()
    with ctx:
        BASE = 16512
        H_AT = BASE
        X_AT = H_AT + 65536
        XT_AT = X_AT + 16384
        RAW_AT = XT_AT + 32768
        WS_AT = RAW_AT + 32768
        C_AT = WS_AT + 32768
        cursor = [C_AT]

        def at(name, shape, offset, dt=F32):
            return nc.alloc_sbuf_tensor_at(name, shape, dt, offset=offset)

        def const(name, shape, dt=F32):
            t = at(name, shape, cursor[0], dt)
            size = int(np.prod(shape[1:])) * (2 if dt == BF16 else 4)
            cursor[0] += -(-size // 32) * 32
            assert cursor[0] <= 229368, (name, cursor[0])
            return t

        def sem(name):
            return ctx.enter_context(nc.semaphore(name))

        h = at("h", [P, T, 4 * D], H_AT)
        x = at("x", [P, T, D], X_AT)
        xt_hi = at("xt_hi", [P, K, S], XT_AT, F32R)
        xt_lo = at("xt_lo", [P, K, S], XT_AT + 16384, F32R)
        raw = at("raw", [P, RAW, KC, N], RAW_AT)
        w_hi = at("w_hi", [P, WS, N], WS_AT, F32R)
        w_lo = at("w_lo", [P, WS, N], WS_AT + 8192, F32R)
        ada_ring = at("ada_ring", [P, 2, D], RAW_AT + 16384)
        xn = at("xn", [P, T, D], WS_AT)
        xf = at("xf", [P, 2, 4 * P], H_AT + 8192)

        eye = const("eye_sb", [P, P])
        ones = const("ones", [P, P])
        small = const("small", [P, 64])
        g_ab = const("g_ab", [P, K])
        g_c = const("g_c", [P, K])
        first_const = cursor[0]
        rope_cos = const("rope_cos_sb", [P, T, HD])
        rope_sin = const("rope_sin_sb", [P, T, HD])
        dil_neg = const("dil_neg", [P, T, S])
        dil_count = const("dil_count", [P, T, S])
        cau_neg = const("cau_neg", [P, T, S])
        subln = const("subln", [P, 256])
        lam_in = const("lam_in", [P, 4])
        lam = const("lam", [P, 4])

        rot1 = [at(f"rot1{i}", [P, T, 2 * HD], o) for i, o in enumerate((XT_AT, WS_AT + 8192))]
        rot2 = [at(f"rot2{i}", [P, T, 2 * HD], o) for i, o in enumerate((XT_AT + 2048, WS_AT + 10240))]
        qk_rot = [[at(f"qk_rot{i}{s}", [P, T, 2 * HD], XT_AT + 4096 + (2 * s + i) * 2048) for i in range(2)] for s in range(2)]
        qk_t = [[at(f"qk_t{i}{s}", [P, 2, S], XT_AT + 12288 + (2 * s + i) * 2048) for i in range(2)] for s in range(2)]
        prob = [at(f"prob{s}", [P, 2, P + S], XT_AT + 20480 + s * 3072) for s in range(2)]
        prob_t = [at(f"prob_t{s}", [P, 2, 3 * P], XT_AT + 26624 + s * 3072) for s in range(2)]
        stat = [at(f"stat{s}", [P, 20], WS_AT + s * 128) for s in range(2)]
        sub_sq = at("sub_sq", [P, 1024], WS_AT + 1024)
        row_w = at("row_w", [P, D], H_AT + 16384)

        m_row = [const(f"m_row{i}", [P, D]) for i in range(2)]
        m_row1_at = cursor[0] - 8192
        m_col = const("m_col", [P, 12, K])
        ada_bias = const("ada_bias", [P, 6, K])
        ada_bias_row = at("ada_bias_row", [1, 2, D], XT_AT)
        c_col = const("c_col", [P, 2, K])
        g_mix = const("g_mix", [P, K])
        g_ffn = const("g_ffn", [P, K])
        mod = const("mod", [P, 3, K])
        gate_b = const("gate_b", [P, 16])
        gates = const("gates", [P, T, 16])
        wg = const("wg", [P, K, 16])
        cursor[0] = first_const
        wg_parts = const("wg_parts", [P, K, 32], F32R)
        flip = const("flip_sb", [P, P])
        order_neg = const("order_neg_sb", [P, 2, P])
        conv_w = const("conv_w", [P, 16, 3])
        pick = const("pick", [MH, MH, P])
        m_now = const("m_now", [MH, 2])
        m_from = const("m_from", [MH, 2, 2])
        m_to = const("m_to", [MH, 2, 2])
        decay_x = const("decay_x", [MH, 4, MH])
        col = const("col", [P, 64])
        sgu_b = const("sgu_b_sb", [P, 4])
        acc = [at(f"acc{i}", [P, D], WS_AT + 16384 + i * 8192) for i in range(2)] + [at(f"acc{i + 2}", [P, D], m_row1_at - 8192 + i * 8192) for i in range(2)]
        q_t = at("q_t", [P, 8, S], XT_AT)
        k_t = at("k_t", [P, 8, S], XT_AT + 8192)
        rows = {n: at(f"row_{n}", [MH, 2, S], XT_AT + 16384 + i * 2048) for i, n in enumerate(("i", "f", "b", "m", "a_true", "nm_true", "wk", "wp"))}
        rows["th"] = at("row_th", [MH, 2, S], WS_AT + 30720)
        v_one = at("v_one", [P, T, MH, MD + 1], WS_AT)
        v_weighed = [at(f"v_weighed{i}", [P, MD + 1], WS_AT + 8256 + i * 1056) for i in range(2)]
        from_state = [at(f"from_state{i}", [P, MD + 1], WS_AT + 10368 + i * 1056) for i in range(2)]
        num = [at(f"num{i}", [P, MD + 1], WS_AT + 12480 + i * 1056) for i in range(2)]
        e_arg = [at(f"e_arg{i}", [P, P], WS_AT + 14592 + i * 512) for i in range(2)]
        p_t = [at(f"p_t{i}", [P, P], WS_AT + 15616 + i * 512) for i in range(2)]
        conv = [at(f"conv{i}", [P, S], WS_AT + 16640 + i * 1024) for i in range(2)]
        mlstm_g = at("mlstm_g", [P, 1024], WS_AT + 18688)
        square = at("square", [P, 1024], WS_AT + 22784)

        def state(d, hh, b):
            o = 5632 + (hh * 2 + b) * (MD + 1)
            return h[:, d, o:o + MD + 1]

        sgu_w = at("sgu_w_sb", [P, 4, P], WS_AT)
        sgu_g = at("sgu_g", [P, 512], WS_AT + 2048)
        pool_w = at("pool_w_sb", [P, 4, P], WS_AT + 4096)
        pool_g = at("pool_g", [P, 512], WS_AT + 6144)
        windows = at("windows_sb", [P, T, 4, S], WS_AT + 8192)
        pooled = [at(f"pooled{i}", [P, S], WS_AT + 16384 + i * 1024) for i in range(4)]
        full = at("full", [P, K, S], H_AT + 8192)
        parts = at("parts", [P, T, 3, D], H_AT + 40960, BF16)
        rest = at("rest", [P, 2, 512], WS_AT)
        hf_rows = nc.dram_tensor("hf_rows", (3, S, D), BF16, kind="Internal").ap()
        keys = at("keys", [P, 2, NK], RAW_AT + 24576)
        pq_t = at("pq_t", [P, K, S], XT_AT)
        key_s = at("key_s", [P, T, 16, NK], XT_AT + 16384)
        less = at("less", [P, 16, NK], WS_AT + 8192)
        less2 = at("less2", [P, PH, 256], WS_AT + 16384)
        top_v = at("top_v", [P, T, 16, 16], RAW_AT + 4096)
        top_i = at("top_i", [P, T, 16, 16], RAW_AT + 6144, U32)
        top_f = at("top_f", [P, T, 16, 16], RAW_AT + 8192)
        cand = at("cand", [P, PH, 256], WS_AT + 24576)
        best_v = at("best_v", [P, T, PH, PK], RAW_AT + 12288)
        best_i = at("best_i", [P, T, PH, PK], RAW_AT + 13312, U32)
        best_s = at("best_s", [P, 2, PH * PK], RAW_AT + 14336, U32)
        best_f = at("best_f", [P, 2, PH * PK], RAW_AT + 15360)
        side = at("side", [P, T, 2, PH * PK], RAW_AT + 20480)
        expert_f = at("expert_f", [P, T, PH * PK], RAW_AT + 17408)
        gate_f = at("gate_f", [P, T, PH * PK], RAW_AT + 18432)
        gate_s = at("gate_s", [P, 32], RAW_AT + 19456)
        count16 = at("count16_sb", [P, 16], RAW_AT + 19584)
        match = at("match", [P, PH * PK, 16], WS_AT)
        cursor[0] = first_const
        idx = const("idx", [P, S], U32)
        gate_t = const("gate_t", [P, S])
        side_t = [const(f"side_t{i}", [P, S]) for i in range(2)]
        count128 = const("count128_sb", [P, P])
        three = const("three", [P, P], BF16)
        idx4 = [const(f"idx4{i}", [P, 4], U32) for i in range(2)]
        act_in = const("act_in", [P, 8])
        act_half = const("act_half", [P, 8])
        act_out = const("act_out", [P, 8])
        hot_side0 = const("hot_side0", [P, 4, P])
        hot_side1 = const("hot_side1", [P, 4, P])
        row_ring = const("row_ring", [P, 2, D], BF16)
        assert cursor[0] <= m_row1_at
        u_ring = at("u_ring", [P, 4, D], WS_AT)
        placed_w = [at(f"placed_w{t}", [P, NK, P], o) for t, o in ((0, H_AT), (1, XT_AT))]
        v_raw = [at(f"v_raw{i}", [P, D], o) for i, o in enumerate((WS_AT + 16384, WS_AT + 24576, first_const, first_const + 8192))]
        assert first_const + 16384 <= m_row1_at
        vw_hi = at("vw_hi", [P, 2, S], m_row1_at + 8192, F32R)
        vw_lo = at("vw_lo", [P, 2, S], m_row1_at + 10240, F32R)
        assert m_row1_at + 12288 <= 229368
        xe = [at(f"xe{t}", [P, D], XT_AT + t * 8192) for t in range(T)]
        last_w = at("last_w", [P, D], XT_AT + 16384)
        gated = at("gated", [P, T, N], H_AT)

        bank = ctx.enter_context(nc.psum_tensor("bank", [P, 8, 512], F32))

        x_landed, const_landed, aux_landed = sem("x_landed"), sem("const_landed"), sem("aux_landed")
        w_landed = [sem(f"w_landed{i}") for i in range(RAW)]
        out_stored = sem("out_stored")
        stage_done = sem("stage_done")
        passed, passed_pool = sem("passed"), sem("passed_pool")
        raw_used = sem("raw_used")
        hi_ready = sem("hi_ready")
        chunk_multiplied = sem("chunk_multiplied")
        ada_landed = [sem(f"ada_landed{i}") for i in range(2)]
        ada_used = sem("ada_used")
        evacuated = sem("evacuated")
        norm_step, act_step = sem("norm_step"), sem("act_step")
        blocks_turned, hi_written, lo_written = sem("blocks_turned"), sem("hi_written"), sem("lo_written")
        k_roped, second_ready, part_scaled = sem("k_roped"), sem("second_ready"), sem("part_scaled")
        roped, qk_turned, qk_copied, scored, shifted = sem("roped"), sem("qk_turned"), sem("qk_copied"), sem("scored"), sem("shifted")
        exped, weighed, p_turned, p_copied, mixed, mix_taken = (sem(n) for n in ("exped", "weighed", "p_turned", "p_copied", "mixed", "mix_taken"))

        names = """silu_done acc_summed row_taken gates_multiplied ml_a ml_row ml_exp conv_turned convolved conv_silu conv_scaled
            upd_weighed upd_multiplied upd_taken ml_weighted ml_scored ml_taken ml_mixed ml_exponent ml_exped ml_scaled
            mix_ready mix_multiplied mix_scaled mix_gelu mix_square out_root out_square full_ready part_copied part_rest part_low
            back_turned hf_stored pq_copied pq_turned keys_copied keys_scored gate_shifted gate_exped chosen chosen_turned
            rings_free half_spread halves_read placed one_hot weights_taken values_free indices_copied values_high values_split values_multiplied vw_high vw_low gelued wg_ready"""
        (silu_done, acc_summed, row_taken, gates_multiplied, ml_a, ml_row, ml_exp, conv_turned, convolved, conv_silu, conv_scaled,
         upd_weighed, upd_multiplied, upd_taken, ml_weighted, ml_scored, ml_taken, ml_mixed, ml_exponent, ml_exped, ml_scaled,
         mix_ready, mix_multiplied, mix_scaled, mix_gelu, mix_square, out_root, out_square, full_ready, part_copied, part_rest, part_low,
         back_turned, hf_stored, pq_copied, pq_turned, keys_copied, keys_scored, gate_shifted, gate_exped, chosen, chosen_turned,
         rings_free, half_spread, halves_read, placed, one_hot, weights_taken, values_free, indices_copied, values_high, values_split, values_multiplied, vw_high, vw_low, gelued, wg_ready) = (sem(n) for n in names.split())
        rows_landed = [sem(f"rows_landed{i}") for i in range(4)]
        u_landed = [sem(f"u_landed{i}") for i in range(4)]
        v_landed = [sem(f"v_landed{i}") for i in range(4)]

        block = ctx.enter_context(nc.Block())

        plan = {}
        chunks = tiles = 0
        for name, n in (("ab_in", 16), ("ab_out", 4), ("c_in", 16), ("c_out", 4)):
            plan[name] = dict(n=n, c0=chunks, t0=tiles)
            chunks += n * Q
            tiles += n
        weights = {"ab_in": A["w_in_ab"][0], "ab_out": A["w_out_ab"][0], "c_in": A["w_in_c"][0], "c_out": A["w_out_c"][0]}
        for name, n, first in (("ctx", 4, K_AT), ("lat", 11, 0), ("mix_out", 4, 0), ("wq", 4, 0)):
            plan[name] = dict(n=n, c0=chunks, t0=tiles, **{"from": first})
            chunks += n * Q
            tiles += n + n % 2
        weights.update(ctx=A["w_in_2"][0], lat=A["w_in_2"][0], mix_out=A["w_out_2"][0], wq=A["peer_wq_2"][0])

        one = [[(j, 0, 0, True)] for j in range(4)]
        plan["ab_in"]["ada"] = dict(a0=0, per=2, groups=(0, 1), sums=range(4), work=[[(0, 0, 0, False)], [(0, 1, 2, True)], [(1, 0, 1, False)], [(1, 1, 3, True)]])
        plan["ab_out"]["ada"] = dict(a0=32, per=4, groups=(3,), sums=(0,), work=one)
        plan["c_in"]["ada"] = dict(a0=48, per=2, groups=(2, 5), sums=(0, 1), work=[[(0, 0, 0, True)], [], [(1, 0, 1, True)], []])
        plan["c_out"]["ada"] = dict(a0=80, per=4, groups=(4,), sums=(0,), work=one)
        plan["ctx"]["to"] = K_AT

        stages = {"pe": 0, "act": 0, "dve": 0}

        def end_of_stage(eng, who):
            stages[who] += 1
            eng.drain().then_inc(stage_done, 1)
            eng.wait_ge(stage_done, 3 * stages[who])

        def wide(ap, shape):
            return ap.broadcast_to(shape)

        def stream_sp(sp, g):
            w = weights[g["name"]].rearrange("(q k p) n -> q p k n", k=KC, p=P)

            def tile(n, dt):
                for q in range(Q):
                    c = g["c0"] + Q * n + q
                    sp.wait_ge(raw_used, KC * (c + 1))
                    sp.dma_start(raw[:, q % RAW, :, :], w[q][:, :, dt(n)]).then_inc(w_landed[q % RAW], 16)

            with sp.Fori(0, g["n"]) as n:
                tile(n, lambda n: bass.ds(n * N + g.get("from", 0), N))

        def pairs_then_rest(eng, n, body, start=0):
            m = (n - start) // 2
            if m:
                with eng.Fori(0, m) as i:
                    for s in range(2):
                        body(2 * i + start + s, (start + s) % 2)
            if (n - start) % 2:
                body(n - 1, (n - 1) % 2)

        def take_h(act, g, n, s):
            act.wait_ge(chunk_multiplied, PRE + g["c0"] * KC + K * (n + 1))
            act.sem_inc(passed, 1)
            for t in range(T):
                last = act.activation(h[:, t, bass.ds(n * N + g.get("to", 0), N)], bank[:, 2 * s + t, :], ACT.Copy)
            last.then_inc(evacuated, 1)

        def gemm_act(act, g, take=False):
            def tile(n, s, before=take):
                for kk in range(K):
                    if before and kk == WS:
                        take_h(act, g, n - 1, 1 - s)
                    q = kk // KC
                    if kk % KC == 0:
                        act.wait_ge(w_landed[q % RAW], 16 * (g["c0"] // RAW + Q // RAW * n + q // RAW + 1))
                    act.wait_ge(chunk_multiplied, PRE + g["c0"] * KC + K * n + kk - WS + 1)
                    act.activation(w_hi[:, kk % WS, :], raw[:, q % RAW, kk % KC, :], ACT.Copy).then_inc(hi_ready, 1)
            tile(0, 0, False)
            pairs_then_rest(act, g["n"], tile, 1)
            if take:
                take_h(act, g, g["n"] - 1, (g["n"] - 1) % 2)
                if g["n"] % 2:
                    act.sem_inc(evacuated, 1)

        def gemm_pe(pe, g):
            def tile(n, s):
                pe.wait_ge(evacuated, PRE + g["t0"] + n - 1)
                for kk in range(K):
                    pe.wait_ge(raw_used, RAW * KC + g["c0"] * KC + K * n + kk + 1)
                    for t in range(T):
                        o = bank[:, 2 * s + t, :]
                        a_hi, a_lo = xt_hi[:, kk, t * P:(t + 1) * P], xt_lo[:, kk, t * P:(t + 1) * P]
                        b_hi, b_lo = w_hi[:, kk % WS, :], w_lo[:, kk % WS, :]
                        pe.matmul(o, a_hi, b_hi, start=kk == 0, stop=False)
                        pe.matmul(o, a_hi, b_lo, start=False, stop=False)
                        last = pe.matmul(o, a_lo, b_hi, start=False, stop=kk == K - 1)
                    last.then_inc(chunk_multiplied, 1)
            pairs_then_rest(pe, g["n"], tile)

        def gemm_dve(dve, g, take=None):
            ada = g.get("ada")

            def low(n, kk):
                dve.wait_ge(hi_ready, PRE + g["c0"] * KC + K * n + kk + 1)
                dve.tensor_tensor(w_lo[:, kk % WS, :], raw[:, kk // KC % RAW, kk % KC, :],
                                  w_hi[:, kk % WS, :].bitcast(F32), ALU.subtract).then_inc(raw_used, 1)

            def evacuate(n, s):
                dve.wait_ge(chunk_multiplied, PRE + g["c0"] * KC + K * (n + 1))
                take(dve, n, s)

            def modulate(n, part):
                for j, v, to, last in ada["work"][part]:
                    k = n if ada["per"] == 2 else n * 4 + j
                    dve.drain()
                    dve.wait_ge(ada_landed[j % 2], 16 * (ada["per"] // 2 * n + (ada["a0"] // 2 + j // 2 + 1)))
                    o = acc[to][:, :]
                    done = dve.scalar_tensor_tensor(o, ada_ring[:, j % 2, :], c_col[:, v, bass.ds(k, 1)], o, ALU.mult, ALU.add)
                    if last:
                        done.then_inc(ada_used, 1)

            def step(n, s, before=True):
                for kk in range(K):
                    low(n, kk)
                    if kk == WS - 1 and before and take:
                        evacuate(n - 1, 1 - s)
                    if kk % 4 == 3 and ada:
                        modulate(n, kk // 4)

            if ada:
                for to in ada["sums"]:
                    dve.memset(acc[to][:, :], 0.0)
            step(0, 0, False)
            pairs_then_rest(dve, g["n"], step, 1)
            if take:
                evacuate(g["n"] - 1, (g["n"] - 1) % 2)

        def take_residual(dve, n, s):
            for t in range(T):
                o = x[:, t, bass.ds(n * N, N)]
                last = dve.tensor_tensor(o, bank[:, 2 * s + t, :], o, ALU.add)
            last.then_inc(evacuated, 1)

        GQ = K // 4
        NG = T * GQ

        def newton(dve, r, root, v, tmp):
            dve.reciprocal(r, root)
            dve.drain()
            dve.tensor_tensor(tmp, r, r, ALU.mult)
            dve.drain()
            dve.tensor_tensor(tmp, tmp, v, ALU.mult)
            dve.drain()
            dve.tensor_scalar(tmp, tmp, -0.5, 1.5, ALU.mult, ALU.add)
            dve.drain()
            dve.tensor_tensor(r, r, tmp, ALU.mult)

        def rstd_act(act, src, u):
            act.activation(xn[:, 0, :], src[:, 0, :], ACT.Square, accum_out=small[:, 0:1]).then_inc(act_step, 1)
            act.wait_ge(norm_step, PRE + 3 * u + 1)
            act.activation(small[:, 4:4 + T], small[:, 2:2 + T], ACT.Sqrt).then_inc(act_step, 1)

        def rstd_dve(dve, u, src):
            dve.tensor_tensor_reduce(xn[:, 1, :], src[:, 1, :], src[:, 1, :], 1.0, 0.0, ALU.mult, ALU.add, small[:, 1:2])
            dve.drain()
            dve.wait_ge(act_step, PRE + 2 * u + 1)
            dve.tensor_scalar(small[:, 2:2 + T], small[:, 0:T], 1.0 / D, EPS, ALU.mult, ALU.add).then_inc(norm_step, 1)
            dve.wait_ge(act_step, PRE + 2 * u + 2)
            newton(dve, small[:, 6:6 + T], small[:, 4:4 + T], small[:, 2:2 + T], small[:, 62:62 + T])
            dve.drain().then_inc(norm_step, 1)

        def normalise_dve(dve, u, src):
            rstd_dve(dve, u, src)
            dve.tensor_scalar(xn[:, 0, :], src[:, 0, :], small[:, 6:7], None, ALU.mult).then_inc(norm_step, 1)

        def normalise_act(act, src, u):
            rstd_act(act, src, u)
            act.wait_ge(norm_step, PRE + 3 * u + 2)
            act.activation(xn[:, 1, :], src[:, 1, :], ACT.Copy, scale=small[:, 7:8]).then_inc(second_ready, 1)

        def turn_pe(pe, v, src, rows, column=lambda kk: kk * P):
            if rows:
                pe.wait_ge(norm_step, rows)
            ring = 3 if rows else 4
            for g in range(NG):
                t = g // GQ
                if g >= ring:
                    pe.wait_ge(lo_written, PRE + NG * v + g - ring + 1)
                if g == GQ and rows:
                    pe.wait_ge(second_ready, (0, 2, 4, 5, 7).index(v) + 1)
                for j in range(4):
                    kk = (g % GQ) * 4 + j
                    o = bank[:, g % 3 + 4 * (j // 2), j % 2 * P:(j % 2 + 1) * P] if rows else bank[:, g % 4, j * P:(j + 1) * P]
                    last = pe.transpose(o, src[:, t, column(kk):column(kk) + P], eye[:, :])
                last.then_inc(blocks_turned, 1)

        def group(xt, g):
            return xt[:, (g % GQ) * 4:(g % GQ) * 4 + 4, (g // GQ) * P:(g // GQ + 1) * P]

        def turned(g):
            return bank[:, g % 4, :].rearrange("p (k n) -> p k n", k=4)

        def turn_act(act, v, scaled):
            for g in range(NG):
                act.wait_ge(blocks_turned, PRE + NG * v + g + 1)
                src = turned(g)
                if scaled:
                    (scale, shift), s0 = scaled
                    if g >= 2:
                        act.wait_ge(lo_written, PRE + NG * v + g - 1)
                    for j in range(2):
                        k = g % GQ * 4 + j
                        act.activation(xf[:, g % 2, j * P:(j + 1) * P], bank[:, g % 3, j * P:(j + 1) * P], ACT.Identity,
                                       scale=scale[:, k:k + 1], bias=0.0 if shift is None else shift[:, k:k + 1])
                    act.drain()
                    act.wait_ge(part_scaled, s0 + g + 1)
                    src = xf[:, g % 2, :].rearrange("p (k n) -> p k n", k=4)
                act.activation(group(xt_hi, g), src, ACT.Copy).then_inc(hi_written, 1)

        def turn_dve(dve, v, scaled):
            def low(g):
                src = xf[:, g % 2, :].rearrange("p (k n) -> p k n", k=4) if scaled else turned(g)
                dve.wait_ge(hi_written, PRE + NG * v + g + 1)
                dve.tensor_tensor(group(xt_lo, g), src, group(xt_hi, g).bitcast(F32), ALU.subtract).then_inc(lo_written, 1)

            for g in range(NG):
                if scaled:
                    (scale, shift), s0 = scaled
                    f = xf[:, g % 2, 2 * P:].rearrange("p (k n) -> p k n", k=2)
                    c = slice(g % GQ * 4 + 2, g % GQ * 4 + 4)
                    dve.drain()
                    dve.wait_ge(blocks_turned, PRE + NG * v + g + 1)
                    last = dve.tensor_tensor(f, bank[:, 4 + g % 3, 0:2 * P].rearrange("p (k n) -> p k n", k=2), wide(scale[:, c].unsqueeze(2), [P, 2, P]), ALU.mult)
                    if shift is not None:
                        dve.drain()
                        last = dve.tensor_tensor(f, f, wide(shift[:, c].unsqueeze(2), [P, 2, P]), ALU.add)
                    last.then_inc(part_scaled, 1)
                    if g:
                        low(g - 1)
                else:
                    low(g)
            if scaled:
                low(NG - 1)

        SCALE = HD ** -0.5
        W = (P, S)
        OFF = (0, P)

        def rope(eng, a, p, s, i, done, carrier):
            g = a["p0"] + p
            src = h[:, :, bass.ds(p * 256 + a["qk"[i]], 256)].rearrange("p t (h d) -> p t h d", h=2)
            tw = lambda b: b.rearrange("p t (h d) -> p t h d", h=2)
            r1, r2, dst = tw(rot1[i][:, :, :]), tw(rot2[i][:, :, :]), tw(qk_rot[s][i][:, :, :])
            cos = wide(rope_cos[:, :, :].unsqueeze(2), [P, T, 2, HD])
            sin = wide(rope_sin[:, :, :].unsqueeze(2), [P, T, 2, HD])
            eng.drain()
            eng.tensor_tensor(r1, src, cos, ALU.mult)
            eng.tensor_tensor(r2[:, :, :, 0:64], src[:, :, :, 64:128], sin[:, :, :, 0:64], ALU.mult)
            eng.tensor_tensor(r2[:, :, :, 64:128], src[:, :, :, 0:64], sin[:, :, :, 64:128], ALU.mult)
            eng.drain()
            eng.wait_ge(qk_turned, PRE + g - 1)
            eng.sem_inc(carrier, 1)
            eng.tensor_tensor(dst, r1, r2, ALU.add).then_inc(done, 1)

        def attention_pool(pool, a):
            pool.wait_ge(stage_done, 3 * attention_from[a["kind"]])
            with pool.Fori(0, a["n"] // 2) as i:
                for s in range(2):
                    rope(pool, a, 2 * i + s, s, 1, k_roped, passed_pool)

        def turn_qk_pe(pe, a, p, s):
            g = a["p0"] + p
            pe.wait_ge(roped, PRE + g + 1)
            pe.wait_ge(k_roped, PRE + g + 1)
            pe.wait_ge(qk_copied, PRE + g)
            for i in range(2):
                for hh in range(2):
                    for t in range(T):
                        last = pe.transpose(bank[:, i, (hh * T + t) * P:(hh * T + t + 1) * P],
                                            qk_rot[s][i][:, t, hh * HD:(hh + 1) * HD], eye[:, :])
            last.then_inc(qk_turned, 1)

        def copy_qk_act(act, a, p, s):
            g = a["p0"] + p
            act.wait_ge(qk_turned, PRE + g + 1)
            act.wait_ge(scored, PRE + g - 1)
            for i in range(2):
                last = act.activation(qk_t[s][i][:, :, :].rearrange("p h n -> p (h n)"), bank[:, i, :], ACT.Copy)
            last.then_inc(qk_copied, 1)

        def score_pe(pe, a, p, s):
            g = a["p0"] + p
            pe.wait_ge(qk_copied, PRE + g + 1)
            pe.wait_ge(shifted, PRE + g)
            for t in range(T):
                for hh in range(2):
                    last = pe.matmul(bank[:, 2 + t, hh * S:hh * S + W[t]], qk_t[s][0][:, hh, t * P:(t + 1) * P],
                                     qk_t[s][1][:, hh, 0:W[t]], start=True, stop=True)
            last.then_inc(scored, 1)

        def shift_dve(dve, a, p, s):
            g = a["p0"] + p
            dve.wait_ge(scored, PRE + g + 1)
            dve.wait_ge(p_turned, PRE + g - 1)
            dve.sem_inc(passed, 1)
            for t in range(T):
                for hh in range(2):
                    last = dve.tensor_tensor_reduce(prob[s][:, hh, OFF[t]:OFF[t] + W[t]], bank[:, 2 + t, hh * S:hh * S + W[t]],
                                                    a["neg"][:, t, 0:W[t]], SCALE, NEG, ALU.add, ALU.max,
                                                    stat[s][:, 2 * t + hh:2 * t + hh + 1])
            dve.drain()
            dve.tensor_scalar(stat[s][:, 4:8], stat[s][:, 0:4], -1.0, None, ALU.mult).then_inc(shifted, 1)

        def exp_act(act, a, p, s):
            g = a["p0"] + p
            act.wait_ge(shifted, PRE + g + 1)
            for t in range(T):
                for hh in range(2):
                    c = 2 * t + hh
                    e = prob[s][:, hh, OFF[t]:OFF[t] + W[t]]
                    last = act.activation(e, e, ACT.Exp, bias=stat[s][:, 4 + c:5 + c], accum_out=stat[s][:, 8 + c:9 + c])
            last.then_inc(exped, 1)

        def weigh_dve(dve, a, p, s):
            g = a["p0"] + p
            dve.wait_ge(exped, PRE + g + 1)
            if a["kind"] == "dilated":
                dve.sem_inc(passed, 1)
                for t in range(T):
                    for hh in range(2):
                        c = 2 * t + hh
                        e = prob[s][:, hh, OFF[t]:OFF[t] + W[t]]
                        dve.tensor_tensor_reduce(e, e, dil_count[:, t, 0:W[t]], 1.0, 0.0, ALU.mult, ALU.add,
                                                 stat[s][:, 8 + c:9 + c])
                dve.drain()
            last = dve.reciprocal(stat[s][:, 12:16], stat[s][:, 8:12])
            if a["kind"] == "difference":
                dve.drain()
                for t in range(T):
                    dve.tensor_scalar(stat[s][:, 16 + t:17 + t], stat[s][:, 13 + 2 * t:14 + 2 * t], lam[:, 2:3], None, ALU.mult)
                dve.drain()
                for t in range(T):
                    e = prob[s][:, 1, OFF[t]:OFF[t] + W[t]]
                    dve.tensor_scalar(e, e, stat[s][:, 16 + t:17 + t], None, ALU.mult)
                dve.drain()
                for t in range(T):
                    e = prob[s][:, 0, OFF[t]:OFF[t] + W[t]]
                    last = dve.scalar_tensor_tensor(e, e, stat[s][:, 12 + 2 * t:13 + 2 * t], prob[s][:, 1, OFF[t]:OFF[t] + W[t]],
                                                    ALU.mult, ALU.add)
            last.then_inc(weighed, 1)

        def heads_of(a):
            return 1 if a["kind"] == "difference" else 2

        def turn_p_pe(pe, a, p, s):
            g = a["p0"] + p
            pe.wait_ge(weighed, PRE + g + 1)
            pe.wait_ge(p_copied, PRE + g)
            for hh in range(heads_of(a)):
                for b in range(3):
                    last = pe.transpose(bank[:, 4 + hh, b * P:(b + 1) * P], prob[s][:, hh, b * P:(b + 1) * P], eye[:, :])
            last.then_inc(p_turned, 1)

        def copy_p_act(act, a, p, s):
            g = a["p0"] + p
            act.wait_ge(p_turned, PRE + g + 1)
            act.wait_ge(mixed, PRE + g - 1)
            for hh in range(heads_of(a)):
                last = act.activation(prob_t[s][:, hh, :], bank[:, 4 + hh, 0:3 * P], ACT.Copy)
            last.then_inc(p_copied, 1)

        def mix_pe(pe, a, p, s):
            g = a["p0"] + p
            w = 256 // heads_of(a)
            pe.wait_ge(p_copied, PRE + g + 1)
            pe.wait_ge(mix_taken, PRE + g)
            for hh in range(heads_of(a)):
                v = [h[:, t, bass.ds(p * 256 + (a["v"] + hh * w), w)] for t in range(T)]
                o = [bank[:, 6, t * 256 + hh * w:t * 256 + hh * w + w] for t in range(T)]
                pe.matmul(o[0], prob_t[s][:, hh, 0:P], v[0], start=True, stop=True)
                pe.matmul(o[1], prob_t[s][:, hh, P:2 * P], v[0], start=True, stop=False)
                last = pe.matmul(o[1], prob_t[s][:, hh, 2 * P:3 * P], v[1], start=False, stop=True)
            last.then_inc(mixed, 1)

        def out_dve(dve, a, p, s):
            g = a["p0"] + p
            dve.wait_ge(mixed, PRE + g + 1)
            for t in range(T):
                if a["kind"] == "difference":
                    last = dve.tensor_scalar(h[:, t, bass.ds(p * 256 + a["q"], 256)], bank[:, 6, t * 256:(t + 1) * 256], 1.0, None, ALU.mult)
                else:
                    for hh in range(2):
                        z = h[:, t, bass.ds(p * 256 + (a["z"] + hh * HD), HD)]
                        last = dve.scalar_tensor_tensor(z, bank[:, 6, t * 256 + hh * HD:t * 256 + (hh + 1) * HD],
                                                        stat[s][:, 12 + 2 * t + hh:13 + 2 * t + hh], z, ALU.mult, ALU.mult)
            last.then_inc(mix_taken, 1)

        def steps(eng, n, step):
            if n > 2:
                with eng.Fori(0, (n - 2) // 2) as i:
                    step(2 * i, 0, 2)
                    step(2 * i + 1, 1, 2)
            step(n - 2, 0, 1)
            step(n - 1, 1, 0)

        def attention_pe(pe, a):
            def step(p, s, ahead):
                if ahead:
                    turn_qk_pe(pe, a, p + 1, 1 - s)
                turn_p_pe(pe, a, p, s)
                if ahead:
                    score_pe(pe, a, p + 1, 1 - s)
                mix_pe(pe, a, p, s)
            turn_qk_pe(pe, a, 0, 0)
            score_pe(pe, a, 0, 0)
            steps(pe, a["n"], step)

        def attention_act(act, a):
            def step(p, s, ahead):
                if ahead:
                    copy_qk_act(act, a, p + 1, 1 - s)
                copy_p_act(act, a, p, s)
                if ahead:
                    exp_act(act, a, p + 1, 1 - s)
            copy_qk_act(act, a, 0, 0)
            exp_act(act, a, 0, 0)
            steps(act, a["n"], step)

        attention_from = {}

        def attention_dve(dve, a):
            def step(p, s, ahead):
                if ahead > 1:
                    rope(dve, a, p + 2, s, 0, roped, passed)
                if ahead:
                    shift_dve(dve, a, p + 1, 1 - s)
                out_dve(dve, a, p, s)
                if ahead:
                    weigh_dve(dve, a, p + 1, 1 - s)
            attention_from[a["kind"]] = stages["dve"]
            rope(dve, a, 0, 0, 0, roped, passed)
            rope(dve, a, 1, 1, 0, roped, passed)
            shift_dve(dve, a, 0, 0)
            weigh_dve(dve, a, 0, 0)
            steps(dve, a["n"], step)

        ATT = {
            "a": dict(kind="dilated", n=4, p0=0, q=0, k=1024, v=2048, z=6144, neg=dil_neg),
            "b": dict(kind="difference", n=4, p0=4, q=3072, k=4096, v=5120, z=7168, neg=cau_neg),
            "c": dict(kind="causal", n=8, p0=8, q=0, k=2048, v=4096, z=6144, neg=cau_neg),
        }
        LAM_INIT = 0.8 - 0.6 * math.exp(-0.3 * 0)
        for name in plan:
            plan[name]["name"] = name
        gate = lambda b: b[:, :, 6144:8192]



        def ada_pool(pool):
            w = A["ada_w_2"][0].rearrange("(k p) n -> k p n", p=P)
            for name in ("ab_in", "ab_out", "c_in", "c_out"):
                for kind in {"ab_out": "ab", "c_out": "c"}.get(name, ""):
                    attention_pool(pool, ATT[kind])
                a = plan[name]["ada"]
                with pool.Fori(0, plan[name]["n"]) as n:
                    for j in range(a["per"]):
                        k, g = (n, a["groups"][j]) if a["per"] == 2 else (4 * n + j, a["groups"][0])
                        pool.wait_ge(ada_used, PRE + (a["per"] * n + (a["a0"] + j - 1)))
                        pool.sem_inc(passed_pool, 1)
                        pool.dma_start(ada_ring[:, j % 2, :], w[bass.ds(k, 1), :, g * D:(g + 1) * D].rearrange("o p n -> p (o n)")).then_inc(ada_landed[j % 2], 16)

        def sum_pe(pe, sums, b=5):
            for i, v, g in sums:
                for kk in range(K):
                    o = (v * 6 + g) * K + kk
                    last = pe.matmul(bank[:, b, o:o + 1], acc[i][:, kk * P:(kk + 1) * P], ones[:, 0:1], start=True, stop=True)
            last.then_inc(acc_summed, 1)

        def sum_dve(dve, sums, count, b=5):
            dve.wait_ge(acc_summed, count)
            for i, v, g in sums:
                o = (v * 6 + g) * K
                dve.tensor_tensor(m_col[:, v * 6 + g, :], bank[:, b, o:o + K], ada_bias[:, g, :], ALU.add)

        SUM_AB_IN = ((0, 0, 0), (1, 0, 1), (2, 1, 0), (3, 1, 1))
        SUM_AB_OUT = ((0, 0, 3),)
        SUM_C_OUT = ((0, 0, 4),)

        def rows_pe(pe):
            pe.wait_ge(aux_landed, 16)
            for i in range(2):
                if i:
                    pe.wait_ge(row_taken, 1)
                for c in range(4):
                    pe.matmul(bank[:, 4 + c, :], ones[:, :], acc[i][:, c * 512:(c + 1) * 512], start=True, stop=False)
                    last = pe.matmul(bank[:, 4 + c, :], ones[0:1, :], ada_bias_row[0:1, i, c * 512:(c + 1) * 512], start=False, stop=True)
                last.then_inc(acc_summed, 1)

        def rows_act(act):
            for i in range(2):
                act.wait_ge(acc_summed, 3 + i)
                act.activation(m_row[i][:, :].rearrange("p (c n) -> p c n", c=4), bank[:, 4:8, :], ACT.Copy).then_inc(row_taken, 1)

        def gates_pe(pe, u):
            for t in range(T):
                for kk in range(K):
                    a_hi, a_lo = xt_hi[:, kk, t * P:(t + 1) * P], xt_lo[:, kk, t * P:(t + 1) * P]
                    o = bank[:, 4 + t, 0:32]
                    pe.matmul(o, a_hi, wg_parts[:, kk, :], start=kk == 0, stop=False, skip_group_check=True)
                    last = pe.matmul(o[:, 0:16], a_lo, wg_parts[:, kk, 0:16], start=False, stop=kk == K - 1, skip_group_check=True)
            last.then_inc(gates_multiplied, 1)

        def gates_dve(dve, u):
            dve.wait_ge(gates_multiplied, u + 1)
            for t in range(T):
                dve.tensor_tensor(gates[:, t, :], bank[:, 4 + t, 0:16], gate_b[:, :], ALU.add)
            dve.drain()
            for t in range(T):
                dve.tensor_tensor(gates[:, t, :], gates[:, t, :], bank[:, 4 + t, 16:32], ALU.add)

        r_ = lambda n: rows[n][:, :, :]
        chunk = lambda n: rows[n][:, :, :].rearrange("h d (c n) -> h d c n", c=2)

        def ml_rows_pe(pe):
            for kind in range(2):
                for d in range(2):
                    for ci in range(2):
                        t = 1 - ci if d else ci
                        o = (d * 2 + ci) * P
                        last = pe.matmul(bank[0:MH, 4 + kind, o:o + P], gates[:, t, d * 8 + kind * 4:d * 8 + kind * 4 + 4],
                                         (flip if d else eye)[:, :], start=True, stop=True)
            last.then_inc(ml_a, 1)

        def ml_rows_dve(dve, u):
            dve.wait_ge(ml_a, 2 * u + 1)
            for kind, n in ((0, "i"), (1, "f")):
                dve.tensor_copy(r_(n), bank[0:MH, 4 + kind, :].rearrange("h (d n) -> h d n", d=2))
            dve.drain()
            dve.scalar_tensor_tensor(r_("b"), r_("f"), -1.0, r_("f"), ALU.mult, ALU.max)
            dve.drain().then_inc(ml_row, 1)
            dve.wait_ge(ml_exp, 3 * u + 1)
            dve.tensor_scalar(r_("b"), r_("b"), 1.0, None, ALU.add)
            dve.drain().then_inc(ml_row, 1)
            dve.wait_ge(ml_exp, 3 * u + 2)
            dve.scalar_tensor_tensor(r_("f"), r_("f"), 0.0, r_("b"), ALU.min, ALU.subtract)
            dve.drain()
            for d in range(2):
                for ci in range(2):
                    o = slice(ci * P, (ci + 1) * P)
                    dve.tensor_tensor_scan(rows["b"][:, d, o], ones[0:MH, :], rows["f"][:, d, o], 0.0, ALU.mult, ALU.add)
            dve.drain()
            dve.tensor_tensor(r_("i"), r_("i"), r_("b"), ALU.subtract)
            for ci in range(2):
                o = slice(ci * P, (ci + 1) * P)
                dve.drain()
                dve.tensor_copy(m_from[:, :, ci], m_now[:, :])
                dve.drain()
                for d in range(2):
                    dve.tensor_tensor_scan(rows["m"][:, d, o], ones[0:MH, :], rows["i"][:, d, o], m_now[:, d:d + 1], ALU.mult, ALU.max)
                dve.drain()
                dve.tensor_copy(m_to[:, :, ci], rows["m"][:, :, ci * P + P - 1])
                dve.drain()
                dve.tensor_tensor(m_now[:, :], rows["b"][:, :, ci * P + P - 1], m_to[:, :, ci], ALU.add)
            dve.drain()
            dve.tensor_tensor(r_("th"), r_("b"), r_("m"), ALU.add)
            dve.drain()
            dve.tensor_tensor(chunk("f"), chunk("i"), wide(m_to[:, :, :].unsqueeze(3), [MH, 2, 2, P]), ALU.subtract)
            dve.tensor_tensor(chunk("b"), wide(m_from[:, :, :].unsqueeze(3), [MH, 2, 2, P]), chunk("m"), ALU.subtract)
            dve.drain()
            dve.tensor_tensor(m_from[:, :, :], m_from[:, :, :], m_to[:, :, :], ALU.subtract)
            for d in range(2):
                step = -1 if d else 1
                dve.tensor_copy(rows["a_true"][:, d, :], rows["i"][:, d, ::step])
                dve.tensor_scalar(rows["nm_true"][:, d, :], rows["m"][:, d, ::step], -1.0, None, ALU.mult)
            dve.drain().then_inc(ml_row, 1)
            dve.wait_ge(ml_exp, 3 * u + 3)
            dve.tensor_tensor(decay_x[:, :, :], wide(m_from[:, :, :].rearrange("h d c -> h (d c)").unsqueeze(2), [MH, 4, MH]),
                              wide(eye[0:MH, 0:MH].unsqueeze(1), [MH, 4, MH]), ALU.mult)

        def ml_rows_act(act, u):
            act.wait_ge(ml_row, 3 * u + 1)
            act.activation(r_("b"), r_("b"), ACT.Exp, scale=-1.0).then_inc(ml_exp, 1)
            act.wait_ge(ml_row, 3 * u + 2)
            act.activation(r_("b"), r_("b"), ACT.Ln).then_inc(ml_exp, 1)
            act.wait_ge(ml_row, 3 * u + 3)
            for d in range(2):
                step = -1 if d else 1
                act.activation(rows["wk"][:, d, :], rows["f"][:, d, ::step], ACT.Exp)
                act.activation(rows["wp"][:, d, :], rows["b"][:, d, ::step], ACT.Exp)
            act.activation(m_from[:, :, :], m_from[:, :, :], ACT.Exp)
            for d in range(2):
                step = -1 if d else 1
                last = act.activation(rows["i"][:, d, :], rows["th"][:, d, ::step], ACT.Exp, scale=-1.0)
            act.drain().then_inc(ml_exp, 1)

        def conv_blocks(out):
            return [(K_AT + j * P, k_t, j, 8 + j) for j in range(8)] + ([(Q_AT + j * P, q_t, j, j) for j in range(8)] if out else [])

        def conv_pe(pe, c0, out):
            for i, (at_, _, _, _) in enumerate(conv_blocks(out)):
                if i >= 4:
                    pe.wait_ge(convolved, c0 + i - 3)
                for t in range(T):
                    last = pe.transpose(bank[:, i % 4, t * P:(t + 1) * P], h[:, t, at_:at_ + P], eye[:, :])
                last.then_inc(conv_turned, 1)

        def conv_dve(dve, c0, out):
            for i, (_, _, _, b) in enumerate(conv_blocks(out)):
                src, dst = bank[:, i % 4, 0:S], conv[i % 2]
                dve.wait_ge(conv_scaled, c0 + i + 1)
                dve.scalar_tensor_tensor(dst[:, 1:S], src[:, 0:S - 1], conv_w[:, b, 0:1], dst[:, 1:S], ALU.mult, ALU.add)
                dve.drain()
                dve.scalar_tensor_tensor(dst[:, 0:S - 1], src[:, 1:S], conv_w[:, b, 2:3], dst[:, 0:S - 1], ALU.mult, ALU.add).then_inc(convolved, 1)

        def conv_act(act, c0, out):
            blocks = conv_blocks(out)
            for i in range(len(blocks) + 1):
                if i < len(blocks):
                    b = blocks[i][3]
                    act.drain()
                    act.wait_ge(conv_turned, c0 + i + 1)
                    act.activation(conv[i % 2][:, :], bank[:, i % 4, 0:S], ACT.Copy, scale=conv_w[:, b, 1:2]).then_inc(conv_scaled, 1)
                if i:
                    _, target, j, _ = blocks[i - 1]
                    act.wait_ge(convolved, c0 + i)
                    act.activation(target[:, j, :], conv[(i - 1) % 2][:, :], ACT.Silu).then_inc(conv_silu, 1)

        def ml_cols_pe(pe, u):
            for g in range(4):
                t, half = g // 2, g % 2
                for j in range(4):
                    last = pe.transpose(bank[:, g, j * P:(j + 1) * P], k_t[:, half * 4 + j, t * P:(t + 1) * P], eye[:, :])
            for q, n in enumerate(("wk", "wp", "i")):
                for d in range(2):
                    for t in range(T):
                        o = q * 16 + d * 8 + t * 4
                        pe.matmul(bank[:, 6, o:o + 4], rows[n][:, d, t * P:(t + 1) * P], eye[0:MH, 0:MH], start=True, stop=True)
            pe.matmul(bank[:, 6, 48:64], ones[0:MH, :], decay_x[:, :, :].rearrange("h c n -> h (c n)"), start=True, stop=True).then_inc(ml_a, 1)

        def ml_cols_act(act, u):
            act.wait_ge(ml_a, 2 * u + 2)
            for g in range(4):
                t, half = g // 2, g % 2
                act.activation(h[:, t, K_AT + half * 512:K_AT + half * 512 + 512], bank[:, g, :], ACT.Copy, scale=MD ** -0.5)

        def ml_cols_dve(dve, u):
            for t in range(T):
                dve.tensor_copy(v_one[:, t, :, 0:MD], h[:, t, VM_AT:VM_AT + 1024].rearrange("p (h d) -> p h d", h=MH))
                dve.memset(v_one[:, t, :, MD:MD + 1], 1.0)
            dve.wait_ge(ml_a, 2 * u + 2)
            dve.tensor_copy(col[:, :], bank[:, 6, 0:64])

        def units(ci):
            return [(d, 1 - ci if d else ci, hh) for d in range(2) for hh in range(MH)]

        def coef(q, d, t, hh):
            return col[:, q * 16 + d * 8 + t * 4 + hh:q * 16 + d * 8 + t * 4 + hh + 1]

        def update_act(act, w0, ci):
            for j, (d, t, hh) in enumerate(units(ci)):
                if j >= 2:
                    act.wait_ge(upd_multiplied, w0 + j - 1)
                act.activation(v_weighed[j % 2][:, :], v_one[:, t, hh, :], ACT.Copy, scale=coef(0, d, t, hh)).then_inc(upd_weighed, 1)

        def update_pe(pe, w0, ci):
            for j, (d, t, hh) in enumerate(units(ci)):
                pe.wait_ge(upd_weighed, w0 + j + 1)
                if j >= 4:
                    pe.wait_ge(upd_taken, w0 + j - 3)
                for b in range(2):
                    o = K_AT + hh * MD + b * P
                    last = pe.matmul(bank[:, 2 * (j % 4) + b, 0:MD + 1], h[:, t, o:o + P], v_weighed[j % 2][:, :], start=True, stop=True)
                last.then_inc(upd_multiplied, 1)

        def update_dve(dve, w0, ci):
            for j, (d, t, hh) in enumerate(units(ci)):
                dve.wait_ge(upd_multiplied, w0 + j + 1)
                decay = col[:, 48 + (d * 2 + ci) * 4 + hh:49 + (d * 2 + ci) * 4 + hh]
                for b in range(2):
                    st = state(d, hh, b)
                    last = dve.scalar_tensor_tensor(st, st, decay, bank[:, 2 * (j % 4) + b, 0:MD + 1], ALU.mult, ALU.add)
                last.then_inc(upd_taken, 1)

        def unit_pe(pe, ci):
            us = units(ci)
            u0 = 8 * ci

            def first(j):
                d, t, hh = us[j]
                tok = slice(t * P, (t + 1) * P)
                if j >= 2:
                    pe.wait_ge(ml_weighted, u0 + j - 1)
                o = bank[:, j % 2, 0:P]
                pe.matmul(o, rows["a_true"][:, d, tok], pick[:, hh, :], start=True, stop=False)
                pe.matmul(o, pick[:, hh, :], rows["nm_true"][:, d, tok], start=False, stop=True)
                o = bank[:, 2 + j % 2, 0:P]
                for b in range(2):
                    last = pe.matmul(o, k_t[:, hh * 2 + b, tok], q_t[:, hh * 2 + b, tok], start=b == 0, stop=b == 1)
                last.then_inc(ml_scored, 1)

            def second(j):
                d, t, hh = us[j]
                tok = slice(t * P, (t + 1) * P)
                if j >= 2:
                    pe.wait_ge(ml_taken, u0 + j - 1)
                o = bank[:, 6 + j % 2, 0:MD + 1]
                for b in range(2):
                    pe.matmul(o, q_t[:, hh * 2 + b, tok], state(d, hh, b), start=b == 0, stop=b == 1)
                pe.wait_ge(ml_weighted, u0 + j + 1)
                pe.matmul(bank[:, 4 + j % 2, 0:MD + 1], p_t[j % 2][:, :], v_one[:, t, hh, :], start=True, stop=True).then_inc(ml_mixed, 1)

            first(0)
            for j in range(8):
                if j < 7:
                    first(j + 1)
                second(j)

        def unit_act(act, ci):
            us = units(ci)
            u0 = 8 * ci
            for j in range(9):
                if j < 8:
                    act.wait_ge(ml_exponent, u0 + j + 1)
                    act.activation(e_arg[j % 2][:, :], e_arg[j % 2][:, :], ACT.Exp).then_inc(ml_exped, 1)
                if j:
                    d, t, hh = us[j - 1]
                    act.wait_ge(ml_mixed, u0 + j)
                    act.activation(from_state[(j - 1) % 2][:, :], bank[:, 6 + (j - 1) % 2, 0:MD + 1], ACT.Copy, scale=coef(1, d, t, hh)).then_inc(ml_scaled, 1)

        def unit_dve(dve, ci):
            us = units(ci)
            u0 = 8 * ci

            def finish(j):
                d, t, hh = us[j]
                dve.wait_ge(ml_scaled, u0 + j + 1)
                n_ = num[j % 2]
                dve.tensor_tensor(n_[:, :], bank[:, 4 + j % 2, 0:MD + 1], from_state[j % 2][:, :], ALU.add)
                dve.drain()
                den = n_[:, MD:MD + 1]
                floor = small[:, 10 + j % 2:11 + j % 2]
                dve.tensor_scalar(floor, den, coef(2, d, t, hh), None, ALU.max)
                dve.drain()
                dve.scalar_tensor_tensor(den, den, -1.0, floor, ALU.mult, ALU.max)
                dve.drain()
                dve.reciprocal(small[:, 8 + j % 2:9 + j % 2], den)
                dve.drain()
                o = h[:, t, Q_AT + hh * MD:Q_AT + (hh + 1) * MD]
                r = small[:, 8 + j % 2:9 + j % 2]
                if ci == 0:
                    last = dve.tensor_scalar(o, n_[:, 0:MD], r, None, ALU.mult)
                else:
                    last = dve.scalar_tensor_tensor(o, n_[:, 0:MD], r, o, ALU.mult, ALU.add)
                last.then_inc(ml_taken, 1)

            for j in range(9):
                if j < 8:
                    d, t, hh = us[j]
                    dve.wait_ge(ml_scored, u0 + j + 1)
                    dve.tensor_tensor(e_arg[j % 2][:, :], bank[:, j % 2, 0:P], order_neg[:, d, :], ALU.add).then_inc(ml_exponent, 1)
                if j:
                    finish(j - 1)
                if j < 8:
                    dve.wait_ge(ml_exped, u0 + j + 1)
                    dve.scalar_tensor_tensor(p_t[j % 2][:, :], bank[:, 2 + j % 2, 0:P], MD ** -0.5, e_arg[j % 2][:, :], ALU.mult, ALU.mult).then_inc(ml_weighted, 1)

        def mixers_pe(pe):
            pe.wait_ge(aux_landed, 16 * 7)
            pe.wait_ge(mix_ready, 1)
            for t in range(T):
                for g in range(4):
                    last = pe.matmul(bank[:, t, g * P:(g + 1) * P], sgu_w[:, g, :], h[:, t, V_AT + g * P:V_AT + (g + 1) * P], start=True, stop=True)
            last.then_inc(mix_multiplied, 1)
            for g in range(4):
                for t in range(T):
                    last = pe.matmul(bank[:, 2 + g, 0:S], h[:, t, PL_AT + g * P:PL_AT + (g + 1) * P], windows[:, t, g, :], start=t == 0, stop=t == 1)
            last.then_inc(mix_multiplied, 1)
            pe.wait_ge(mix_scaled, 1)
            for t in range(T):
                for g in range(4):
                    last = pe.matmul(bank[:, 6 + t, g * P:(g + 1) * P], pooled[g][:, t * P:(t + 1) * P], pool_w[:, g, :], start=True, stop=True)
            last.then_inc(mix_multiplied, 1)

        def mixers_act(act):
            for t in range(T):
                act.activation(h[:, t, U_AT:U_AT + 1024], h[:, t, U_AT:U_AT + 1024], ACT.Gelu_apprx_tanh)
            act.drain()
            for t in range(T):
                act.activation(square[:, t * 512:(t + 1) * 512], h[:, t, V_AT:V_AT + 512], ACT.Square, accum_out=small[:, t:t + 1])
            act.drain().then_inc(mix_gelu, 1)
            act.wait_ge(mix_square, 1)
            act.activation(small[:, 4:6], small[:, 2:4], ACT.Sqrt).then_inc(mix_gelu, 1)
            act.wait_ge(mix_multiplied, 2)
            for g in range(4):
                last = act.activation(pooled[g][:, :], bank[:, 2 + g, 0:S], ACT.Copy)
            last.then_inc(mix_scaled, 1)

        def mixers_dve(dve):
            dve.wait_ge(mix_gelu, 1)
            dve.tensor_scalar(small[:, 2:4], small[:, 0:2], 1.0 / 512, EPS, ALU.mult, ALU.add)
            dve.drain().then_inc(mix_square, 1)
            dve.wait_ge(mix_gelu, 2)
            newton(dve, small[:, 6:8], small[:, 4:6], small[:, 2:4], small[:, 62:64])
            dve.drain()
            dve.wait_ge(aux_landed, 16 * 7)
            for t in range(T):
                v = h[:, t, V_AT:V_AT + 512]
                last = dve.scalar_tensor_tensor(v, v, small[:, 6 + t:7 + t], sgu_g[:, :], ALU.mult, ALU.mult)
            dve.drain().then_inc(mix_ready, 1)
            dve.wait_ge(mix_multiplied, 1)
            for t in range(T):
                for g in range(4):
                    u = h[:, t, U_AT + g * P:U_AT + (g + 1) * P]
                    dve.scalar_tensor_tensor(u, bank[:, t, g * P:(g + 1) * P], sgu_b[:, g:g + 1], u, ALU.add, ALU.mult)
            dve.wait_ge(mix_multiplied, 3)
            for t in range(T):
                dve.tensor_tensor(h[:, t, PL_AT:PL_AT + 512], bank[:, 6 + t, :], pool_g[:, :], ALU.mult)

        def ml_out_act(act):
            for t in range(T):
                act.activation(h[:, t, O_AT:O_AT + 1024], h[:, t, O_AT:O_AT + 1024], ACT.Sigmoid)
            act.drain().then_inc(out_root, 1)
            act.wait_ge(out_square, 1)
            act.activation(small[:, 24:32], small[:, 16:24], ACT.Sqrt).then_inc(out_root, 1)

        def ml_out_dve(dve):
            heads = lambda ap: ap.rearrange("p (h d) -> p h d", h=MH)
            for t in range(T):
                y = h[:, t, Q_AT:Q_AT + 1024]
                dve.tensor_tensor(square[:, :], y, y, ALU.mult)
                dve.drain()
                dve.tensor_reduce(small[:, 8 + 4 * t:12 + 4 * t], heads(square[:, :]), AX.X, ALU.add)
                dve.drain()
            dve.tensor_scalar(small[:, 16:24], small[:, 8:16], 1.0 / MD, EPS, ALU.mult, ALU.add)
            dve.drain().then_inc(out_square, 1)
            dve.wait_ge(out_root, 2)
            newton(dve, small[:, 32:40], small[:, 24:32], small[:, 16:24], small[:, 48:56])
            dve.drain()
            dve.wait_ge(aux_landed, 16 * 8)
            for t in range(T):
                y = h[:, t, Q_AT:Q_AT + 1024]
                dve.tensor_tensor(heads(y), heads(y), wide(small[:, 32 + 4 * t:36 + 4 * t].unsqueeze(2), [P, MH, MD]), ALU.mult)
                dve.drain()
                dve.tensor_tensor(y, y, mlstm_g[:, :], ALU.mult)
                dve.drain()
                dve.tensor_tensor(y, y, h[:, t, O_AT:O_AT + 1024], ALU.mult)

        def mixed_column(kk):
            return U_AT + kk * P if kk < 4 else Q_AT + (kk - 4) * P if kk < 12 else PL_AT + (kk - 12) * P

        def take_gated(dve, n, s):
            for t in range(T):
                o = x[:, t, bass.ds(n * N, N)]
                b = bank[:, 2 * s + t, :]
                dve.drain()
                dve.tensor_tensor(gated[:, t, :], b, m_row[0][:, bass.ds(n * N, N)], ALU.mult)
                dve.drain()
                last = dve.tensor_tensor(o, gated[:, t, :], o, ALU.add)
            last.then_inc(evacuated, 1)

        def hf_dve(dve):
            dve.tensor_tensor(full[:, :, :], xt_hi[:, :, :].bitcast(F32), xt_lo[:, :, :].bitcast(F32), ALU.add)
            dve.drain().then_inc(full_ready, 1)
            for g in range(NG):
                t, c = g // GQ, slice((g % GQ) * 512, (g % GQ) * 512 + 512)
                dve.wait_ge(part_copied, 2 * g + 1)
                dve.tensor_tensor(rest[:, g % 2, :], bank[:, g % 4, :], parts[:, t, 0, c], ALU.subtract).then_inc(part_rest, 1)
                dve.wait_ge(part_copied, 2 * g + 2)
                dve.tensor_tensor(parts[:, t, 2, c], rest[:, g % 2, :], parts[:, t, 1, c], ALU.subtract).then_inc(part_low, 1)

        def hf_act(act):
            for g in range(NG):
                t, c = g // GQ, slice((g % GQ) * 512, (g % GQ) * 512 + 512)
                act.wait_ge(back_turned, g + 1)
                act.activation(parts[:, t, 0, c], bank[:, g % 4, :], ACT.Copy).then_inc(part_copied, 1)
                act.wait_ge(part_rest, g + 1)
                act.activation(parts[:, t, 1, c], rest[:, g % 2, :], ACT.Copy).then_inc(part_copied, 1)
            act.wait_ge(part_low, NG)
            for i in range(3):
                act.dma_start(hf_rows[i].rearrange("(t p) d -> p t d", p=P), parts[:, :, i, :]).then_inc(hf_stored, 16)

        def hf_pe(pe):
            pe.wait_ge(full_ready, 1)
            for g in range(NG):
                t = g // GQ
                if g >= 4:
                    pe.wait_ge(part_low, g - 3)
                for j in range(4):
                    last = pe.transpose(bank[:, g % 4, j * P:(j + 1) * P], full[:, (g % GQ) * 4 + j, t * P:(t + 1) * P], eye[:, :])
                last.then_inc(back_turned, 1)

        def keys_pe(pe):
            for t in range(T):
                for g in range(t * GQ, (t + 1) * GQ):
                    if g >= 4:
                        pe.wait_ge(pq_copied, g - 3)
                    for j in range(4):
                        kk = (g % GQ) * 4 + j
                        last = pe.transpose(bank[:, g % 4, j * P:(j + 1) * P], h[:, t, kk * P:(kk + 1) * P], eye[:, :])
                    last.then_inc(pq_turned, 1)
                for g in range(t * GQ, (t + 1) * GQ):
                    pe.wait_ge(pq_copied, g + 1)
                    if g >= 4:
                        pe.wait_ge(keys_copied, g - 3)
                    for j in range(4):
                        kk = (g % GQ) * 4 + j
                        last = pe.matmul(bank[:, 4 + g % 4, j * P:(j + 1) * P], pq_t[:, kk, t * P:(t + 1) * P], keys[:, kk % 2, :], start=True, stop=True)
                    last.then_inc(keys_scored, 1)

        def keys_act(act):
            for t in range(T):
                for g in range(t * GQ, (t + 1) * GQ):
                    act.wait_ge(pq_turned, g + 1)
                    act.activation(group(pq_t, g), turned(g), ACT.Copy).then_inc(pq_copied, 1)
                for g in range(t * GQ, (t + 1) * GQ):
                    act.wait_ge(keys_scored, g + 1)
                    act.activation(key_s[:, t, (g % GQ) * 4:(g % GQ) * 4 + 4, :], bank[:, 4 + g % 4, :].rearrange("p (k n) -> p k n", k=4), ACT.Copy).then_inc(keys_copied, 1)

        def top16(dve, lists):
            dve.drain()
            for values, left, best, where in lists:
                dve.max(best[:, 0:8], values)
            dve.drain()
            for values, left, best, where in lists:
                dve.max_index(where[:, 0:8], best[:, 0:8], values)
                dve.match_replace(left, best[:, 0:8], values, -3e38)
            dve.drain()
            for values, left, best, where in lists:
                dve.max(best[:, 8:16], left)
            dve.drain()
            for values, left, best, where in lists:
                dve.max_index(where[:, 8:16], best[:, 8:16], left)

        def choose_dve(dve):
            for t in range(T):
                dve.wait_ge(keys_copied, GQ * (t + 1))
                top16(dve, [(key_s[:, t, j, :], less[:, j, :], top_v[:, t, j, :], top_i[:, t, j, :]) for j in range(16)])
            dve.drain()
            dve.tensor_copy(top_f[:, :, :, :].rearrange("p t j k -> p (t j k)"), top_i[:, :, :, :].rearrange("p t j k -> p (t j k)"))
            for t in range(T):
                for j in range(PH):
                    dve.tensor_tensor(cand[:, j, :].rearrange("p (a b) -> p a b", a=16), wide(top_v[:, t, 2 * j, :].unsqueeze(2), [P, 16, 16]),
                                      wide(top_v[:, t, 2 * j + 1, :].unsqueeze(1), [P, 16, 16]), ALU.add)
                top16(dve, [(cand[:, j, :], less2[:, j, :], best_v[:, t, j, :], best_i[:, t, j, :]) for j in range(PH)])
                dve.drain()
                pairs = best_i[:, t, :, :].rearrange("p h k -> p (h k)")
                dve.tensor_scalar(best_s[:, 0, :], pairs, 4, None, ALU.logical_shift_right)
                dve.tensor_scalar(best_s[:, 1, :], pairs, 15, None, ALU.bitwise_and)
                dve.drain()
                dve.tensor_copy(best_f[:, :, :].rearrange("p a n -> p (a n)"), best_s[:, :, :].rearrange("p a n -> p (a n)"))
                dve.drain()
                for i in range(2):
                    dve.drain()
                    dve.tensor_tensor(match[:, :, :], wide(best_f[:, i, :].unsqueeze(2), [P, PH * PK, 16]),
                                      wide(count16[:, :].unsqueeze(1), [P, PH * PK, 16]), ALU.is_equal)
                    dve.drain()
                    for j in range(PH):
                        m = match[:, j * PK:(j + 1) * PK, :]
                        dve.tensor_tensor(m, m, wide(top_f[:, t, 2 * j + i, :].unsqueeze(1), [P, PK, 16]), ALU.mult)
                    dve.drain()
                    dve.tensor_reduce(side[:, t, i, :], match[:, :, :], AX.X, ALU.add)
                dve.drain()
                dve.scalar_tensor_tensor(expert_f[:, t, :], side[:, t, 0, :], float(NK), side[:, t, 1, :], ALU.mult, ALU.add)
                g3 = gate_f[:, t, :].rearrange("p (h k) -> p h k", h=PH)
                dve.tensor_tensor(g3, best_v[:, t, :, :], wide(best_v[:, t, :, 0:1], [P, PH, PK]), ALU.subtract)
                dve.drain().then_inc(gate_shifted, 1)
                dve.wait_ge(gate_exped, t + 1)
                dve.tensor_reduce(gate_s[:, 8 * t:8 * t + 8], g3, AX.X, ALU.add)
                dve.drain()
                dve.reciprocal(gate_s[:, 16 + 8 * t:24 + 8 * t], gate_s[:, 8 * t:8 * t + 8])
                dve.drain()
                dve.tensor_tensor(g3, g3, wide(gate_s[:, 16 + 8 * t:24 + 8 * t].unsqueeze(2), [P, PH, PK]), ALU.mult)
                dve.drain().then_inc(chosen, 1)
            dve.wait_ge(chosen_turned, 1)
            dve.tensor_copy(idx[:, :], bank[:, 0, 0:S])
            dve.tensor_copy(gate_t[:, :], bank[:, 1, 0:S])
            for i in range(2):
                dve.tensor_copy(side_t[i][:, :], bank[:, 2 + i, 0:S])
            dve.memset(three[:, :], 1.0)

        def choose_act(act):
            for t in range(T):
                act.wait_ge(gate_shifted, t + 1)
                act.activation(gate_f[:, t, :], gate_f[:, t, :], ACT.Exp).then_inc(gate_exped, 1)

        def choose_pe(pe):
            pe.wait_ge(chosen, T)
            for t in range(T):
                pe.transpose(bank[:, 0, t * P:(t + 1) * P], expert_f[:, t, :], eye[:, :])
                pe.transpose(bank[:, 1, t * P:(t + 1) * P], gate_f[:, t, :], eye[:, :])
                for i in range(2):
                    last = pe.transpose(bank[:, 2 + i, t * P:(t + 1) * P], side[:, t, i, :], eye[:, :])
            last.then_inc(chosen_turned, 1)

        TOK = 8
        PASSES = S // TOK

        def rows_slot(j):
            return row_ring[64 * (j % 2):64 * (j % 2) + 3, j // 2 % 2, :]

        def experts_pool(pool):
            pool.wait_ge(rings_free, 1)
            with pool.Fori(0, PASSES) as i:
                for b in range(2):
                    n0 = TOK * i + 4 * b
                    pool.tensor_copy(idx4[b][:, :], idx[:, bass.ds(n0, 4)]).then_inc(indices_copied, 1)
                    pool.wait_ge(indices_copied, 2 * i + b + 1)
                    pool.sem_inc(passed_pool, 1)
                    for j in range(4):
                        pool.wait_ge(halves_read, 2 * PRE + 2 * (n0 + j) - 6)
                        pool.sem_inc(passed_pool, 1)
                        pool.indirect_dma_start(u_ring[:, j, :], None, A["peer_u_2"][0],
                                                bass.IndirectOffsetOnAxis(ap=idx4[b][:, j:j + 1], axis=0)).then_inc(u_landed[j], 16)

        def experts_sp(sp):
            sp.wait_ge(hf_stored, 48)
            sp.wait_ge(rings_free, 1)
            with sp.Fori(0, PASSES) as i:
                for j in range(TOK):
                    sp.wait_ge(half_spread, 2 * PRE + 2 * (TOK * i + j) - 6)
                    sp.dma_start(rows_slot(j), hf_rows[:, bass.ds(TOK * i + j, 1), :].rearrange("a o d -> (a o) d")).then_inc(rows_landed[j % 4], 16)

        def experts_pe(pe):
            def row(m, j):
                n = TOK * m + j
                pe.wait_ge(rows_landed[j % 4], 16 * (2 * m + j // 4 + 1))
                for hf in range(2):
                    pe.wait_ge(halves_read, 2 * PRE + 2 * n + hf - 1)
                    for b in range(2):
                        c = (2 * hf + b) * 512
                        k = 64 * (j % 2)
                        last = pe.matmul(bank[:, 2 * hf + b, :], three[k:k + 3, :], rows_slot(j)[:, c:c + 512], start=True, stop=True)
                    last.then_inc(half_spread, 1)

            def place(m, j):
                n = TOK * m + j
                if j % 4 == 0:
                    pe.wait_ge(weights_taken, PRE + 2 * m + j // 4 - 1)
                pe.wait_ge(one_hot, PRE + n + 1)
                pe.matmul(bank[:, 4 + j // 4, (j % 4) * P:(j % 4 + 1) * P], hot_side1[:, j % 4, :], hot_side0[:, j % 4, :],
                          start=True, stop=True).then_inc(placed, 1)

            def tokens(m, end):
                for j in range(TOK):
                    if j + 2 < end:
                        row(m + (j + 2) // TOK, (j + 2) % TOK)
                    place(m, j)

            row(0, 0)
            row(0, 1)
            with pe.Fori(0, PASSES - 1) as m:
                tokens(m, TOK + 2)
            tokens(PASSES - 1, TOK)

        def experts_act(act):
            def take(g, t, b):
                act.wait_ge(placed, PRE + 4 * g + 4)
                act.sem_inc(passed, 1)
                act.activation(placed_w[t][:, :, bass.ds(4 * g - t * P, 4)], bank[:, 4 + b, :].rearrange("p (j c) -> p c j", j=4),
                               ACT.Copy).then_inc(weights_taken, 1)

            def tokens(m, t, before):
                for j in range(TOK):
                    act.wait_ge(halves_read, 2 * PRE + 2 * (TOK * m + j) + 2)
                    act.activation(act_out[:, j:j + 1], act_in[:, j:j + 1], ACT.Gelu_apprx_tanh, bias=act_half[:, j:j + 1]).then_inc(gelued, 1)
                    if j == 1 and before is not None:
                        take(2 * m - 1, before, 1)
                    if j == 5:
                        take(2 * m, t, 0)

            half = PASSES // T
            for t in range(T):
                tokens(t * half, t, t - 1 if t else None)
                with act.Fori(0, half - 1) as i:
                    tokens(i + (t * half + 1), t, t)
            take(2 * PASSES - 1, T - 1, 1)

        def experts_dve(dve):
            def dot(m, j):
                n = TOK * m + j
                dve.wait_ge(u_landed[j % 4], 16 * (2 * m + j // 4 + 1))
                for hf in range(2):
                    u = u_ring[:, j % 4, hf * 1024:(hf + 1) * 1024]
                    dve.wait_ge(half_spread, 2 * PRE + 2 * n + hf + 1)
                    dve.sem_inc(passed, 1)
                    dve.tensor_tensor_reduce(u, u, bank[:, 2 * hf:2 * hf + 2, :].rearrange("p b n -> p (b n)"), 1.0, 0.0,
                                             ALU.mult, ALU.add, (act_in, act_half)[hf][:, j:j + 1]).then_inc(halves_read, 1)

            def spread(m, j):
                n = TOK * m + j
                at_ = bass.ds(n, 1)
                dve.wait_ge(placed, PRE + n - 3)
                dve.sem_inc(passed, 1)
                dve.tensor_scalar(hot_side1[:, j % 4, :], count128[:, :], side_t[1][:, at_], gate_t[:, at_], ALU.is_equal, ALU.mult)
                dve.wait_ge(gelued, PRE + n + 1)
                dve.sem_inc(passed, 1)
                dve.tensor_scalar(hot_side0[:, j % 4, :], count128[:, :], side_t[0][:, at_], act_out[:, j:j + 1], ALU.is_equal, ALU.mult).then_inc(one_hot, 1)

            def tokens(m, end):
                for j in range(TOK):
                    if j + 1 < end:
                        dot(m + (j + 1) // TOK, (j + 1) % TOK)
                    spread(m, j)

            dot(0, 0)
            with dve.Fori(0, PASSES - 1) as m:
                tokens(m, TOK + 1)
            tokens(PASSES - 1, TOK)

        def passes_of_blocks(eng, body):
            body(0, True)
            with eng.Fori(0, NK // 4 - 1) as i:
                body(i + 1, False)

        def values_sp(sp):
            table = A["peer_v_2"][0].rearrange("(b p) d -> b p d", p=P)
            sp.wait_ge(values_free, 1)

            def four(m, first):
                for j in range(4):
                    b = 4 * m + j
                    if not first:
                        sp.wait_ge(values_split, PRE + 4 * b - 12)
                    sp.dma_start(v_raw[j][:, :], table[bass.ds(b, 1)].rearrange("o p d -> p (o d)")).then_inc(v_landed[j], 16)
            passes_of_blocks(sp, four)

        def values_act(act):
            def four(m, first):
                for j in range(4):
                    b = 4 * m + j
                    act.wait_ge(values_multiplied, 2 * PRE + 4 * b - 4)
                    act.sem_inc(passed, 1)
                    for t in range(T):
                        last = act.activation(vw_hi[:, j % 2, t * P:(t + 1) * P], placed_w[t][:, bass.ds(b, 1), :].rearrange("p o n -> p (o n)"), ACT.Copy)
                    last.then_inc(vw_high, 1)
                    act.wait_ge(v_landed[j], 16 * (m + 1))
                    for c in range(4):
                        act.wait_ge(values_multiplied, 2 * PRE + 4 * b + c - 3)
                        act.activation(w_hi[:, c, :], v_raw[j][:, c * N:(c + 1) * N], ACT.Copy).then_inc(values_high, 1)
            passes_of_blocks(act, four)

        def values_dve(dve):
            def four(m, first):
                for j in range(4):
                    b = 4 * m + j
                    dve.wait_ge(vw_high, PRE + b + 1)
                    dve.sem_inc(passed, 1)
                    for t in range(T):
                        o = slice(t * P, (t + 1) * P)
                        last = dve.tensor_tensor(vw_lo[:, j % 2, o], placed_w[t][:, bass.ds(b, 1), :].rearrange("p o n -> p (o n)"),
                                                 vw_hi[:, j % 2, o].bitcast(F32), ALU.subtract)
                    last.then_inc(vw_low, 1)
                    for c in range(4):
                        dve.wait_ge(values_high, PRE + 4 * b + c + 1)
                        dve.tensor_tensor(w_lo[:, c, :], v_raw[j][:, c * N:(c + 1) * N], w_hi[:, c, :].bitcast(F32), ALU.subtract).then_inc(values_split, 1)
            passes_of_blocks(dve, four)
            dve.wait_ge(values_multiplied, 2 * PRE + 4 * NK)
            for t in range(T):
                sums = bank[:, 4 * t:4 * t + 4, :].rearrange("p b n -> p (b n)")
                dve.tensor_tensor(xe[t][:, :], sums, m_row[1][:, :], ALU.mult)
            dve.drain()
            for t in range(T):
                dve.tensor_tensor(x[:, t, :], x[:, t, :], xe[t][:, :], ALU.add)

        def values_pe(pe):
            def four(m, first):
                for j in range(4):
                    b = 4 * m + j
                    pe.wait_ge(vw_low, PRE + b + 1)
                    for c in range(4):
                        pe.wait_ge(values_split, PRE + 4 * b + c + 1)
                        for t in range(T):
                            o = bank[:, 4 * t + c, :]
                            a_hi, a_lo = vw_hi[:, j % 2, t * P:(t + 1) * P], vw_lo[:, j % 2, t * P:(t + 1) * P]
                            pe.matmul(o, a_hi, w_hi[:, c, :], start=first and j == 0, stop=False, skip_group_check=True)
                            pe.matmul(o, a_hi, w_lo[:, c, :], start=False, stop=False, skip_group_check=True)
                            last = pe.matmul(o, a_lo, w_hi[:, c, :], start=False, stop=True, skip_group_check=True)
                        last.then_inc(values_multiplied, 1)
            passes_of_blocks(pe, four)

        def pe_program(pe):
            pe.sem_inc(chunk_multiplied, PRE)
            for s_ in (blocks_turned, qk_turned, scored, p_turned, mixed, placed):
                pe.sem_inc(s_, PRE)
            for s_ in (half_spread, values_multiplied):
                pe.sem_inc(s_, 2 * PRE)
            pe.wait_ge(const_landed, 16 * 16)
            turn_pe(pe, 0, xn, PRE + 3)
            end_of_stage(pe, "pe")
            gemm_pe(pe, plan["ab_in"])
            end_of_stage(pe, "pe")
            sum_pe(pe, SUM_AB_IN)
            pe.wait_ge(aux_ready, 1)
            pe.matmul(bank[:, 7, 0:2], ones[:, :], lam[:, 0:2], start=True, stop=True).then_inc(aux_summed, 1)
            end_of_stage(pe, "pe")
            attention_pe(pe, ATT["a"])
            end_of_stage(pe, "pe")
            attention_pe(pe, ATT["b"])
            end_of_stage(pe, "pe")
            end_of_stage(pe, "pe")
            turn_pe(pe, 1, gate(h), 0)
            end_of_stage(pe, "pe")
            gemm_pe(pe, plan["ab_out"])
            end_of_stage(pe, "pe")
            sum_pe(pe, SUM_AB_OUT, 7)
            turn_pe(pe, 2, xn, PRE + 6)
            end_of_stage(pe, "pe")
            gemm_pe(pe, plan["c_in"])
            end_of_stage(pe, "pe")
            rows_pe(pe)
            end_of_stage(pe, "pe")
            attention_pe(pe, ATT["c"])
            end_of_stage(pe, "pe")
            turn_pe(pe, 3, gate(h), 0)
            end_of_stage(pe, "pe")
            gemm_pe(pe, plan["c_out"])
            end_of_stage(pe, "pe")
            sum_pe(pe, SUM_C_OUT)
            end_of_stage(pe, "pe")
            end_of_stage(pe, "pe")
            turn_pe(pe, 4, xn, PRE + 12)
            end_of_stage(pe, "pe")
            gemm_pe(pe, plan["ctx"])
            gates_pe(pe, 0)
            end_of_stage(pe, "pe")
            ml_rows_pe(pe)
            conv_pe(pe, 0, False)
            end_of_stage(pe, "pe")
            ml_cols_pe(pe, 0)
            end_of_stage(pe, "pe")
            for ci in range(2):
                update_pe(pe, 8 * ci, ci)
                end_of_stage(pe, "pe")
            turn_pe(pe, 5, xn, PRE + 15)
            end_of_stage(pe, "pe")
            gemm_pe(pe, plan["lat"])
            gates_pe(pe, 1)
            end_of_stage(pe, "pe")
            ml_rows_pe(pe)
            conv_pe(pe, 8, True)
            end_of_stage(pe, "pe")
            mixers_pe(pe)
            end_of_stage(pe, "pe")
            ml_cols_pe(pe, 1)
            end_of_stage(pe, "pe")
            unit_pe(pe, 0)
            end_of_stage(pe, "pe")
            update_pe(pe, 16, 0)
            end_of_stage(pe, "pe")
            unit_pe(pe, 1)
            end_of_stage(pe, "pe")
            end_of_stage(pe, "pe")
            turn_pe(pe, 6, h, 0, mixed_column)
            end_of_stage(pe, "pe")
            gemm_pe(pe, plan["mix_out"])
            end_of_stage(pe, "pe")
            turn_pe(pe, 7, xn, PRE + 18)
            end_of_stage(pe, "pe")
            hf_pe(pe)
            end_of_stage(pe, "pe")
            gemm_pe(pe, plan["wq"])
            end_of_stage(pe, "pe")
            pe.wait_ge(keys_landed, 48)
            keys_pe(pe)
            choose_pe(pe)
            end_of_stage(pe, "pe")
            experts_pe(pe)
            end_of_stage(pe, "pe")
            values_pe(pe)
            end_of_stage(pe, "pe")
            end_of_stage(pe, "pe")

        def act_program(act):
            for s_ in (hi_ready, act_step, hi_written, qk_copied, exped, p_copied, gelued, weights_taken, values_high, vw_high):
                act.sem_inc(s_, PRE)
            act.wait_ge(x_landed, 16)
            normalise_act(act, x, 0)
            turn_act(act, 0, ((g_ab, None), 0))
            act.wait_ge(const_landed, 16 * 16)
            act.activation(c_col[:, :, :], c_col[:, :, :], ACT.Silu).then_inc(silu_done, 1)
            end_of_stage(act, "act")
            gemm_act(act, plan["ab_in"], take=True)
            end_of_stage(act, "act")
            act.activation(gate(h), gate(h), ACT.Silu)
            act.wait_ge(aux_summed, 1)
            act.activation(lam[:, 0:2], bank[:, 7, 0:2], ACT.Exp).then_inc(aux_summed, 1)
            end_of_stage(act, "act")
            attention_act(act, ATT["a"])
            end_of_stage(act, "act")
            attention_act(act, ATT["b"])
            end_of_stage(act, "act")
            act.wait_ge(aux_ready, 3)
            act.activation(small[:, 24:32], small[:, 16:24], ACT.Sqrt).then_inc(aux_summed, 1)
            end_of_stage(act, "act")
            turn_act(act, 1, None)
            end_of_stage(act, "act")
            gemm_act(act, plan["ab_out"])
            end_of_stage(act, "act")
            normalise_act(act, x, 1)
            turn_act(act, 2, ((g_c, None), NG))
            end_of_stage(act, "act")
            gemm_act(act, plan["c_in"], take=True)
            end_of_stage(act, "act")
            act.dma_start(ada_bias_row[:, :, :], A["ada_b_rows"]).then_inc(aux_landed, 16)
            act.activation(gate(h), gate(h), ACT.Silu)
            rows_act(act)
            end_of_stage(act, "act")
            attention_act(act, ATT["c"])
            end_of_stage(act, "act")
            turn_act(act, 3, None)
            end_of_stage(act, "act")
            act.dma_start(row_w[:, :], A["final_norm"].partition_broadcast(P)).then_inc(aux_landed, 16)
            for dst, src in ((flip, "flip"), (order_neg, "order_neg"), (conv_w, "qk_conv_2"), (sgu_b, "sgu_b_2")):
                act.dma_start(dst[:, :] if len(dst.shape) == 2 else dst[:, :, :], A[src]).then_inc(ctx_landed, 16)
            act.dma_start(h[:, :, 0:D], A["ctx_2"][0].rearrange("(t p) d -> p t d", p=P)).then_inc(ctx_landed, 16)
            gemm_act(act, plan["c_out"])
            end_of_stage(act, "act")
            rstd_act(act, x, 2)
            end_of_stage(act, "act")
            act.activation(wg_parts[:, :, 0:16], wg[:, :, :], ACT.Copy).then_inc(wg_ready, 1)
            act.wait_ge(ctx_landed, 80)
            end_of_stage(act, "act")
            normalise_act(act, h[:, :, 0:D], 3)
            turn_act(act, 4, ((mod[:, 0, :], m_col[:, 6, :]), 2 * NG))
            end_of_stage(act, "act")
            gemm_act(act, plan["ctx"], take=True)
            end_of_stage(act, "act")
            ml_rows_act(act, 0)
            conv_act(act, 0, False)
            end_of_stage(act, "act")
            ml_cols_act(act, 0)
            end_of_stage(act, "act")
            for ci in range(2):
                update_act(act, 8 * ci, ci)
                end_of_stage(act, "act")
            normalise_act(act, x, 4)
            turn_act(act, 5, ((mod[:, 1, :], m_col[:, 0, :]), 3 * NG))
            end_of_stage(act, "act")
            gemm_act(act, plan["lat"], take=True)
            end_of_stage(act, "act")
            for dst, src in ((sgu_w, "sgu_w_2"), (pool_w, "pool_w_2")):
                act.dma_start(dst[:, :, :], A[src]).then_inc(aux_landed, 16)
            act.dma_start(windows[:, :, :, :], A["windows"]).then_inc(aux_landed, 16)
            act.dma_start(sgu_g[:, :], A["sgu_norm_2"].partition_broadcast(P)).then_inc(aux_landed, 16)
            act.dma_start(pool_g[:, :], A["pool_scale_2"].partition_broadcast(P)).then_inc(aux_landed, 16)
            ml_rows_act(act, 1)
            conv_act(act, 8, True)
            end_of_stage(act, "act")
            mixers_act(act)
            end_of_stage(act, "act")
            act.dma_start(mlstm_g[:, :], A["mlstm_norm_2"].partition_broadcast(P)).then_inc(aux_landed, 16)
            ml_cols_act(act, 1)
            end_of_stage(act, "act")
            unit_act(act, 0)
            end_of_stage(act, "act")
            update_act(act, 16, 0)
            end_of_stage(act, "act")
            unit_act(act, 1)
            end_of_stage(act, "act")
            ml_out_act(act)
            end_of_stage(act, "act")
            turn_act(act, 6, None)
            end_of_stage(act, "act")
            gemm_act(act, plan["mix_out"])
            end_of_stage(act, "act")
            normalise_act(act, x, 5)
            turn_act(act, 7, ((mod[:, 2, :], m_col[:, 3, :]), 4 * NG))
            end_of_stage(act, "act")
            hf_act(act)
            end_of_stage(act, "act")
            for dst, src in ((keys, "peer_keys_2"), (count16, "count16"), (count128, "count128")):
                act.dma_start(dst[:, :] if len(dst.shape) == 2 else dst[:, :, :], A[src]).then_inc(keys_landed, 16)
            gemm_act(act, plan["wq"], take=True)
            end_of_stage(act, "act")
            keys_act(act)
            choose_act(act)
            end_of_stage(act, "act")
            experts_act(act)
            end_of_stage(act, "act")
            values_act(act)
            end_of_stage(act, "act")
            act.dma_start(last_w[:, :], A["norm_final_2"].partition_broadcast(P)).then_inc(aux_landed, 16)
            rstd_act(act, x, 6)
            end_of_stage(act, "act")

        def dve_program(dve):
            dve.sem_inc(raw_used, RAW * KC)
            dve.sem_inc(halves_read, 2 * PRE)
            for s_ in (evacuated, norm_step, lo_written, roped, k_roped, shifted, weighed, mix_taken, one_hot, values_split, vw_low, ada_used):
                dve.sem_inc(s_, PRE)
            dve.memset(ones[:, :], 1.0)
            dve.wait_ge(const_landed, 16 * 16)
            dve.tensor_tensor(lam[:, 0:1], lam_in[:, 0:1], lam_in[:, 1:2], ALU.mult)
            dve.tensor_tensor(lam[:, 1:2], lam_in[:, 2:3], lam_in[:, 3:4], ALU.mult)
            dve.drain().then_inc(aux_ready, 1)
            dve.wait_ge(x_landed, 16)
            normalise_dve(dve, 0, x)
            turn_dve(dve, 0, ((g_ab, None), 0))
            end_of_stage(dve, "dve")
            dve.wait_ge(silu_done, 1)
            gemm_dve(dve, plan["ab_in"])
            end_of_stage(dve, "dve")
            sum_dve(dve, SUM_AB_IN, 1)
            dve.wait_ge(aux_summed, 2)
            dve.tensor_tensor(lam[:, 3:4], lam[:, 1:2], lam[:, 0:1], ALU.subtract)
            dve.drain()
            dve.tensor_scalar(lam[:, 2:3], lam[:, 3:4], -LAM_INIT, None, ALU.add).then_inc(aux_ready, 1)
            end_of_stage(dve, "dve")
            attention_dve(dve, ATT["a"])
            end_of_stage(dve, "dve")
            attention_dve(dve, ATT["b"])
            end_of_stage(dve, "dve")
            hb = ATT["b"]
            heads = lambda ap: ap.rearrange("p (h d) -> p h d", h=4)
            for t in range(T):
                y = h[:, t, hb["q"]:hb["q"] + 1024]
                dve.tensor_tensor(sub_sq[:, :], y, y, ALU.mult)
                dve.drain()
                dve.tensor_reduce(small[:, 8 + 4 * t:12 + 4 * t], heads(sub_sq[:, :]), AX.X, ALU.add)
                dve.drain()
            dve.tensor_scalar(small[:, 16:24], small[:, 8:16], 1.0 / 256, EPS, ALU.mult, ALU.add).then_inc(aux_ready, 1)
            dve.wait_ge(aux_summed, 3)
            newton(dve, small[:, 32:40], small[:, 24:32], small[:, 16:24], small[:, 48:56])
            dve.drain()
            dve.tensor_scalar(small[:, 40:48], small[:, 32:40], 1.0 - LAM_INIT, None, ALU.mult)
            dve.drain()
            for t in range(T):
                y = h[:, t, hb["q"]:hb["q"] + 1024]
                z = h[:, t, hb["z"]:hb["z"] + 1024]
                dve.tensor_tensor(heads(y), heads(y), wide(small[:, 40 + 4 * t:44 + 4 * t].unsqueeze(2), [P, 4, 256]), ALU.mult)
                dve.drain()
                dve.tensor_tensor(heads(y), heads(y), wide(subln[:, :].unsqueeze(1), [P, 4, 256]), ALU.mult)
                dve.drain()
                dve.tensor_tensor(z, z, y, ALU.mult)
            end_of_stage(dve, "dve")
            turn_dve(dve, 1, None)
            end_of_stage(dve, "dve")
            gemm_dve(dve, plan["ab_out"], take_residual)
            end_of_stage(dve, "dve")
            normalise_dve(dve, 1, x)
            turn_dve(dve, 2, ((g_c, None), NG))
            sum_dve(dve, SUM_AB_OUT, 2, 7)
            end_of_stage(dve, "dve")
            gemm_dve(dve, plan["c_in"])
            end_of_stage(dve, "dve")
            end_of_stage(dve, "dve")
            attention_dve(dve, ATT["c"])
            end_of_stage(dve, "dve")
            turn_dve(dve, 3, None)
            end_of_stage(dve, "dve")
            gemm_dve(dve, plan["c_out"], take_residual)
            end_of_stage(dve, "dve")
            rstd_dve(dve, 2, x)
            dve.wait_ge(aux_landed, 32)
            for t in range(T):
                dve.scalar_tensor_tensor(x[:, t, :], x[:, t, :], small[:, 6 + t:7 + t], row_w[:, :], ALU.mult, ALU.mult)
            sum_dve(dve, SUM_C_OUT, 5)
            dve.drain()
            for i, (v, g, norm) in enumerate(((1, 1, g_mix), (0, 1, g_mix), (0, 4, g_ffn))):
                dve.scalar_tensor_tensor(mod[:, i, :], m_col[:, v * 6 + g, :], 1.0, norm[:, :], ALU.add, ALU.mult)
            dve.drain().then_inc(norm_step, 1)
            end_of_stage(dve, "dve")
            dve.memset(h[:, :, 5632:5632 + 8 * (MD + 1)], 0.0)
            dve.memset(m_now[:, :], 0.0)
            dve.tensor_copy(pick[:, :, :], wide(eye[0:MH, 0:MH].unsqueeze(2), [MH, MH, P]))
            dve.wait_ge(wg_ready, 1)
            dve.tensor_tensor(wg_parts[:, :, 16:32], wg[:, :, :], wg_parts[:, :, 0:16].bitcast(F32), ALU.subtract)
            end_of_stage(dve, "dve")
            normalise_dve(dve, 3, h[:, :, 0:D])
            turn_dve(dve, 4, ((mod[:, 0, :], m_col[:, 6, :]), 2 * NG))
            end_of_stage(dve, "dve")
            gemm_dve(dve, plan["ctx"])
            gates_dve(dve, 0)
            end_of_stage(dve, "dve")
            ml_rows_dve(dve, 0)
            conv_dve(dve, 0, False)
            end_of_stage(dve, "dve")
            ml_cols_dve(dve, 0)
            end_of_stage(dve, "dve")
            for ci in range(2):
                update_dve(dve, 8 * ci, ci)
                end_of_stage(dve, "dve")
            normalise_dve(dve, 4, x)
            turn_dve(dve, 5, ((mod[:, 1, :], m_col[:, 0, :]), 3 * NG))
            end_of_stage(dve, "dve")
            gemm_dve(dve, plan["lat"])
            gates_dve(dve, 1)
            end_of_stage(dve, "dve")
            ml_rows_dve(dve, 1)
            conv_dve(dve, 8, True)
            end_of_stage(dve, "dve")
            mixers_dve(dve)
            end_of_stage(dve, "dve")
            ml_cols_dve(dve, 1)
            end_of_stage(dve, "dve")
            unit_dve(dve, 0)
            end_of_stage(dve, "dve")
            update_dve(dve, 16, 0)
            end_of_stage(dve, "dve")
            unit_dve(dve, 1)
            end_of_stage(dve, "dve")
            ml_out_dve(dve)
            end_of_stage(dve, "dve")
            turn_dve(dve, 6, None)
            end_of_stage(dve, "dve")
            gemm_dve(dve, plan["mix_out"], take_gated)
            end_of_stage(dve, "dve")
            normalise_dve(dve, 5, x)
            turn_dve(dve, 7, ((mod[:, 2, :], m_col[:, 3, :]), 4 * NG))
            end_of_stage(dve, "dve")
            hf_dve(dve)
            end_of_stage(dve, "dve")
            gemm_dve(dve, plan["wq"])
            end_of_stage(dve, "dve")
            dve.wait_ge(keys_landed, 48)
            choose_dve(dve)
            end_of_stage(dve, "dve")
            dve.sem_inc(rings_free, 1)
            experts_dve(dve)
            end_of_stage(dve, "dve")
            dve.sem_inc(values_free, 1)
            values_dve(dve)
            end_of_stage(dve, "dve")
            rstd_dve(dve, 6, x)
            dve.wait_ge(aux_landed, 16 * 8 + 16)
            for t in range(T):
                dve.scalar_tensor_tensor(x[:, t, :], x[:, t, :], small[:, 6 + t:7 + t], last_w[:, :], ALU.mult, ALU.mult)
            end_of_stage(dve, "dve")

        aux_ready, aux_summed, ctx_landed, keys_landed = (sem(n) for n in ("aux_ready", "aux_summed", "ctx_landed", "keys_landed"))
        TOTAL = [0]

        @block.vector
        def _(dve):
            dve_program(dve)
            TOTAL[0] = stages["dve"]

        @block.tensor
        def _(pe):
            pe_program(pe)

        @block.scalar
        def _(act):
            act_program(act)

        @block.gpsimd
        def _(pool):
            ada_pool(pool)
            experts_pool(pool)

        @block.sync
        def _(sp):
            sp.dma_start(x[:, :, :], A["x"][0].rearrange("(t p) d -> p t d", p=P)).then_inc(x_landed, 16)
            for dst, src in ((eye, "eye"), (rope_cos, "rope_cos"), (rope_sin, "rope_sin"), (dil_neg, "dilated_neg"),
                             (dil_count, "dilated_count"), (cau_neg, "causal_neg"), (g_ab, "norm_ab"), (g_c, "norm_c"),
                             (lam_in, "lam_ab"), (c_col, "c_cols"), (ada_bias, "ada_b_cols"), (g_mix, "norm_mix_2"),
                             (g_ffn, "norm_ffn_2"), (wg, "w_gates")):
                ap = dst[:, :, :] if len(dst.shape) == 3 else dst[:, :]
                sp.dma_start(ap, A[src]).then_inc(const_landed, 16)
            sp.dma_start(gate_b[:, :], A["b_gate_2"].partition_broadcast(P)).then_inc(const_landed, 16)
            sp.dma_start(subln[:, :], A["subln_ab"].rearrange("a n -> (a n)").partition_broadcast(P)).then_inc(const_landed, 16)
            for name in ("ab_in", "ab_out", "c_in", "c_out", "ctx", "lat", "mix_out", "wq"):
                stream_sp(sp, plan[name])
            experts_sp(sp)
            values_sp(sp)
            sp.wait_ge(stage_done, 3 * TOTAL[0])
            sp.dma_start(out[0].rearrange("(t p) d -> p t d", p=P), x[:, :, :]).then_inc(out_stored, 16)
            sp.wait_ge(out_stored, 16)


def _columns(a):
    return np.ascontiguousarray(np.reshape(a, (-1, P)).T)


def host_layout(i):
    keep = ("x", "w_in_ab", "w_out_ab", "w_in_c", "w_out_c", "subln_ab", "final_norm", "ctx_2", "ada_w_2", "w_in_2", "w_out_2",
            "peer_wq_2", "peer_u_2", "peer_v_2", "norm_final_2")
    a = {k: i[k] for k in keep}
    a.update({k: _columns(i[k]) for k in ("norm_ab", "norm_c", "norm_mix_2", "norm_ffn_2")})
    a["lam_ab"] = i["lam_ab"][0].T
    a["c_cols"] = np.stack([_columns(i["c_2"]), _columns(i["c_ctx_2"])], 1)
    a["ada_b_cols"] = _columns(i["ada_b_2"]).reshape(P, 6, K)
    a["ada_b_rows"] = i["ada_b_2"].reshape(1, 6, D)[:, 2::3, :]
    a["w_gates"] = i["w_in_2"][0, :, G_AT:].reshape(K, P, 16).transpose(1, 0, 2)
    a["b_gate_2"] = i["b_gate_2"][0]
    a["sgu_norm_2"], a["pool_scale_2"], a["mlstm_norm_2"] = (i[k][0] for k in ("sgu_norm_2", "pool_scale_2", "mlstm_norm_2"))
    a["sgu_w_2"] = i["sgu_w_2"][0].transpose(2, 0, 1)
    a["sgu_b_2"] = i["sgu_b_2"][0].T
    a["pool_w_2"] = i["pool_w_2"][0].transpose(1, 0, 2)
    a["qk_conv_2"] = i["qk_conv_2"][0].reshape(3, 16, P).transpose(2, 1, 0)
    a["peer_keys_2"] = i["peer_keys_2"][0].transpose(2, 0, 1)
    a.update(shape_constants())
    return {k: np.ascontiguousarray(v) for k, v in a.items()}


def kernel(**inputs):
    import concourse.bacc as bacc
    from concourse.bass_utils import run_bass_kernel_spmd

    nc = bacc.Bacc("TRN2", target_bir_lowering=False, num_devices=1)
    arrays = host_layout({k: np.asarray(v) for k, v in inputs.items()})
    A = {k: nc.dram_tensor(f"in_{k}", v.shape, mybir.dt.from_np(v.dtype), kind="ExternalInput").ap() for k, v in arrays.items()}
    out = nc.dram_tensor("out", (1, S, D), F32, kind="ExternalOutput").ap()
    bass_hybrid_stack_kernel(nc, A, out)
    result = run_bass_kernel_spmd(nc, [{f"in_{k}": v for k, v in arrays.items()}], core_ids=[0])
    return result.results[0]["out"]
```
